# Optimizing a Trainium2 kernel written in Bass

```python
import math
import functools
import jax, jax.numpy as jnp
from jax import lax
import numpy as np

D_MODEL = 1024
BATCH = 1
SEQ = 512
DEPTH = 2
DEC_BATCH = 8
DEC_SEQ = 8
PAST_LEN = 2048
PAGE_SIZE = 128

HEAD_DIM = 64
N_MIXERS = 4
H_A = D_MODEL // (N_MIXERS * HEAD_DIM)
H_B = D_MODEL // (N_MIXERS * HEAD_DIM)
H_C = D_MODEL // (N_MIXERS * HEAD_DIM)
H_D = D_MODEL // (N_MIXERS * HEAD_DIM)
MIX_WIDTH = (H_A + H_B + H_C + H_D) * HEAD_DIM
DK_B = HEAD_DIM // 2
GLA_RANK = 16
GLA_TAU = 16.0
CHUNK = 64
Q_BLOCK = 128
ROPE_THETA = 500000.0
ROPE_DIMS = HEAD_DIM // 4
DILATIONS = ((128, 1), (512, 4), (2048, 16))
MAX_WINDOW = 2048
SB_BIAS_INIT = -6.0
D_FF = 2 * D_MODEL
EPS = 1e-6
PROJ_SIZES = (
    H_A * HEAD_DIM, H_A * HEAD_DIM, H_A * HEAD_DIM, H_A, H_A, H_A * HEAD_DIM,
    H_B * DK_B, H_B * DK_B, H_B * HEAD_DIM, H_B * HEAD_DIM, GLA_RANK,
    H_C * HEAD_DIM, H_C * HEAD_DIM, H_C * HEAD_DIM,
    H_D * HEAD_DIM, H_D * HEAD_DIM, H_D * HEAD_DIM,
)
N_IN = sum(PROJ_SIZES)

kernel_name = "hybrid_mlstm_gla_dilated_stickbreak_decoder_step"

def rms_norm(x, g):
    xf = x.astype(jnp.float32)
    y = xf * lax.rsqrt(jnp.mean(xf * xf, -1, keepdims=True) + EPS)
    return (y * g.astype(jnp.float32)).astype(x.dtype)

def head_rms(x, g):
    y = x * lax.rsqrt(jnp.mean(x * x, -1, keepdims=True) + EPS)
    y = y * g.astype(jnp.float32).reshape(x.shape[2], x.shape[3])
    return y.reshape(x.shape[0], x.shape[1], -1)

def swiglu(x, w_in, w_out):
    g, u = jnp.split(x @ w_in, 2, axis=-1)
    return (jax.nn.silu(g) * u) @ w_out

def rope(x, pos):
    half = ROPE_DIMS // 2
    inv = ROPE_THETA ** (-jnp.arange(half, dtype=jnp.float32) / half)
    ang = pos.astype(jnp.float32)[:, None] * inv[None, :]
    cos = jnp.cos(ang)[None, :, None, :]
    sin = jnp.sin(ang)[None, :, None, :]
    xr = x[..., :ROPE_DIMS].astype(jnp.float32)
    x1, x2 = xr[..., :half], xr[..., half:]
    rot = jnp.concatenate([x1 * cos - x2 * sin, x1 * sin + x2 * cos], -1)
    return jnp.concatenate([rot.astype(x.dtype), x[..., ROPE_DIMS:]], -1)

def split_columns(p):
    points, acc = [], 0
    for s in PROJ_SIZES[:-1]:
        acc += s
        points.append(acc)
    return jnp.split(p, points, axis=-1)

def run_chunks(step, carry, seqs):
    T = seqs[0].shape[2]
    L = CHUNK if T % CHUNK == 0 else T
    nc = T // L
    xs = tuple(jnp.moveaxis(s.reshape(s.shape[:2] + (nc, L) + s.shape[3:]), 2, 0) for s in seqs)
    carry, ys = lax.scan(step, carry, xs)
    ys = jnp.moveaxis(ys, 0, 2)
    return carry, ys.reshape(ys.shape[:2] + (T,) + ys.shape[4:])

def mlstm_chunk(carry, xs):
    c0, n0, m0 = carry
    q, k, v, ig, lf = xs
    L = q.shape[2]
    b = jnp.cumsum(lf, -1)
    causal = jnp.tril(jnp.ones((L, L), dtype=bool))
    dmat = jnp.where(causal, b[..., :, None] - b[..., None, :] + ig[..., None, :], -jnp.inf)
    a = b + m0[..., None]
    m = jnp.maximum(a, jnp.max(dmat, -1))
    s = jnp.einsum('bhtd,bhsd->bhts', q, k) * jnp.exp(dmat - m[..., None])
    inter = jnp.exp(a - m)
    num = jnp.einsum('bhts,bhse->bhte', s, v) + inter[..., None] * jnp.einsum('bhtd,bhde->bhte', q, c0)
    den = jnp.sum(s, -1) + inter * jnp.einsum('bhtd,bhd->bht', q, n0)
    h = num / jnp.maximum(jnp.abs(den), jnp.exp(-m))[..., None]
    m_new = m[..., -1]
    ws = jnp.exp(b[..., -1:] - b + ig - m_new[..., None])
    decay = jnp.exp(b[..., -1] + m0 - m_new)
    c_new = decay[..., None, None] * c0 + jnp.einsum('bhs,bhsd,bhse->bhde', ws, k, v)
    n_new = decay[..., None] * n0 + jnp.einsum('bhs,bhsd->bhd', ws, k)
    return (c_new, n_new, m_new), h

def gla_chunk(s0, xs):
    q, k, v, la = xs
    L = q.shape[2]
    bc = jnp.cumsum(la, 2)
    causal = jnp.tril(jnp.ones((L, L), dtype=bool))[:, :, None]
    diff = jnp.where(causal, bc[:, :, :, None, :] - bc[:, :, None, :, :], -jnp.inf)
    att = jnp.einsum('bhtd,bhsd,bhtsd->bhts', q, k, jnp.exp(diff))
    o = jnp.einsum('bhts,bhse->bhte', att, v) + jnp.einsum('bhtd,bhde->bhte', q * jnp.exp(bc), s0)
    last = bc[:, :, -1]
    s_new = jnp.exp(last)[..., None] * s0 + jnp.einsum('bhsd,bhse->bhde', k * jnp.exp(last[:, :, None, :] - bc), v)
    return s_new, o

def dilated_window_attention(q, kc, vc, q_idx, first_valid):
    qf = q.astype(jnp.float32) * (HEAD_DIM ** -0.5)
    outs, lses = [], []
    for window, dil in DILATIONS:
        j = jnp.arange(window // dil + 1)
        idx = q_idx[:, None] - dil * j[None, :]
        valid = idx >= first_valid
        idx = jnp.maximum(idx, 0)
        kg = jnp.take(kc, idx, axis=1).astype(jnp.float32)
        vg = jnp.take(vc, idx, axis=1).astype(jnp.float32)
        s = jnp.einsum('bqhd,bqjhd->bhqj', qf, kg)
        s = jnp.where(valid[None, None], s, -jnp.inf)
        lse = jax.nn.logsumexp(s, axis=-1)
        outs.append(jnp.einsum('bhqj,bqjhd->bqhd', jnp.exp(s - lse[..., None]), vg))
        lses.append(lse)
    wts = jax.nn.softmax(jnp.stack(lses, 0), axis=0)
    o = jnp.einsum('gbhq,gbqhd->bqhd', wts, jnp.stack(outs, 0))
    return o.astype(q.dtype)

def stick_breaking_attention(q, kc, vc, q_pos, bias):
    z = jnp.einsum('bqhd,bkhd->bhqk', q.astype(jnp.float32), kc.astype(jnp.float32)) * (HEAD_DIM ** -0.5)
    z = z + bias.astype(jnp.float32)[None, :, None, None]
    valid = jnp.arange(kc.shape[1])[None, :] < q_pos[:, None]
    log_beta = jnp.where(valid, jax.nn.log_sigmoid(z), -jnp.inf)
    log_keep = jnp.where(valid, jax.nn.log_sigmoid(-z), 0.0)
    later = lax.cumsum(log_keep, axis=3, reverse=True) - log_keep
    a = jnp.exp(log_beta + later)
    return jnp.einsum('bhqk,bkhd->bqhd', a, vc.astype(jnp.float32)).astype(q.dtype)

def prompt_window(q, k, v):
    B, T, H, d = q.shape
    nb = T // Q_BLOCK
    pad = ((0, 0), (MAX_WINDOW, 0), (0, 0), (0, 0))
    kp, vp = jnp.pad(k, pad), jnp.pad(v, pad)
    qb = jnp.moveaxis(q.reshape(B, nb, Q_BLOCK, H, d), 1, 0)
    starts = jnp.arange(nb) * Q_BLOCK
    q_idx = MAX_WINDOW + jnp.arange(Q_BLOCK)

    def block(args):
        qi, t0 = args
        kc = lax.dynamic_slice_in_dim(kp, t0, MAX_WINDOW + Q_BLOCK, axis=1)
        vc = lax.dynamic_slice_in_dim(vp, t0, MAX_WINDOW + Q_BLOCK, axis=1)
        return dilated_window_attention(qi, kc, vc, q_idx, MAX_WINDOW - t0)

    o = lax.map(block, (qb, starts))
    return jnp.moveaxis(o, 0, 1).reshape(B, T, H, d)

def prompt_stick_breaking(q, k, v, bias):
    B, T, H, d = q.shape
    nb = T // Q_BLOCK
    qb = jnp.moveaxis(q.reshape(B, nb, Q_BLOCK, H, d), 1, 0)
    starts = jnp.arange(nb) * Q_BLOCK

    def block(args):
        qi, t0 = args
        return stick_breaking_attention(qi, k, v, t0 + jnp.arange(Q_BLOCK), bias)

    o = lax.map(block, (qb, starts))
    return jnp.moveaxis(o, 0, 1).reshape(B, T, H, d)

def sample_window(q, k, v, buf_k, buf_v):
    w = buf_k.shape[1]
    kc = jnp.concatenate([buf_k.astype(k.dtype), k], 1)
    vc = jnp.concatenate([buf_v.astype(v.dtype), v], 1)
    return dilated_window_attention(q, kc, vc, w + jnp.arange(q.shape[1]), 0)

def sample_stick_breaking(q, k, v, bias, pool_k, pool_v, page_table):
    n_seq, n_pages = page_table.shape
    past = n_pages * PAGE_SIZE
    k_past = pool_k[page_table].reshape(n_seq, past, H_D, HEAD_DIM)
    v_past = pool_v[page_table].reshape(n_seq, past, H_D, HEAD_DIM)
    kc = jnp.concatenate([k_past.astype(k.dtype), k], 1)
    vc = jnp.concatenate([v_past.astype(v.dtype), v], 1)
    return stick_breaking_attention(q, kc, vc, past + jnp.arange(q.shape[1]), bias)

def mix_layer(h, pos, mstate, gstate, window_fn, sb_fn, w_in, b_ig, b_fg, g_head_a,
              w_gla_a2, b_gla_a, g_head_b, b_sb, w_out):
    B, T, _ = h.shape
    f32 = jnp.float32
    (aq, ak, av, ai, af, ao, bq, bk, bv, bg, blr,
     cq, ck, cv, dq, dk, dv) = split_columns(h @ w_in)

    def heads(x, n):
        return x.reshape(B, T, n, -1)

    def bhtd(x, n):
        return heads(x, n).transpose(0, 2, 1, 3).astype(f32)

    qa, ka, va = bhtd(aq, H_A), bhtd(ak, H_A) * (HEAD_DIM ** -0.5), bhtd(av, H_A)
    ig = (ai.astype(f32) + b_ig.astype(f32)).transpose(0, 2, 1)
    lf = jax.nn.log_sigmoid(af.astype(f32) + b_fg.astype(f32)).transpose(0, 2, 1)
    mstate, ha = run_chunks(mlstm_chunk, mstate, (qa, ka, va, ig, lf))
    ha = head_rms(ha.transpose(0, 2, 1, 3), g_head_a) * jax.nn.sigmoid(ao.astype(f32))
    qb, kb, vb = bhtd(bq, H_B) * (DK_B ** -0.5), bhtd(bk, H_B), bhtd(bv, H_B)
    la = jax.nn.log_sigmoid((blr @ w_gla_a2 + b_gla_a).astype(f32)) / GLA_TAU
    la = la.reshape(B, T, H_B, DK_B).transpose(0, 2, 1, 3)
    gstate, hb = run_chunks(gla_chunk, gstate, (qb, kb, vb, la))
    hb = head_rms(hb.transpose(0, 2, 1, 3), g_head_b) * jax.nn.silu(bg.astype(f32))
    qc, kc, vc = rope(heads(cq, H_C), pos), rope(heads(ck, H_C), pos), heads(cv, H_C)
    hc = window_fn(qc, kc, vc).reshape(B, T, -1)
    qd, kd, vd = heads(dq, H_D), heads(dk, H_D), heads(dv, H_D)
    hd = sb_fn(qd, kd, vd, b_sb).reshape(B, T, -1)
    mixed = jnp.concatenate([ha.astype(h.dtype), hb.astype(h.dtype), hc, hd], -1)
    return mixed @ w_out, kc, vc, kd, vd, mstate, gstate

def setup_inputs(seed: int = 0) -> dict:
    key = jax.random.key(seed)
    ks = iter(jax.random.split(key, 48))

    def nrm(shape, scale):
        return jax.random.normal(next(ks), shape, jnp.float32) * scale

    def gain(width):
        return 1.0 + nrm((DEPTH, width), 0.05)

    n_pages = PAST_LEN // PAGE_SIZE
    n_used = DEC_BATCH * n_pages
    n_pool = n_used + n_used // 4
    w_buf = min(MAX_WINDOW, PAST_LEN)
    return {
        "x_prompt": nrm((BATCH, SEQ, D_MODEL), 1.0),
        "x_sample": nrm((DEC_BATCH, DEC_SEQ, D_MODEL), 1.0),
        "cache_sb_k": nrm((DEPTH, n_pool, PAGE_SIZE, H_D, HEAD_DIM), 1.0),
        "cache_sb_v": nrm((DEPTH, n_pool, PAGE_SIZE, H_D, HEAD_DIM), 1.0),
        "page_table": jax.random.permutation(next(ks), n_pool)[:n_used].reshape(DEC_BATCH, n_pages).astype(jnp.int32),
        "cache_win_k": nrm((DEPTH, DEC_BATCH, w_buf, H_C, HEAD_DIM), 1.0),
        "cache_win_v": nrm((DEPTH, DEC_BATCH, w_buf, H_C, HEAD_DIM), 1.0),
        "state_mlstm_c": nrm((DEPTH, DEC_BATCH, H_A, HEAD_DIM, HEAD_DIM), 1.0),
        "state_mlstm_n": nrm((DEPTH, DEC_BATCH, H_A, HEAD_DIM), 1.0),
        "state_mlstm_m": nrm((DEPTH, DEC_BATCH, H_A), 1.0),
        "state_gla_s": nrm((DEPTH, DEC_BATCH, H_B, DK_B, HEAD_DIM), 0.5),
        "g_ffn1_pre": gain(D_MODEL),
        "w_ffn1_in": nrm((DEPTH, D_MODEL, 2 * D_FF), D_MODEL ** -0.5),
        "w_ffn1_out": nrm((DEPTH, D_FF, D_MODEL), D_FF ** -0.5),
        "g_ffn1_post": gain(D_MODEL),
        "g_mix_pre": gain(D_MODEL),
        "w_in": nrm((DEPTH, D_MODEL, N_IN), D_MODEL ** -0.5),
        "b_ig": nrm((DEPTH, H_A), 0.1),
        "b_fg": 3.0 + nrm((DEPTH, H_A), 0.5),
        "g_head_a": gain(H_A * HEAD_DIM),
        "w_gla_a2": nrm((DEPTH, GLA_RANK, H_B * DK_B), GLA_RANK ** -0.5),
        "b_gla_a": nrm((DEPTH, H_B * DK_B), 0.1),
        "g_head_b": gain(H_B * HEAD_DIM),
        "b_sb": SB_BIAS_INIT + nrm((DEPTH, H_D), 0.5),
        "w_out": nrm((DEPTH, MIX_WIDTH, D_MODEL), MIX_WIDTH ** -0.5),
        "g_mix_post": gain(D_MODEL),
        "g_ffn2_pre": gain(D_MODEL),
        "w_ffn2_in": nrm((DEPTH, D_MODEL, 2 * D_FF), D_MODEL ** -0.5),
        "w_ffn2_out": nrm((DEPTH, D_FF, D_MODEL), D_FF ** -0.5),
        "g_ffn2_post": gain(D_MODEL),
    }

def reference(x_prompt, x_sample, cache_sb_k, cache_sb_v, page_table, cache_win_k, cache_win_v,
              state_mlstm_c, state_mlstm_n, state_mlstm_m, state_gla_s,
              g_ffn1_pre, w_ffn1_in, w_ffn1_out, g_ffn1_post, g_mix_pre, w_in, b_ig, b_fg,
              g_head_a, w_gla_a2, b_gla_a, g_head_b, b_sb, w_out, g_mix_post,
              g_ffn2_pre, w_ffn2_in, w_ffn2_out, g_ffn2_post):
    f32 = jnp.float32

    def layer(x, l, pos, mstate, gstate, window_fn, sb_fn):
        h = rms_norm(x, g_ffn1_pre[l])
        x = x + 0.5 * rms_norm(swiglu(h, w_ffn1_in[l], w_ffn1_out[l]), g_ffn1_post[l])
        mix, kc, vc, kd, vd, mstate, gstate = mix_layer(
            rms_norm(x, g_mix_pre[l]), pos, mstate, gstate, window_fn, sb_fn,
            w_in[l], b_ig[l], b_fg[l], g_head_a[l], w_gla_a2[l], b_gla_a[l], g_head_b[l], b_sb[l], w_out[l])
        x = x + rms_norm(mix, g_mix_post[l])
        h = rms_norm(x, g_ffn2_pre[l])
        x = x + 0.5 * rms_norm(swiglu(h, w_ffn2_in[l], w_ffn2_out[l]), g_ffn2_post[l])
        return x, kd, vd, kc, vc, mstate, gstate

    bp, tp, _ = x_prompt.shape
    pos_p = jnp.arange(tp)
    keep = min(MAX_WINDOW, tp)
    x = x_prompt
    rows_p = []
    for l in range(DEPTH):
        mstate = (jnp.zeros((bp, H_A, HEAD_DIM, HEAD_DIM), f32), jnp.zeros((bp, H_A, HEAD_DIM), f32),
                  jnp.zeros((bp, H_A), f32))
        gstate = jnp.zeros((bp, H_B, DK_B, HEAD_DIM), f32)
        x, kd, vd, kc, vc, (mc, mn, mm), gs = layer(x, l, pos_p, mstate, gstate,
                                                    prompt_window, prompt_stick_breaking)
        rows_p.append((kd, vd, kc[:, tp - keep:], vc[:, tp - keep:], mc, mn, mm, gs))
    y_prompt = x
    p_sb_k, p_sb_v, p_win_k, p_win_v, p_mlstm_c, p_mlstm_n, p_mlstm_m, p_gla_s = [jnp.stack(z, 0) for z in zip(*rows_p)]

    past = page_table.shape[1] * PAGE_SIZE
    pos_s = past + jnp.arange(x_sample.shape[1])
    x = x_sample
    rows_s = []
    for l in range(DEPTH):
        mstate = (state_mlstm_c[l].astype(f32), state_mlstm_n[l].astype(f32), state_mlstm_m[l].astype(f32))
        gstate = state_gla_s[l].astype(f32)
        window_fn = functools.partial(sample_window, buf_k=cache_win_k[l], buf_v=cache_win_v[l])
        sb_fn = functools.partial(sample_stick_breaking, pool_k=cache_sb_k[l], pool_v=cache_sb_v[l],
                                  page_table=page_table)
        x, kd, vd, kc, vc, (mc, mn, mm), gs = layer(x, l, pos_s, mstate, gstate, window_fn, sb_fn)
        rows_s.append((kd, vd, kc, vc, mc, mn, mm, gs))
    y_sample = x
    s_sb_k, s_sb_v, s_win_k, s_win_v, s_mlstm_c, s_mlstm_n, s_mlstm_m, s_gla_s = [jnp.stack(z, 0) for z in zip(*rows_s)]

    return (y_prompt, y_sample,
            p_sb_k, p_sb_v, p_win_k, p_win_v, p_mlstm_c, p_mlstm_n, p_mlstm_m, p_gla_s,
            s_sb_k, s_sb_v, s_win_k, s_win_v, s_mlstm_c, s_mlstm_n, s_mlstm_m, s_gla_s)


_drawn_inputs = setup_inputs


def setup_inputs(seed=0):
    import zlib

    import numpy as np

    out = dict(_drawn_inputs(seed))
    spreads = {}
    factors = {}
    for name, (base, spread) in spreads.items():
        noise = np.random.default_rng([zlib.crc32(name.encode()), seed]).standard_normal(out[name].shape)
        drawn = base * np.exp(spread * noise) if base else spread * noise
        out[name] = __import__('jax').numpy.asarray(drawn.astype(out[name].dtype))
    for name, factor in factors.items():
        out[name] = (out[name] * factor).astype(out[name].dtype)
    return out
```

```python
from contextlib import ExitStack, contextmanager

import numpy as np
import concourse.bass as bass
from concourse import mybir

ALU = mybir.AluOpType
ACT = mybir.ActivationFunctionType
AX = mybir.AxisListType
F32 = mybir.dt.float32
I32 = mybir.dt.int32

D_MODEL = 1024
SEQ = 512
DEPTH = 2
DEC_BATCH = 8
DEC_SEQ = 8
PAST_LEN = 2048
PAGE = 128
N_PAGES = PAST_LEN // PAGE
N_POOL = DEC_BATCH * N_PAGES * 5 // 4
HD = 64
H = 4
DK_B = HD // 2
RANK = 16
TAU = 16.0
CHUNK = 64
D_FF = 2 * D_MODEL
EPS = 1e-6
ROPE_HALF = HD // 8
THETA = 500000.0
DILATIONS = ((128, 1), (512, 4), (2048, 16))
NEG = -1e30

P = 128
KC = D_MODEL // P
W4 = H * HD
NS = DEC_BATCH * DEC_SEQ
NT = SEQ + NS
PT_TILES = SEQ // P
TILES = PT_TILES + 1
ROWS = [P] * PT_TILES + [NS]
HALF = NT // 2
FF = D_FF // P

SIZES = (W4, W4, W4, H, H, W4, H * DK_B, H * DK_B, W4, W4, RANK, W4, W4, W4, W4, W4, W4)
NAMES = ("aq", "ak", "av", "ai", "af", "ao", "bq", "bk", "bv", "bg", "blr", "cq", "ck", "cv", "dq", "dk", "dv")
COL = {n: sum(SIZES[:i]) for i, n in enumerate(NAMES)}
N_IN = sum(SIZES)

NEAR = DILATIONS[1][0]
FAR_TILES = (PAST_LEN - NEAR) // (2 * P)
WIN_TILES = FAR_TILES + NEAR // P
SG = 4
GROUPS = DEC_BATCH // SG


def tok(t):
    return slice(t * P, t * P + ROWS[t])


PARTS = ((slice(0, P), slice(0, PT_TILES)), (slice(0, NS), slice(PT_TILES, TILES)))


def constants():
    f = np.float32
    c = {}
    c["ident"] = np.eye(P, dtype=f)
    p = np.arange(P)
    u = np.arange(SEQ)

    def log_count(delta):
        n = sum(((delta >= 0) & (delta <= w) & (delta % d == 0)).astype(np.int64) for w, d in DILATIONS)
        return np.where(n > 0, np.log(np.maximum(n, 1)), NEG).astype(f)

    c["win_mask"] = log_count(p[:, None] + (SEQ - P) - u[None, :])
    c["strict_mask"] = np.where(p[:, None] > p[None, :], 0, NEG).astype(f)
    c["turned_mask"] = np.where(p[None, :] >= p[:, None], 0, NEG).astype(f)
    c["gla_mask"] = ((p[None, :] >= p[:, None]) & (p[None, :] // CHUNK == p[:, None] // CHUNK)).astype(f)
    s = np.arange(NS)
    same = s[:, None] // DEC_SEQ == s[None, :] // DEC_SEQ
    ok = same & (s[None, :] >= s[:, None])
    c["s_turned_mask"] = np.where(ok, 0, NEG).astype(f)
    c["s_gla_mask"] = ok.astype(f)
    rs, rh, rq = p // (H * DEC_SEQ), p // DEC_SEQ % H, p % DEC_SEQ
    row = np.zeros((P, WIN_TILES * P), f)
    for t in range(WIN_TILES):
        if t < FAR_TILES:
            pos = t * 2 * P + (np.arange(P) // 8) * 16 + np.arange(P) % 8
        else:
            pos = PAST_LEN - NEAR + (t - FAR_TILES) * P + np.arange(P)
        row[:, t * P:(t + 1) * P] = log_count(PAST_LEN + rq[:, None] - pos[None, :])
    c["s_win_mask"] = row
    g = np.arange(GROUPS)
    mine = (g[:, None, None] * SG + rs[None, :, None]) == (s // DEC_SEQ)[None, None, :]
    delta = (rq[:, None] - (s % DEC_SEQ)[None, :])[None]
    c["s_win_new"] = np.where(mine, log_count(delta), NEG).astype(f).transpose(1, 0, 2).copy()
    c["s_sb_new"] = np.where(mine & (delta > 0), 0, NEG).astype(f).transpose(1, 0, 2).copy()
    c["head_cols"] = np.repeat((rh[:, None] == np.arange(H)[None, :]), HD, axis=1).astype(f)
    c["gather_rows"] = ((rs * DEC_SEQ + rq)[:, None] == np.arange(SG * DEC_SEQ)[None, :]).astype(f)
    c["pair_head"] = np.stack([(np.arange(H)[None, :] == 2 * pr + (p // HD)[:, None]) for pr in range(2)],
                              1).astype(f)
    c["bias_rows"] = (np.arange(H)[:, None] == rh[None, :]).astype(f)
    c["head_rows"] = np.repeat(np.eye(H, dtype=f)[:, :, None], P, axis=2)
    first = (np.arange(NT) >= SEQ) & ((np.arange(NT) - SEQ) % DEC_SEQ == 0)
    c["keep_a"] = np.repeat(np.where(first, 0, 1)[None], H, 0).astype(f)
    c["cut_a"] = np.repeat(np.where(first, NEG, 0)[None], H, 0).astype(f)
    start = first | ((np.arange(NT) < SEQ) & (np.arange(NT) % CHUNK == 0))
    c["keep_b"] = np.repeat(np.where(start, 0, 1)[None], P, 0).astype(f)
    q = np.arange(DEC_BATCH // 2)
    req = 2 * q[None, :] + (p // HD)[:, None]
    c["pair_tokens"] = (req[:, :, None] == (s // DEC_SEQ)[None, None, :]).astype(f)
    c["pair_last"] = ((req.T[None] * DEC_SEQ + DEC_SEQ - 1) == s[:, None, None]).astype(f)
    c["token_request"] = ((s // DEC_SEQ)[:, None] == np.arange(DEC_BATCH)[None, :]).astype(f)
    c["request_tokens"] = np.repeat(c["token_request"].T[None], P, 0).copy()
    c["gla_head"] = ((p // DK_B)[:, None] == np.arange(H)[None, :]).astype(f)
    c["gla_cols"] = np.repeat(c["gla_head"], HD, axis=1)
    inv = np.float32(THETA) ** (-np.arange(ROPE_HALF, dtype=f) / np.float32(ROPE_HALF))
    pos = np.concatenate([np.arange(SEQ), PAST_LEN + np.arange(NS) % DEC_SEQ, np.zeros(P - NS)]).astype(f)
    ang = (pos[:, None] * inv[None, :].astype(f)).astype(f)
    for name, fn in (("cos", np.cos), ("sin", np.sin)):
        c[name] = fn(ang).astype(f).reshape(TILES, P, ROPE_HALF).transpose(1, 0, 2).copy()
    return c


RESIDENT = ("ident",)


@contextmanager
def stage(nc, name, sems):
    with ExitStack() as st:
        S = dict(**{s: st.enter_context(nc.semaphore(f"{name}_{s}")) for s in sems.split()})
        st2 = ExitStack()

        def sb(n, shape, dt=F32):
            return st.enter_context(nc.sbuf_tensor(f"{name}_{n}", shape, dt))

        with st2:
            block = st2.enter_context(nc.Block())
            yield S, sb, block
        nums = sorted(s.num for s in S.values())
        while nums:
            run = 1
            while run < len(nums) and nums[run] == nums[0] + run:
                run += 1
            nc.all_engine_barrier(sems_to_clear=range(nums[0], nums[0] + run))
            nums = nums[run:]


def stepper(eng, sem):
    n = [0]

    def step(ins):
        n[0] += 1
        ins.then_inc(sem, 1)
        eng.wait_ge(sem, n[0])
    return step


def layer_row(w, l):
    return w[bass.ds(l, 1), :].rearrange("o n -> (o n)").partition_broadcast(P)


def layer_col(w, l):
    return w[bass.ds(l, 1), :].rearrange("o n -> n o")


PRE_SEMS = "pre_gain_loaded squares_done rms_done inv_done normed turned low_copied high_copied "


def pre_buffers(sb):
    return dict(gain=sb("pre_gain", [P, D_MODEL]), scratch=sb("scratch", [P, D_MODEL]),
                           rms=sb("pre_rms", [P, TILES]), inv=sb("pre_inv", [P, TILES]),
                           normed=sb("normed", [P, 2, D_MODEL]))


def pre_scalar(act, E, S, B):
    for t, r in enumerate(ROWS):
        if t > 0:
            act.wait_ge(S["squares_done"], t)
        act.activation(B["scratch"][:r, :], E["x"][:r, t, :], ACT.Square,
                       accum_out=E["sumsq"][:r, t:t + 1]).then_inc(S["squares_done"], 1)
    act.wait_ge(S["squares_done"], TILES)
    act.activation(B["rms"][:, :], E["sumsq"][:, :], ACT.Sqrt, bias=E["eps"][:, 0:1], scale=1.0 / D_MODEL).then_inc(S["rms_done"], 1)
    for t in range(TILES):
        act.wait_ge(S["turned"], 2 * t + 1)
        act.activation(E["hT"][:, 0:4, tok(t)],
                       E["ps"][:, 2 * (t % 2), 0:4 * ROWS[t]].rearrange("p (c r) -> p c r", c=4),
                       ACT.Copy).then_inc(S["low_copied"], 1)


def pre_vector(dve, E, S, B):
    dve.wait_ge(S["rms_done"], 1)
    dve.reciprocal(B["inv"][:, :], B["rms"][:, :]).then_inc(S["inv_done"], 1)
    dve.wait_ge(S["inv_done"], 1)
    dve.wait_ge(S["pre_gain_loaded"], 16)
    for t in range(TILES + 1):
        if t < TILES:
            r = ROWS[t]
            dve.scalar_tensor_tensor(B["normed"][:r, t % 2, :], E["x"][:r, t, :], B["inv"][:r, t:t + 1], B["gain"][:r, :],
                                     ALU.mult, ALU.mult).then_inc(S["normed"], 1)
        if t > 0:
            dve.wait_ge(S["turned"], 2 * t)
            dve.tensor_copy(E["hT"][:, 4:8, tok(t - 1)],
                            E["ps"][:, 2 * ((t - 1) % 2) + 1, 0:4 * ROWS[t - 1]].rearrange("p (c r) -> p c r", c=4)
                            ).then_inc(S["high_copied"], 1)


def pre_tensor(pe, E, S, B):
    for t, r in enumerate(ROWS):
        pe.wait_ge(S["normed"], t + 1)
        for half in range(2):
            if t >= 2:
                pe.wait_ge((S["low_copied"], S["high_copied"])[half], t - 1)
            for c in range(4):
                mm = pe.transpose(E["ps"][:, 2 * (t % 2) + half, c * r:(c + 1) * r],
                                  B["normed"][:r, t % 2, (4 * half + c) * P:(4 * half + c + 1) * P], E["ident"][:r, :r])
            mm.then_inc(S["turned"], 1)
    pe.wait_ge(S["low_copied"], TILES)
    pe.wait_ge(S["high_copied"], TILES)


OUT_SLOTS = 3
POST_SEMS = ("out_loaded0 out_loaded1 out_loaded2 post_gain_loaded group_done half_done "
             "y_act y_dve y_squares y_rms y_inv scaled added ")


def post_buffers(sb):
    return dict(w=sb("w_out", [P, OUT_SLOTS, 4, 512]), y=sb("y", [P, TILES, D_MODEL]),
                           gain=sb("post_gain", [P, D_MODEL]), rms=sb("post_rms", [P, TILES]),
                           inv=sb("post_inv", [P, TILES]))


def post_groups(nk):
    return [(h, k) for h in range(2) for k in range(0, nk, 4)]


def post_sync(sp, S, B, w, l, nk):
    wv = w[bass.ds(l, 1)].rearrange("o (k p) n -> p (o k) n", p=P)
    loaded = (S["out_loaded0"], S["out_loaded1"], S["out_loaded2"])
    for n, (h, k) in enumerate(post_groups(nk)):
        if n >= OUT_SLOTS:
            sp.wait_ge(S["group_done"], n - OUT_SLOTS + 1)
        sp.dma_start(B["w"][:, n % OUT_SLOTS], wv[:, k:k + 4, h * 512:(h + 1) * 512]).then_inc(loaded[n % OUT_SLOTS], 16)


def post_tensor(pe, E, S, B, lhs, nk):
    loaded = (S["out_loaded0"], S["out_loaded1"], S["out_loaded2"])
    for n, (h, k) in enumerate(post_groups(nk)):
        pe.wait_ge(loaded[n % OUT_SLOTS], 16 * (n // OUT_SLOTS + 1))
        for kk in range(4):
            for t, r in enumerate(ROWS):
                if h == 1 and k + kk == 0:
                    pe.wait_ge(S["y_act"] if t % 2 == 0 else S["y_dve"], t // 2 + 1)
                mm = pe.matmul(E["ps"][:r, t, 0:512], lhs[:, k + kk, tok(t)], B["w"][:, n % OUT_SLOTS, kk, :],
                               start=(k + kk == 0), stop=(k + kk == nk - 1))
                if k + kk == nk - 1 and t < TILES - 1:
                    mm.then_inc(S["half_done"], 1)
        mm.then_inc(S["group_done"], 1)


def post_wait(eng, S, h, t, nk):
    if t < TILES - 1:
        eng.wait_ge(S["half_done"], (TILES - 1) * h + t + 1)
    else:
        eng.wait_ge(S["group_done"], (h + 1) * nk // 4)


def post_scalar(act, E, S, B, nk, weight):
    for h in range(2):
        for t in range(0, TILES, 2):
            post_wait(act, S, h, t, nk)
            act.activation(B["y"][:ROWS[t], t, h * 512:(h + 1) * 512], E["ps"][:ROWS[t], t, 0:512],
                           ACT.Copy).then_inc(S["y_act"], 1)
    act.wait_ge(S["y_act"], 2 * 3)
    act.wait_ge(S["y_dve"], 2 * 2)
    for t, r in enumerate(ROWS):
        if t > 0:
            act.wait_ge(S["y_squares"], t)
        act.activation(B["w"][:r, 0:2].rearrange("p a b c -> p (a b c)")[:, 0:D_MODEL], B["y"][:r, t, :], ACT.Square,
                       accum_out=E["sumsq"][:r, t:t + 1]).then_inc(S["y_squares"], 1)
    act.wait_ge(S["y_squares"], TILES)
    act.activation(B["rms"][:, :], E["sumsq"][:, :], ACT.Sqrt, bias=E["eps"][:, 1:2] if weight == 0.5 else E["eps"][:, 0:1],
                   scale=1.0 / D_MODEL / weight ** 2).then_inc(S["y_rms"], 1)


def post_vector(dve, E, S, B, nk):
    for h in range(2):
        for t in range(1, TILES, 2):
            post_wait(dve, S, h, t, nk)
            dve.tensor_copy(B["y"][:ROWS[t], t, h * 512:(h + 1) * 512], E["ps"][:ROWS[t], t, 0:512]).then_inc(S["y_dve"], 1)
    dve.wait_ge(S["y_rms"], 1)
    dve.reciprocal(B["inv"][:, :], B["rms"][:, :]).then_inc(S["y_inv"], 1)
    dve.wait_ge(S["y_inv"], 1)
    dve.wait_ge(S["post_gain_loaded"], 16)
    for t, r in enumerate(ROWS):
        dve.scalar_tensor_tensor(B["y"][:r, t, :], B["y"][:r, t, :], B["inv"][:r, t:t + 1], B["gain"][:r, :],
                                 ALU.mult, ALU.mult).then_inc(S["scaled"], 1)
    for t, r in enumerate(ROWS):
        dve.wait_ge(S["scaled"], t + 1)
        dve.tensor_tensor(E["x"][:r, t, :], E["x"][:r, t, :], B["y"][:r, t, :], ALU.add).then_inc(S["added"], 1)


def ffn(nc, E, l, name, g_pre, w_in, w_out, g_post):
    STEP = 2 * P
    STEPS = D_FF // STEP
    sems = PRE_SEMS + POST_SEMS + "in_loaded0 in_loaded1 step_done unit_done silu_done a_ready"
    with stage(nc, name, sems) as (S, sb, block):
        B = pre_buffers(sb)
        C = post_buffers(sb)
        w = sb("w_in", [P, 2, KC, 2, STEP])
        aT = sb("aT", [P, FF, NT])
        gate = sb("gate", [P, 4, HALF])
        in_loaded = (S["in_loaded0"], S["in_loaded1"])
        w_v = w_in[bass.ds(l, 1)].rearrange("o (c p) (b f) -> p b (o c) f", p=P, b=2)

        @block.sync
        def _(sp):
            sp.dma_start(B["gain"][:], layer_row(g_pre, l)).then_inc(S["pre_gain_loaded"], 16)

            def load(slot, j):
                for b in range(2):
                    sp.dma_start(w[:, slot, :, b, :], w_v[:, b, :, bass.ds(j * STEP, STEP)]).then_inc(
                        in_loaded[slot], 16)

            load(0, 0)
            load(1, 1)
            sp.dma_start(C["gain"][:], layer_row(g_post, l)).then_inc(S["post_gain_loaded"], 16)
            with sp.Fori(1, STEPS // 2) as i:
                for slot in range(2):
                    sp.wait_ge(S["step_done"], 2 * i + slot - 1)
                    load(slot, 2 * i + slot)
            post_sync(sp, S, C, w_out, l, FF)

        @block.tensor
        def _(pe):
            pre_tensor(pe, E, S, B)

            def two_steps(i, first):
                for slot in range(2):
                    pe.wait_ge(in_loaded[slot], 32 * i + 32)
                    for k in range(4):
                        if not (first and slot == 0):
                            pe.wait_ge(S["a_ready"], 8 * i + 4 * slot + k - 3)
                        for b in range(2):
                            for c in range(KC):
                                mm = pe.matmul(E["ps"][:, 2 * k + b, 0:HALF],
                                               w[:, slot, c, b, (k // 2) * P:(k // 2 + 1) * P],
                                               E["hT"][:, c, (k % 2) * HALF:(k % 2 + 1) * HALF],
                                               start=(c == 0), stop=(c == KC - 1))
                        if k < 3:
                            mm.then_inc(S["unit_done"], 1)
                    mm.then_inc(S["step_done"], 1)

            two_steps(0, True)
            with pe.Fori(1, STEPS // 2) as i:
                two_steps(i, False)
            pe.wait_ge(S["a_ready"], 4 * STEPS)
            post_tensor(pe, E, S, C, aT, FF)

        def unit_wait(eng, i, slot, k):
            if k < 3:
                eng.wait_ge(S["unit_done"], 6 * i + 3 * slot + k + 1)
            else:
                eng.wait_ge(S["step_done"], 2 * i + slot + 1)

        @block.scalar
        def _(act):
            pre_scalar(act, E, S, B)

            def two_steps(i, first):
                for slot in range(2):
                    for k in range(4):
                        unit_wait(act, i, slot, k)
                        if not (first and slot == 0):
                            act.wait_ge(S["a_ready"], 8 * i + 4 * slot + k - 3)
                        act.activation(gate[:, k, :], E["ps"][:, 2 * k, 0:HALF], ACT.Silu).then_inc(S["silu_done"], 1)

            two_steps(0, True)
            with act.Fori(1, STEPS // 2) as i:
                two_steps(i, False)
            post_scalar(act, E, S, C, FF, 0.5)

        @block.vector
        def _(dve):
            pre_vector(dve, E, S, B)
            with dve.Fori(0, STEPS // 2) as i:
                for slot in range(2):
                    for k in range(4):
                        dve.wait_ge(S["silu_done"], 8 * i + 4 * slot + k + 1)
                        dve.tensor_tensor(aT[:, bass.ds(4 * i + 2 * slot + k // 2, 1),
                                             (k % 2) * HALF:(k % 2 + 1) * HALF].rearrange("p o n -> p (o n)"),
                                          gate[:, k, :], E["ps"][:, 2 * k + 1, 0:HALF], ALU.mult).then_inc(S["a_ready"], 1)
            post_vector(dve, E, S, C, FF)


BLOCKS = (
    ("turned", ((0, COL["aq"], 2 * W4),)),
    ("turned", ((0, COL["bq"], W4),)),
    ("turned", ((0, COL["dq"], 2 * W4),)),
    ("rows", ((0, COL["ak"], 2 * W4),)),
    ("rows", ((0, COL["ao"], W4), (W4, COL["cv"], W4))),
    ("rows", ((0, COL["bv"], 2 * W4),)),
    ("rows", ((0, COL["cq"], 2 * W4),)),
    ("rows", ((0, COL["dk"], 2 * W4),)),
)
AQ, AK, BQ, BK, DQ, DK = 0, 2, 4, 5, 6, 8
GATE_I, GATE_F, LOWRANK = 0, 32, 64
GATE_ROWS = LOWRANK + RANK
QK_SCALE = HD ** -0.5


def project(nc, E, M, l, g_pre, w_in, O):
    sems = PRE_SEMS + "loaded0 loaded1 gates_cleared gates_loaded unit_done act_out dve_out ones_set stored"
    with stage(nc, "pr", sems) as (S, sb, block):
        B = pre_buffers(sb)
        w = sb("w", [P, 2, KC, 512])
        wg = sb("w_gates", [P, KC, GATE_ROWS])
        w_v = w_in[bass.ds(l, 1)].rearrange("o (c p) f -> p (o c) f", p=P)
        loaded = (S["loaded0"], S["loaded1"])

        units = []
        for b, (kind, parts) in enumerate(BLOCKS):
            if kind == "turned":
                width = sum(n for _, _, n in parts)
                units += [(b, kind, m, half) for m in range(width // P) for half in range(2)]
                if b == 1:
                    units += [(b, "gates", 0, half) for half in range(2)]
            else:
                units += [(b, kind, t, 0) for t in range(TILES)]
        first_tile = {0: AQ, 1: BQ, 2: DQ}
        last_of_block = {u[0]: n for n, u in enumerate(units)}

        @block.sync
        def _(sp):
            sp.dma_start(B["gain"][:], layer_row(g_pre, l)).then_inc(S["pre_gain_loaded"], 16)
            for b, (kind, parts) in enumerate(BLOCKS):
                if b >= 2:
                    sp.wait_ge(S["unit_done"], last_of_block[b - 2] + 1)
                for dst, src, n in parts:
                    sp.dma_start(w[:, b % 2, :, dst:dst + n], w_v[:, :, src:src + n]).then_inc(loaded[b % 2], 16)
                if b == 1:
                    sp.wait_ge(S["gates_cleared"], 1)
                    for row, part, n in ((GATE_I, "ai", H), (GATE_F, "af", H), (LOWRANK, "blr", RANK)):
                        sp.dma_start(wg[:, :, row:row + n], w_v[:, :, COL[part]:COL[part] + n]).then_inc(
                            S["gates_loaded"], 16)
            sp.wait_ge(S["act_out"], (len(units) + 1) // 2)
            sp.wait_ge(S["dve_out"], len(units) // 2)
            n = 0
            for src, pn, sn in ((M["DKV"][:, :, 0:W4], "p_sb_k", "s_sb_k"), (M["DKV"][:, :, W4:], "p_sb_v", "s_sb_v"),
                                (M["CV"][:], "p_win_v", "s_win_v")):
                po = O[pn][bass.ds(l, 1)].rearrange("o b (t p) h d -> p (o b t) (h d)", p=P)
                so = O[sn][bass.ds(l, 1)].rearrange("o b t h d -> (o b t) (h d)")
                sp.dma_start(po, src[:, 0:PT_TILES, :]).then_inc(S["stored"], 16)
                sp.dma_start(so, src[:NS, PT_TILES, :]).then_inc(S["stored"], 16)
                n += 2
            sp.wait_ge(S["stored"], 16 * n)

        @block.tensor
        def _(pe):
            pre_tensor(pe, E, S, B)
            need = [0, 0]
            seen = -1
            for n, (b, kind, m, half) in enumerate(units):
                if b != seen:
                    seen = b
                    need[b % 2] += 16 * len(BLOCKS[b][1])
                    pe.wait_ge(loaded[b % 2], need[b % 2])
                if kind == "gates" and half == 0:
                    pe.wait_ge(S["gates_loaded"], 48)
                if n >= 8:
                    pe.wait_ge(S["act_out"] if n % 2 == 0 else S["dve_out"], (n - 8) // 2 + 1)
                for c in range(KC):
                    if kind == "turned":
                        out = E["ps"][:, n % 8, 0:HALF]
                        lhs, rhs = w[:, b % 2, c, m * P:(m + 1) * P], E["hT"][:, c, half * HALF:(half + 1) * HALF]
                    elif kind == "gates":
                        out = E["ps"][:GATE_ROWS, n % 8, 0:HALF]
                        lhs, rhs = wg[:, c, :], E["hT"][:, c, half * HALF:(half + 1) * HALF]
                    else:
                        out = E["ps"][:ROWS[m], n % 8, 0:512]
                        lhs, rhs = E["hT"][:, c, tok(m)], w[:, b % 2, c, :]
                    mm = pe.matmul(out, lhs, rhs, start=(c == 0), stop=(c == KC - 1))
                mm.then_inc(S["unit_done"], 1)

        def copies(n):
            b, kind, m, half = units[n]
            hs = slice(half * HALF, (half + 1) * HALF)
            bank = E["ps"][:, n % 8, :]
            if kind == "turned":
                tile = first_tile[b] + m
                scale = {AK: QK_SCALE, AK + 1: QK_SCALE, BQ: DK_B ** -0.5, DQ: QK_SCALE, DQ + 1: QK_SCALE}.get(tile, 1.0)
                return [(M["TR"][:, tile, hs], bank[:, 0:HALF], scale)]
            if kind == "gates":
                return [(M["gates"][:, hs], bank[:GATE_ROWS, 0:HALF], 1.0)]
            r = ROWS[m]
            lo, hi = bank[:r, 0:W4], bank[:r, W4:512]
            if b == 3:
                return [(M["KA"][:r, m, :], lo, QK_SCALE),
                        (M["VA"][:r, m, :, 0:HD], hi.rearrange("p (h d) -> p h d", h=H), 1.0)]
            if b == 4:
                return [(M["AO"][:r, m, :], lo, 1.0), (M["CV"][:r, m, :], hi, 1.0)]
            whole = {5: M["BVG"], 6: M["CQK"], 7: M["DKV"]}[b]
            return [(whole[:r, m, :], bank[:r, :], 1.0)]

        @block.scalar
        def _(act):
            pre_scalar(act, E, S, B)
            for n in range(0, len(units), 2):
                act.wait_ge(S["unit_done"], n + 1)
                for out, src, scale in copies(n):
                    ins = act.activation(out, src, ACT.Copy, scale=scale)
                ins.then_inc(S["act_out"], 1)

        @block.vector
        def _(dve):
            dve.memset(wg[:], 0.0).then_inc(S["gates_cleared"], 1)
            dve.memset(M["VA"][:, :, :, HD:HD + 1], 1.0).then_inc(S["ones_set"], 1)
            pre_vector(dve, E, S, B)
            for n in range(1, len(units), 2):
                dve.wait_ge(S["unit_done"], n + 1)
                for out, src, scale in copies(n):
                    if scale == 1.0:
                        ins = dve.tensor_copy(out, src)
                    else:
                        ins = dve.tensor_scalar(out, src, scale, None, ALU.mult)
                ins.then_inc(S["dve_out"], 1)


HEAD_SEMS = "squared ssq_done root_done root_inv_done head_scaled head_gated head_turned head_out "


def head_vector(dve, S, B, h, gate):
    n = len(PARTS)
    for rs, ts in PARTS:
        dve.tensor_tensor(B["sq"][rs, ts], h[rs, ts], h[rs, ts], ALU.mult).then_inc(S["squared"], 1)
    dve.wait_ge(S["squared"], n)
    for rs, ts in PARTS:
        dve.tensor_reduce(B["ssq"][rs, ts, :], B["sq"][rs, ts].rearrange("p t (h d) -> p t h d", h=H), AX.X,
                          ALU.add).then_inc(S["ssq_done"], 1)
    dve.wait_ge(S["root_done"], n)
    for rs, ts in PARTS:
        dve.reciprocal(B["ssq"][rs, ts, :], B["ssq"][rs, ts, :]).then_inc(S["root_inv_done"], 1)
    dve.wait_ge(S["root_inv_done"], n)
    for rs, ts in PARTS:
        hv = h[rs, ts].rearrange("p t (h d) -> p t h d", h=H)
        dve.tensor_tensor(hv, hv, B["ssq"][rs, ts, :].unsqueeze(3).to_broadcast(list(hv.shape)),
                          ALU.mult).then_inc(S["head_scaled"], 1)
    dve.wait_ge(S["head_scaled"], n)
    for rs, ts in PARTS:
        dve.tensor_tensor(h[rs, ts], h[rs, ts], gate[rs, ts], ALU.mult).then_inc(S["head_gated"], 1)


def head_scalar_root(act, E, S, B):
    act.wait_ge(S["ssq_done"], len(PARTS))
    for rs, ts in PARTS:
        act.activation(B["ssq"][rs, ts, :], B["ssq"][rs, ts, :], ACT.Sqrt, bias=E["eps"][rs, 0:1],
                       scale=1.0 / HD).then_inc(S["root_done"], 1)


def head_tensor(pe, E, S, h, bank):
    pe.wait_ge(S["head_gated"], len(PARTS))
    for t, r in enumerate(ROWS):
        for pair in range(2):
            n = 2 * t + pair
            if n >= 2:
                pe.wait_ge(S["head_out"], n - 1)
            pe.transpose(E["ps"][:, bank + n % 2, 0:r], h[:r, t, pair * P:(pair + 1) * P],
                         E["ident"][:r, :r]).then_inc(S["head_turned"], 1)


def head_scalar_out(act, E, M, S, chunk, bank):
    for t, r in enumerate(ROWS):
        for pair in range(2):
            n = 2 * t + pair
            act.wait_ge(S["head_turned"], n + 1)
            act.activation(M["mixT"][:, chunk + pair, tok(t)], E["ps"][:, bank + n % 2, 0:r], ACT.Copy).then_inc(S["head_out"], 1)


def head_buffers(sb):
    return dict(sq=sb("sq", [P, TILES, W4]), ssq=sb("ssq", [P, TILES, H]))


def mlstm(nc, E, M, l, I, O, C):
    sems = HEAD_SEMS + ("consts state bias gains dve_step act_step pe_step dve_to_act act_to_dve dve_to_pe "
                        "exps_done cols_turned cols_copied decay_copied n0_turned states_whole "
                        "query_bcast query_ready keys_ready bcast_done scores_done weights_done probs_done "
                        "out_whole out_copied p_state_done s_state_done s_state_added p_state_copied "
                        "n_turned n_copied stored gate_done")
    with stage(nc, "ml", sems) as (S, sb, block):
        HB = head_buffers(sb)
        sel = sb("sel", [H, H, P])
        mask = sb("mask", [P, P])
        s_mask = sb("s_mask", [NS, NS])
        keep = sb("keep", [H, NT])
        cut = sb("cut", [H, NT])
        pair_tok = sb("pair_tok", [P, DEC_BATCH // 2, NS])
        pair_last = sb("pair_last", [NS, DEC_BATCH // 2, P])
        tok_req = sb("tok_req", [NS, DEC_BATCH])
        b_i = sb("b_i", [H, 1])
        b_f = sb("b_f", [P, 1])
        m0 = sb("m0", [H, DEC_BATCH])
        n0 = sb("n0", [4 * H, P])
        gain = sb("gain", [P, W4])
        c0 = sb("c0", [P, 4, H, HD + 1])
        ig = sb("ig", [H, NT])
        fy = sb("fy", [H, NT])
        sp_ = sb("softplus", [H, NT])
        lf = sb("lf", [H, NT])
        lfc = sb("lf_cut", [H, NT])
        floor = sb("floor", [H, NT])
        st0 = sb("start", [H, DEC_BATCH])
        bsum = sb("bsum", [H, NT])
        m = sb("m", [H, NT])
        a = sb("a", [H, NT])
        wrow = sb("wrow", [H, NT])
        ws = sb("ws", [H, NT])
        em = sb("em", [H, NT])
        ea = sb("ea", [H, NS])
        cols = sb("cols", [P, 3, TILES, H])
        ea_col = sb("ea_col", [NS, H])
        decay = sb("decay", [P, 4, H])
        qd = sb("qd", [P, H, NS])
        qm = sb("qm", [P, H, 4, NS])
        km = sb("km", [NS, H, DEC_BATCH, HD])
        ex = sb("ex", [P, 2, SEQ])
        pr = sb("pr", [P, 2, SEQ])
        oc = sb("oc", [P, H, TILES, HD + 1])
        den = sb("den", [P, TILES, H])
        den2 = sb("den2", [P, TILES, H])
        hA = sb("hA", [P, TILES, W4])
        pc = sb("pc", [HD, H, HD + 1])
        pn = sb("pn", [4 * H, P])
        np_ = sb("np", [H, HD])
        ps = E["ps"]
        first = SEQ
        last = SEQ + DEC_SEQ - 1

        def s_rows(x):
            return x[:, first:NT].rearrange("p (r t) -> p r t", t=DEC_SEQ)

        @block.sync
        def _(sp):
            for dst, n in ((sel, "head_rows"), (mask, "turned_mask"), (s_mask, "s_turned_mask"), (keep, "keep_a"),
                           (cut, "cut_a"), (pair_tok, "pair_tokens"), (pair_last, "pair_last"),
                           (tok_req, "token_request")):
                sp.dma_start(dst[:], C[n]).then_inc(S["consts"], 16)
            sp.dma_start(b_i[:], layer_col(I["b_ig"], l)).then_inc(S["bias"], 16)
            sp.dma_start(b_f[GATE_F:GATE_F + H, :], layer_col(I["b_fg"], l)).then_inc(S["bias"], 16)
            with nc.allow_non_contiguous_dma(reason="32 stabilisers"):
                sp.dma_start(m0[:], I["state_mlstm_m"][bass.ds(l, 1)].rearrange("o r h -> h (o r)")).then_inc(S["bias"], 16)
            sp.dma_start(gain[:], layer_row(I["g_head_a"], l)).then_inc(S["gains"], 16)
            nv = I["state_mlstm_n"][bass.ds(l, 1)].rearrange("o (q j) h d -> q h (o j) d", j=2)
            for q in range(4):
                sp.dma_start(n0[H * q:H * q + H, :].rearrange("p (j d) -> p j d", j=2), nv[q]).then_inc(S["state"], 16)
            cv = I["state_mlstm_c"][bass.ds(l, 1)].rearrange("o (q j) h d e -> j h (o d) q e", j=2)
            for j in range(2):
                for h in range(H):
                    sp.dma_start(c0[j * HD:(j + 1) * HD, :, h, 0:HD], cv[j, h]).then_inc(S["state"], 16)
            n = 0
            sp.wait_ge(S["p_state_copied"], 1)
            sp.dma_start(O["p_mlstm_c"][bass.ds(l, 1)].rearrange("o b h d e -> d (o b h) e"), pc[:, :, 0:HD]).then_inc(S["stored"], 16)
            n += 1
            with nc.allow_non_contiguous_dma(reason="the last stabilisers"):
                sp.dma_start(O["p_mlstm_m"][bass.ds(l, 1)].rearrange("o b h -> h (o b)"), m[:, SEQ - 1:SEQ]).then_inc(S["stored"], 16)
                sp.dma_start(O["s_mlstm_m"][bass.ds(l, 1)].rearrange("o r h -> h (o r)"),
                             m[:, last:NT:DEC_SEQ]).then_inc(S["stored"], 16)
            n += 2
            sp.wait_ge(S["s_state_added"], 2 * H)
            cw = O["s_mlstm_c"][bass.ds(l, 1)].rearrange("o (q j) h d e -> j h (o d) q e", j=2)
            for j in range(2):
                for h in range(H):
                    sp.dma_start(cw[j, h], c0[j * HD:(j + 1) * HD, :, h, 0:HD]).then_inc(S["stored"], 16)
                    n += 1
            sp.wait_ge(S["n_copied"], 2)
            sp.dma_start(O["p_mlstm_n"][bass.ds(l, 1)].rearrange("o b h d -> (o b h) d"), np_[:]).then_inc(S["stored"], 16)
            nw = O["s_mlstm_n"][bass.ds(l, 1)].rearrange("o (q j) h d -> q h (o j) d", j=2)
            for q in range(4):
                sp.dma_start(nw[q], pn[H * q:H * q + H, :].rearrange("p (j d) -> p j d", j=2)).then_inc(S["stored"], 16)
            n += 5
            sp.wait_ge(S["stored"], 16 * n)

        units = [(h, c) for h in range(H) for c in range(TILES)]

        def width(c):
            return SEQ - c * P if c < PT_TILES else NS

        def queries(c):
            return slice(c * P, SEQ) if c < PT_TILES else slice(SEQ, NT)

        @block.vector
        def _(dve):
            step = stepper(dve, S["dve_step"])
            dve.wait_ge(S["bias"], 48)
            dve.wait_ge(S["consts"], 16 * 8)
            step(dve.tensor_scalar(ig[:], M["gates"][GATE_I:GATE_I + H, :], b_i[:, 0:1], None, ALU.add))
            dve.tensor_scalar(fy[:], M["gates"][GATE_F:GATE_F + H, :], b_f[GATE_F:GATE_F + H, 0:1], None,
                              ALU.add).then_inc(S["dve_to_act"], 1)
            dve.wait_ge(S["dve_to_act"], 1)
            dve.wait_ge(S["act_to_dve"], 3)
            step(dve.scalar_tensor_tensor(lf[:], fy[:], 0.0, sp_[:], ALU.min, ALU.subtract))
            step(dve.tensor_tensor_scan(bsum[:], keep[:], lf[:], 0.0, ALU.mult, ALU.add))
            step(dve.tensor_tensor(lfc[:], lf[:], cut[:], ALU.add))
            step(dve.tensor_copy(floor[:], ig[:]))
            step(dve.tensor_tensor(st0[:], lf[:, first:NT:DEC_SEQ], m0[:], ALU.add))
            step(dve.tensor_tensor(floor[:, first:NT:DEC_SEQ], ig[:, first:NT:DEC_SEQ], st0[:], ALU.max))
            step(dve.tensor_tensor_scan(m[:], lfc[:], floor[:], 0.0, ALU.add, ALU.max))
            step(dve.tensor_tensor(a[:], bsum[:], m[:], ALU.subtract))
            step(dve.tensor_tensor(wrow[:], ig[:], bsum[:], ALU.subtract))
            step(dve.tensor_scalar(ws[:, 0:SEQ], wrow[:, 0:SEQ], a[:, SEQ - 1:SEQ], None, ALU.add))
            step(dve.tensor_tensor(s_rows(ws), s_rows(wrow),
                                   a[:, last:NT:DEC_SEQ].unsqueeze(2).to_broadcast([H, DEC_BATCH, DEC_SEQ]), ALU.add))
            dve.tensor_tensor(ea[:].rearrange("p (r t) -> p r t", t=DEC_SEQ), s_rows(a),
                              m0[:].unsqueeze(2).to_broadcast([H, DEC_BATCH, DEC_SEQ]), ALU.add).then_inc(S["dve_to_act"], 1)

            dve.wait_ge(S["cols_turned"], 1)
            n = TILES * H
            cps = ps[:, 7, 0:3 * n].rearrange("p (k t h) -> p k t h", k=3, t=TILES)
            for rs, ts in PARTS:
                step(dve.tensor_copy(cols[rs, :, ts, :], cps[rs, :, ts, :]))
            dve.tensor_copy(ea_col[:], ps[:NS, 7, 3 * n:3 * n + H]).then_inc(S["cols_copied"], 1)
            dve.wait_ge(S["n0_turned"], 1)
            dve.wait_ge(S["state"], 16 * 12)
            step(dve.tensor_copy(decay[:], ps[:, 7, 0:16].rearrange("p (q h) -> p q h", q=4)))
            step(dve.tensor_copy(c0[:, :, :, HD], ps[:, 7, 16:32].rearrange("p (q h) -> p q h", q=4)))

            dve.wait_ge(S["query_bcast"], 1)
            for h in range(H):
                o = (h % 2) * HD
                for j in range(2):
                    step(dve.tensor_tensor(qd[j * HD:(j + 1) * HD, h, :], M["TR"][o:o + HD, AQ + h // 2, SEQ:NT],
                                           ps[j * HD:(j + 1) * HD, 6, h * NS:(h + 1) * NS], ALU.mult))
            for h in range(H):
                dve.tensor_tensor(qm[:, h], pair_tok[:], qd[:, h, :].unsqueeze(1).to_broadcast([P, 4, NS]),
                                  ALU.mult).then_inc(S["query_ready"], 1)
            for rs, ts in PARTS:
                kv = M["KA"][rs, ts, :].rearrange("p t (h d) -> p t h d", h=H)
                step(dve.tensor_tensor(kv, kv, cols[rs, 1, ts, :].unsqueeze(3).to_broadcast(list(kv.shape)), ALU.mult))
            for h in range(H):
                dve.tensor_tensor(km[:, h], M["KA"][:NS, PT_TILES, h * HD:(h + 1) * HD].unsqueeze(1).to_broadcast(
                    [NS, DEC_BATCH, HD]), tok_req[:].unsqueeze(2).to_broadcast([NS, DEC_BATCH, HD]),
                    ALU.mult).then_inc(S["keys_ready"], 1)
            for u, (h, c) in enumerate(units):
                dve.wait_ge(S["weights_done"], u + 1)
                dve.wait_ge(S["scores_done"], u + 1)
                r, w = ROWS[c], width(c)
                if u >= 2:
                    dve.wait_ge(S["pe_step"], u - 1)
                dve.tensor_tensor(pr[:r, u % 2, 0:w], ex[:r, u % 2, 0:w], ps[:r, 2 + u % 2, 0:w],
                                  ALU.mult).then_inc(S["probs_done"], 1)
            dve.wait_ge(S["p_state_done"], 1)
            dve.tensor_copy(pc[:], ps[:HD, 6, 0:H * (HD + 1)].rearrange("p (h e) -> p h e", h=H)).then_inc(S["p_state_copied"], 1)
            for h in range(H):
                dve.wait_ge(S["out_copied"], H)
                dve.tensor_tensor(c0[:, :, h, :], c0[:, :, h, :],
                                  decay[:, :, h].unsqueeze(2).to_broadcast([P, 4, HD + 1]), ALU.mult).then_inc(S["s_state_added"], 1)
                dve.wait_ge(S["s_state_added"], 2 * h + 1)
                dve.wait_ge(S["s_state_done"], h + 1)
                dve.tensor_tensor(c0[:, :, h, :], c0[:, :, h, :],
                                  ps[:, h % 2, 0:4 * (HD + 1)].rearrange("p (q e) -> p q e", q=4), ALU.add).then_inc(S["s_state_added"], 1)
            for rs, ts in PARTS:
                dv = oc[rs, :, ts, HD].rearrange("p h t -> p t h")
                step(dve.tensor_copy(den[rs, ts], dv))
                step(dve.scalar_tensor_tensor(den2[rs, ts], den[rs, ts], -1.0, den[rs, ts], ALU.mult, ALU.max))
                step(dve.tensor_tensor(den2[rs, ts], den2[rs, ts], cols[rs, 2, ts, :], ALU.max))
                step(dve.reciprocal(den2[rs, ts], den2[rs, ts]))
                for h in range(H):
                    nt = ts.stop - ts.start
                    step(dve.tensor_tensor(hA[rs, ts, h * HD:(h + 1) * HD], oc[rs, h, ts, 0:HD],
                                           den2[rs, ts, h].unsqueeze(2).to_broadcast([rs.stop, nt, HD]), ALU.mult))
            dve.wait_ge(S["gains"], 16)
            dve.wait_ge(S["gate_done"], 2)
            for rs, ts in PARTS:
                nt = ts.stop - ts.start
                step(dve.tensor_tensor(M["AO"][rs, ts, :], M["AO"][rs, ts, :],
                                       gain[rs].unsqueeze(1).to_broadcast([rs.stop, nt, W4]), ALU.mult))
            head_vector(dve, S, HB, hA, M["AO"])

        @block.scalar
        def _(act):
            act.wait_ge(S["dve_to_act"], 1)
            act.activation(sp_[:], fy[:], ACT.Abs).then_inc(S["act_to_dve"], 1)
            act.wait_ge(S["act_to_dve"], 1)
            act.activation(sp_[:], sp_[:], ACT.Exp, scale=-1.0).then_inc(S["act_to_dve"], 1)
            act.wait_ge(S["act_to_dve"], 2)
            act.activation(sp_[:], sp_[:], ACT.Ln, bias=1.0).then_inc(S["act_to_dve"], 1)
            act.wait_ge(S["dve_to_act"], 2)
            act.activation(ws[:], ws[:], ACT.Exp).then_inc(S["exps_done"], 1)
            act.activation(em[:], m[:], ACT.Exp, scale=-1.0).then_inc(S["exps_done"], 1)
            act.activation(ea[:], ea[:], ACT.Exp).then_inc(S["exps_done"], 1)
            act.wait_ge(S["cols_copied"], 1)
            for u, (h, c) in enumerate(units):
                act.wait_ge(S["bcast_done"], u + 1)
                r, w = ROWS[c], width(c)
                if u >= 2:
                    act.wait_ge(S["probs_done"], u - 1)
                act.activation(ex[:r, u % 2, 0:w], ps[:r, u % 2, 0:w], ACT.Exp,
                               bias=cols[:r, 0, c, h:h + 1]).then_inc(S["weights_done"], 1)
                if c == TILES - 1:
                    act.wait_ge(S["out_whole"], h + 1)
                    act.activation(oc[:, h, 0:PT_TILES, :],
                                   ps[:, 4 + h % 2, 0:PT_TILES * (HD + 1)].rearrange("p (t e) -> p t e", t=PT_TILES),
                                   ACT.Copy)
                    act.activation(oc[:NS, h, PT_TILES, :],
                                   ps[:NS, 4 + h % 2, PT_TILES * (HD + 1):TILES * (HD + 1)], ACT.Copy).then_inc(S["out_copied"], 1)
            for rs, ts in PARTS:
                act.activation(M["AO"][rs, ts, :], M["AO"][rs, ts, :], ACT.Sigmoid).then_inc(S["gate_done"], 1)
            head_scalar_root(act, E, S, HB)
            head_scalar_out(act, E, M, S, 0, 2)
            act.wait_ge(S["n_turned"], 1)
            act.activation(np_[:], ps[:H, 4, 0:HD], ACT.Copy).then_inc(S["n_copied"], 1)
            act.activation(pn[:], ps[:4 * H, 4, P:2 * P], ACT.Copy).then_inc(S["n_copied"], 1)

        @block.tensor
        def _(pe):
            pe.wait_ge(S["exps_done"], 3)
            n = TILES * H
            for k, row in enumerate((wrow, ws, em)):
                for t, r in enumerate(ROWS):
                    pe.transpose(ps[:r, 7, k * n + t * H:k * n + (t + 1) * H], row[:, tok(t)], E["ident"][:H, :H])
            pe.transpose(ps[:NS, 7, 3 * n:3 * n + H], ea[:], E["ident"][:H, :H]).then_inc(S["cols_turned"], 1)
            pe.wait_ge(S["consts"], 16 * 8)
            for h in range(H):
                mm = pe.matmul(ps[:, 6, h * NS:(h + 1) * NS], sel[:, h, :], ea[:], start=True, stop=True)
            mm.then_inc(S["query_bcast"], 1)
            pe.wait_ge(S["cols_copied"], 1)
            pe.wait_ge(S["state"], 16 * 12)
            for q in range(4):
                pe.matmul(ps[:, 7, q * H:(q + 1) * H], pair_last[:, q, :], ea_col[:], start=True, stop=True)
            pe.transpose(ps[:, 7, 16:32], n0[:], E["ident"][:4 * H, :4 * H]).then_inc(S["n0_turned"], 1)

            def scores(u):
                h, c = units[u]
                r, w, o = ROWS[c], width(c), (h % 2) * HD
                qs = queries(c)
                if u >= 2:
                    pe.wait_ge(S["weights_done"], u - 1)
                    pe.wait_ge(S["probs_done"], u - 1)
                pe.matmul(ps[:r, u % 2, 0:r], E["ident"][:r, :r], (mask if c < PT_TILES else s_mask)[:r, :r],
                          start=True, stop=False, skip_group_check=True)
                pe.matmul(ps[:r, u % 2, 0:w], sel[:, h, 0:r], a[:, qs], start=False, stop=True,
                          skip_group_check=True).then_inc(S["bcast_done"], 1)
                pe.matmul(ps[:r, 2 + u % 2, 0:w], M["TR"][o:o + HD, AK + h // 2, tok(c)],
                          M["TR"][o:o + HD, AQ + h // 2, qs], start=True, stop=True).then_inc(S["scores_done"], 1)

            def outputs(u):
                h, c = units[u]
                r = ROWS[c]
                pe.wait_ge(S["probs_done"], u + 1)
                if c == 0 and h >= 2:
                    pe.wait_ge(S["out_copied"], h - 1)
                if c < PT_TILES:
                    for t in range(c, PT_TILES):
                        mm = pe.matmul(ps[:, 4 + h % 2, t * (HD + 1):(t + 1) * (HD + 1)],
                                       pr[:r, u % 2, (t - c) * P:(t - c + 1) * P], M["VA"][:r, c, h, :],
                                       start=(c == 0 and t == 0), stop=(c == t), skip_group_check=True)
                    mm.then_inc(S["pe_step"], 1)
                else:
                    out = ps[:NS, 4 + h % 2, PT_TILES * (HD + 1):TILES * (HD + 1)]
                    pe.matmul(out, pr[:NS, u % 2, 0:NS], M["VA"][:NS, c, h, :], start=False, stop=False,
                              skip_group_check=True).then_inc(S["pe_step"], 1)
                    for q in range(4):
                        mm = pe.matmul(out, qm[:, h, q, :], c0[:, q, h, :], start=False, stop=(q == 3),
                                       skip_group_check=True)
                    mm.then_inc(S["out_whole"], 1)

            pe.wait_ge(S["query_ready"], H)
            for u in range(len(units) + 1):
                if u < len(units):
                    scores(u)
                if u >= 1:
                    outputs(u - 1)
            pe.wait_ge(S["keys_ready"], H)
            for h in range(H):
                for t in range(PT_TILES):
                    mm = pe.matmul(ps[:HD, 6, h * (HD + 1):(h + 1) * (HD + 1)], M["KA"][:, t, h * HD:(h + 1) * HD],
                                   M["VA"][:, t, h, :], start=(h == 0 and t == 0), stop=(t == PT_TILES - 1),
                                   skip_group_check=True)
            mm.then_inc(S["p_state_done"], 1)
            pe.wait_ge(S["weights_done"], len(units))
            for h in range(H):
                if h >= 2:
                    pe.wait_ge(S["s_state_added"], 2 * (h - 1))
                for q in range(4):
                    mm = pe.matmul(ps[:, h % 2, q * (HD + 1):(q + 1) * (HD + 1)],
                                   km[:, h, 2 * q:2 * q + 2, :].rearrange("p j d -> p (j d)"),
                                   M["VA"][:NS, PT_TILES, h, :], start=True, stop=True)
                mm.then_inc(S["s_state_done"], 1)
            pe.wait_ge(S["p_state_copied"], 1)
            pe.wait_ge(S["s_state_added"], 2 * H)
            pe.wait_ge(S["out_copied"], H)
            pe.transpose(ps[:H, 4, 0:HD], pc[:, :, HD], E["ident"][:HD, :HD])
            pe.transpose(ps[:4 * H, 4, P:2 * P], c0[:, :, :, HD].rearrange("p q h -> p (q h)"), E["ident"][:]).then_inc(S["n_turned"], 1)
            head_tensor(pe, E, S, hA, 2)


def gla(nc, E, M, l, I, O, C):
    NCH = SEQ // CHUNK
    sems = HEAD_SEMS + ("consts params states cleared dve_step low_ready pre_done pre_out y_ready act_to_dve "
                        "sums_ready exps_done factors_ready query_ready att_done att_ready keys_turned keys_ready "
                        "update_done state_new out_done out_copied s_query_ready s_keys_ready s_update_done "
                        "s_state_new gate_done stored")
    with stage(nc, "gl", sems) as (S, sb, block):
        HB = head_buffers(sb)
        keep = sb("keep", [P, NT])
        mask = sb("mask", [P, P])
        s_mask = sb("s_mask", [NS, NS])
        head = sb("head", [P, H])
        head_cols = sb("head_cols", [P, W4])
        req_tok = sb("req_tok", [P, DEC_BATCH, NS])
        tok_req = sb("tok_req", [NS, DEC_BATCH])
        w2 = sb("w2", [RANK, P])
        bias = sb("bias", [P, 1])
        gain = sb("gain", [P, W4])
        low = sb("low", [RANK, NT])
        y = sb("y", [P, NT])
        sp_ = sb("softplus", [P, NT])
        bsum = sb("bsum", [P, NT])
        mid = sb("mid", [P, NT])
        rest = sb("rest", [P, NT])
        e1 = sb("e1", [P, NT])
        whole = sb("whole", [P, NCH + DEC_BATCH])
        state = sb("state", [P, NCH + 1, W4])
        s_state = sb("s_state", [P, DEC_BATCH, W4])
        upd = sb("upd", [P, W4])
        qq = sb("qq", [P, NT])
        qi = sb("qi", [P, NT])
        kk = sb("kk", [P, NT])
        kd = sb("kd", [P, NT])
        qh = sb("qh", [P, 2, H, P])
        att = sb("att", [P, 2, H, P])
        kdt = sb("kdt", [P, TILES, P])
        s_qi = sb("s_qi", [P, DEC_BATCH, NS])
        s_kd = sb("s_kd", [NS, DEC_BATCH, P])
        hB = sb("hB", [P, TILES, W4])
        ps = E["ps"]

        def chunks(x):
            return (x[:, 0:SEQ].rearrange("p (c t) -> p c t", t=CHUNK),
                    x[:, SEQ:NT].rearrange("p (c t) -> p c t", t=DEC_SEQ))

        @block.sync
        def _(sp):
            for dst, n in ((keep, "keep_b"), (mask, "gla_mask"), (s_mask, "s_gla_mask"), (head, "gla_head"),
                           (head_cols, "gla_cols"), (req_tok, "request_tokens"), (tok_req, "token_request")):
                sp.dma_start(dst[:], C[n]).then_inc(S["consts"], 16)
            sp.dma_start(w2[:], I["w_gla_a2"][bass.ds(l, 1)].rearrange("o r n -> (o r) n")).then_inc(S["params"], 16)
            sp.dma_start(bias[:], layer_col(I["b_gla_a"], l)).then_inc(S["params"], 16)
            sp.dma_start(gain[:], layer_row(I["g_head_b"], l)).then_inc(S["params"], 16)
            sp.wait_ge(S["cleared"], 2)
            for h in range(H):
                sp.dma_start(s_state[h * DK_B:(h + 1) * DK_B, :, h * HD:(h + 1) * HD],
                             I["state_gla_s"][bass.ds(l, 1), :, h].rearrange("o r d e -> d (o r) e")).then_inc(S["states"], 16)
            n = 0
            sp.wait_ge(S["state_new"], NCH)
            for h in range(H):
                sp.dma_start(O["p_gla_s"][bass.ds(l, 1), 0, h].rearrange("o d e -> (o d) e"),
                             state[h * DK_B:(h + 1) * DK_B, NCH, h * HD:(h + 1) * HD]).then_inc(S["stored"], 16)
            sp.wait_ge(S["s_state_new"], DEC_BATCH)
            for h in range(H):
                sp.dma_start(O["s_gla_s"][bass.ds(l, 1), :, h].rearrange("o r d e -> d (o r) e"),
                             s_state[h * DK_B:(h + 1) * DK_B, :, h * HD:(h + 1) * HD]).then_inc(S["stored"], 16)
            sp.wait_ge(S["stored"], 16 * 2 * H)

        @block.vector
        def _(dve):
            step = stepper(dve, S["dve_step"])
            dve.memset(state[:, 0, :], 0.0).then_inc(S["cleared"], 1)
            dve.memset(s_state[:], 0.0).then_inc(S["cleared"], 1)
            dve.tensor_copy(low[:], M["gates"][LOWRANK:LOWRANK + RANK, :]).then_inc(S["low_ready"], 1)
            dve.wait_ge(S["params"], 48)
            dve.wait_ge(S["consts"], 16 * 7)
            dve.wait_ge(S["pre_done"], 1)
            for half in range(2):
                dve.tensor_scalar(y[:, half * HALF:(half + 1) * HALF], ps[:, half, 0:HALF], bias[:, 0:1], None,
                                  ALU.add).then_inc(S["y_ready"], 1)
            dve.wait_ge(S["y_ready"], 2)
            dve.wait_ge(S["act_to_dve"], 3)
            step(dve.scalar_tensor_tensor(y[:], y[:], 0.0, sp_[:], ALU.min, ALU.subtract))
            step(dve.tensor_scalar(y[:], y[:], 1.0 / TAU, None, ALU.mult))
            step(dve.tensor_tensor_scan(bsum[:], keep[:], y[:], 0.0, ALU.mult, ALU.add))
            for v, mv, rv, size in ((chunks(bsum)[0], chunks(mid)[0], chunks(rest)[0], CHUNK),
                                    (chunks(bsum)[1], chunks(mid)[1], chunks(rest)[1], DEC_SEQ)):
                shape = [P, v.shape[1], size]
                step(dve.tensor_tensor(mv, v, v[:, :, size // 2 - 1:size // 2].to_broadcast(shape), ALU.subtract))
                step(dve.tensor_tensor(rv, v[:, :, size - 1:size].to_broadcast(shape), v, ALU.subtract))
            step(dve.tensor_copy(whole[:, 0:NCH], bsum[:, CHUNK - 1:SEQ:CHUNK]))
            dve.tensor_copy(whole[:, NCH:], bsum[:, SEQ + DEC_SEQ - 1:NT:DEC_SEQ]).then_inc(S["sums_ready"], 1)
            for n, (dst, x, e) in enumerate(((qi, BQ, y), (qq, BQ, e1), (kk, BK, mid), (kd, BK, rest))):
                dve.wait_ge(S["exps_done"], n + 1)
                dve.tensor_tensor(dst[:], M["TR"][:, x, :], e[:], ALU.mult).then_inc(S["factors_ready"], 1)
            dve.wait_ge(S["factors_ready"], 4)
            dve.wait_ge(S["exps_done"], 5)
            dve.wait_ge(S["states"], 16 * H)

            def spread_query(t):
                r = ROWS[t]
                if t >= 2:
                    dve.wait_ge(S["att_done"], t - 1)
                dve.tensor_tensor(qh[:, t % 2, :, 0:r], qq[:, tok(t)].unsqueeze(1).to_broadcast([P, H, r]),
                                  head[:].unsqueeze(2).to_broadcast([P, H, r]), ALU.mult).then_inc(S["query_ready"], 1)

            spread_query(0)
            for t, r in enumerate(ROWS):
                if t + 1 < TILES:
                    spread_query(t + 1)
                dve.wait_ge(S["att_done"], t + 1)
                if t >= 2:
                    dve.wait_ge(S["out_done"], t - 1)
                mk = (mask if t < PT_TILES else s_mask)[:r, :r]
                dve.tensor_tensor(att[:r, t % 2, :, 0:r], ps[:r, t % 2, 0:H * r].rearrange("p (h t) -> p h t", h=H),
                                  mk.unsqueeze(1).to_broadcast([r, H, r]), ALU.mult).then_inc(S["att_ready"], 1)
                dve.wait_ge(S["keys_turned"], t + 1)
                dve.tensor_copy(kdt[:r, t, :], ps[:r, 2 + t % 2, 0:P]).then_inc(S["keys_ready"], 1)
                if t < PT_TILES:
                    for j in range(2):
                        c = 2 * t + j
                        dve.wait_ge(S["update_done"], c + 1)
                        step(dve.tensor_tensor(upd[:], ps[:, 4 + j, 0:W4], head_cols[:], ALU.mult))
                        dve.scalar_tensor_tensor(state[:, c + 1, :], state[:, c, :], whole[:, c:c + 1], upd[:],
                                                 ALU.mult, ALU.add).then_inc(S["state_new"], 1)
                        dve.wait_ge(S["state_new"], c + 1)
            dve.tensor_tensor(s_qi[:], qi[:, SEQ:NT].unsqueeze(1).to_broadcast([P, DEC_BATCH, NS]), req_tok[:],
                              ALU.mult).then_inc(S["s_query_ready"], 1)
            dve.wait_ge(S["keys_ready"], TILES)
            dve.tensor_tensor(s_kd[:], kdt[:NS, PT_TILES, :].unsqueeze(1).to_broadcast([NS, DEC_BATCH, P]),
                              tok_req[:].unsqueeze(2).to_broadcast([NS, DEC_BATCH, P]), ALU.mult).then_inc(S["s_keys_ready"], 1)
            dve.wait_ge(S["out_done"], TILES)
            for s in range(DEC_BATCH):
                dve.wait_ge(S["s_update_done"], s + 1)
                step(dve.tensor_tensor(upd[:], ps[:, 4 + s % 2, 0:W4], head_cols[:], ALU.mult))
                dve.scalar_tensor_tensor(s_state[:, s, :], s_state[:, s, :], whole[:, NCH + s:NCH + s + 1], upd[:],
                                         ALU.mult, ALU.add).then_inc(S["s_state_new"], 1)
                dve.wait_ge(S["s_state_new"], s + 1)
            dve.wait_ge(S["gate_done"], 2)
            for rs, ts in PARTS:
                nt = ts.stop - ts.start
                step(dve.tensor_tensor(M["BVG"][rs, ts, W4:], M["BVG"][rs, ts, W4:],
                                       gain[rs].unsqueeze(1).to_broadcast([rs.stop, nt, W4]), ALU.mult))
            dve.wait_ge(S["out_copied"], TILES)
            head_vector(dve, S, HB, hB, M["BVG"][:, :, W4:])

        @block.scalar
        def _(act):
            for rs, ts in PARTS:
                act.activation(M["BVG"][rs, ts, W4:], M["BVG"][rs, ts, W4:], ACT.Silu).then_inc(S["gate_done"], 1)
            act.wait_ge(S["y_ready"], 2)
            act.activation(sp_[:], y[:], ACT.Abs).then_inc(S["act_to_dve"], 1)
            act.wait_ge(S["act_to_dve"], 1)
            act.activation(sp_[:], sp_[:], ACT.Exp, scale=-1.0).then_inc(S["act_to_dve"], 1)
            act.wait_ge(S["act_to_dve"], 2)
            act.activation(sp_[:], sp_[:], ACT.Ln, bias=1.0).then_inc(S["act_to_dve"], 1)
            act.wait_ge(S["sums_ready"], 1)
            act.activation(y[:], bsum[:], ACT.Exp).then_inc(S["exps_done"], 1)
            act.activation(e1[:], mid[:], ACT.Exp).then_inc(S["exps_done"], 1)
            act.wait_ge(S["exps_done"], 2)
            act.activation(mid[:], mid[:], ACT.Exp, scale=-1.0).then_inc(S["exps_done"], 1)
            act.activation(rest[:], rest[:], ACT.Exp).then_inc(S["exps_done"], 1)
            act.activation(whole[:], whole[:], ACT.Exp).then_inc(S["exps_done"], 1)
            for t, r in enumerate(ROWS):
                act.wait_ge(S["out_done"], t + 1)
                act.activation(hB[:r, t, :], ps[:r, 6 + t % 2, 0:W4], ACT.Copy).then_inc(S["out_copied"], 1)
            head_scalar_root(act, E, S, HB)
            head_scalar_out(act, E, M, S, 2, 2)

        @block.tensor
        def _(pe):
            pe.wait_ge(S["params"], 48)
            pe.wait_ge(S["low_ready"], 1)
            for half in range(2):
                mm = pe.matmul(ps[:, half, 0:HALF], w2[:], low[:, half * HALF:(half + 1) * HALF], start=True, stop=True)
            mm.then_inc(S["pre_done"], 1)
            pe.wait_ge(S["factors_ready"], 4)

            def inside(t):
                r = ROWS[t]
                if t >= 2:
                    pe.wait_ge(S["att_ready"], t - 1)
                    pe.wait_ge(S["keys_ready"], t - 1)
                pe.wait_ge(S["query_ready"], t + 1)
                rhs = qh[:, t % 2, :, 0:r]
                out = ps[:r, t % 2, 0:H * r].rearrange("p (h t) -> p h t", h=H)
                pe.matmul(out, kk[:, tok(t)], rhs, start=True, stop=True).then_inc(S["att_done"], 1)
                pe.transpose(ps[:r, 2 + t % 2, 0:P], kd[:, tok(t)], E["ident"][:]).then_inc(S["keys_turned"], 1)

            inside(0)
            for t, r in enumerate(ROWS):
                if t + 1 < TILES:
                    inside(t + 1)
                pe.wait_ge(S["keys_ready"], t + 1)
                if t < PT_TILES:
                    for j in range(2):
                        c = 2 * t + j
                        if c >= 2:
                            pe.wait_ge(S["state_new"], c - 1)
                        pe.matmul(ps[:, 4 + j, 0:W4], kdt[j * CHUNK:(j + 1) * CHUNK, t, :],
                                  M["BVG"][j * CHUNK:(j + 1) * CHUNK, t, 0:W4], start=True, stop=True).then_inc(S["update_done"], 1)
                pe.wait_ge(S["att_ready"], t + 1)
                if t >= 2:
                    pe.wait_ge(S["out_copied"], t - 1)
                for h in range(H):
                    pe.matmul(ps[:r, 6 + t % 2, h * HD:(h + 1) * HD], att[:r, t % 2, h, 0:r],
                              M["BVG"][:r, t, h * HD:(h + 1) * HD], start=(h == 0), stop=False, skip_group_check=True)
                if t < PT_TILES:
                    for j in range(2):
                        c = 2 * t + j
                        if c >= 1:
                            pe.wait_ge(S["state_new"], c)
                        else:
                            pe.wait_ge(S["cleared"], 1)
                        mm = pe.matmul(ps[j * CHUNK:(j + 1) * CHUNK, 6 + t % 2, 0:W4], qi[:, c * CHUNK:(c + 1) * CHUNK],
                                       state[:, c, :], start=False, stop=True, skip_group_check=True)
                else:
                    pe.wait_ge(S["s_query_ready"], 1)
                    pe.wait_ge(S["states"], 16 * H)
                    for s in range(DEC_BATCH):
                        mm = pe.matmul(ps[:NS, 6 + t % 2, 0:W4], s_qi[:, s, :], s_state[:, s, :], start=False,
                                       stop=(s == DEC_BATCH - 1), skip_group_check=True)
                mm.then_inc(S["out_done"], 1)
            pe.wait_ge(S["s_keys_ready"], 1)
            pe.wait_ge(S["state_new"], NCH)
            for s in range(DEC_BATCH):
                if s >= 2:
                    pe.wait_ge(S["s_state_new"], s - 1)
                pe.matmul(ps[:, 4 + s % 2, 0:W4], s_kd[:, s, :], M["BVG"][:NS, PT_TILES, 0:W4], start=True,
                          stop=True).then_inc(S["s_update_done"], 1)
            head_tensor(pe, E, S, hB, 2)


def rotary(nc, E, M, l, O, C):
    with stage(nc, "ro", "consts dve_step turned_q turned_k act_out dve_out stored rotated") as (S, sb, block):
        cos = sb("cos", [P, TILES, ROPE_HALF])
        sin = sb("sin", [P, TILES, ROPE_HALF])
        tmp = sb("tmp", [P, 4, TILES, 2 * H, ROPE_HALF])

        @block.sync
        def _(sp):
            sp.dma_start(cos[:], C["cos"]).then_inc(S["consts"], 16)
            sp.dma_start(sin[:], C["sin"]).then_inc(S["consts"], 16)
            sp.wait_ge(S["rotated"], 4)
            sp.dma_start(O["p_win_k"][bass.ds(l, 1)].rearrange("o b (t p) h d -> p (o b t) (h d)", p=P),
                         M["CQK"][:, 0:PT_TILES, W4:]).then_inc(S["stored"], 16)
            sp.dma_start(O["s_win_k"][bass.ds(l, 1)].rearrange("o b t h d -> (o b t) (h d)"),
                         M["CQK"][:NS, PT_TILES, W4:]).then_inc(S["stored"], 16)
            sp.wait_ge(S["stored"], 32)

        @block.vector
        def _(dve):
            step = stepper(dve, S["dve_step"])
            dve.wait_ge(S["consts"], 32)
            for rs, ts in PARTS:
                for t in range(ts.start, ts.stop):
                    v = M["CQK"][rs, t, :].rearrange("p (h d) -> p h d", h=2 * H)
                    shape = [rs.stop, 2 * H, ROPE_HALF]
                    x1, x2 = v[:, :, 0:ROPE_HALF], v[:, :, ROPE_HALF:2 * ROPE_HALF]
                    for k, (x, f) in enumerate(((x1, cos), (x2, sin), (x1, sin), (x2, cos))):
                        ins = dve.tensor_tensor(tmp[rs, k, t], x, f[rs, t, :].unsqueeze(1).to_broadcast(shape), ALU.mult)
                        if k == 3:
                            step(ins)
                        else:
                            ins.then_inc(S["dve_out"], 1)
            dve.wait_ge(S["dve_out"], 3 * TILES)
            for rs, ts in PARTS:
                for a, b, o, op in ((0, 1, 0, ALU.subtract), (2, 3, ROPE_HALF, ALU.add)):
                    v = M["CQK"][rs, ts, :].rearrange("p t (h d) -> p t h d", h=2 * H)[:, :, :, o:o + ROPE_HALF]
                    dve.tensor_tensor(v, tmp[rs, a, ts], tmp[rs, b, ts], op).then_inc(S["rotated"], 1)
            for n in range(2 * TILES):
                t, pair = n // 2, n % 2
                dve.wait_ge(S["turned_k"], n + 1)
                dve.tensor_copy(M["CKT"][:, pair, tok(t)], E["ps"][:, 2 + n % 2, 0:ROWS[t]]).then_inc(S["dve_out"], 1)

        @block.scalar
        def _(act):
            for n in range(2 * TILES):
                t, pair = n // 2, n % 2
                act.wait_ge(S["turned_q"], n + 1)
                act.activation(M["CQT"][:, pair, tok(t)], E["ps"][:, n % 2, 0:ROWS[t]], ACT.Copy,
                               scale=QK_SCALE).then_inc(S["act_out"], 1)

        @block.tensor
        def _(pe):
            pe.wait_ge(S["rotated"], 4)
            for n in range(2 * TILES):
                t, pair = n // 2, n % 2
                r = ROWS[t]
                if n >= 2:
                    pe.wait_ge(S["act_out"], n - 1)
                    pe.wait_ge(S["dve_out"], 3 * TILES + n - 1)
                pe.transpose(E["ps"][:, n % 2, 0:r], M["CQK"][:r, t, pair * P:(pair + 1) * P],
                             E["ident"][:r, :r]).then_inc(S["turned_q"], 1)
                pe.transpose(E["ps"][:, 2 + n % 2, 0:r], M["CQK"][:r, t, W4 + pair * P:W4 + (pair + 1) * P],
                             E["ident"][:r, :r]).then_inc(S["turned_k"], 1)


def prompt_attention(nc, E, M, l, kind, qT, kT, v, chunk, I, C):
    sems = ("consts scores_done z_ready maxima negated sums_done inverse act_step dve_step scanned a_ready "
            "turned pt_act pt_dve out_done out_copied")
    window = kind == "window"
    with stage(nc, "pw" if window else "pd", sems) as (S, sb, block):
        ps = E["ps"]
        mask = sb("mask", [P, SEQ if window else P])
        z = sb("z", [P, H, SEQ])
        f = sb("f", [P, H, SEQ])
        ones = sb("ones", [P, SEQ])
        mx = sb("mx", [P, H])
        total = sb("total", [P, H])
        bias = sb("bias", [P, H])
        pT = sb("pT", [P, 2, SEQ])
        n_in = 1 if window else 2

        @block.sync
        def _(sp):
            sp.dma_start(mask[:], C["win_mask" if window else "strict_mask"]).then_inc(S["consts"], 16)
            if not window:
                sp.dma_start(bias[:], layer_row(I["b_sb"], l)).then_inc(S["consts"], 16)

        @block.tensor
        def _(pe):
            for i in range(PT_TILES):
                w = (i + 1) * P
                if i > 0:
                    pe.wait_ge(S["z_ready"], i)
                for h in range(H):
                    o = (h % 2) * HD
                    mm = pe.matmul(ps[:, h, 0:w], qT[o:o + HD, h // 2, i * P:(i + 1) * P],
                                   kT[o:o + HD, h // 2, 0:w], start=True, stop=True)
                mm.then_inc(S["scores_done"], 1)
                pe.wait_ge(S["a_ready"], i + 1)

                def turn(h):
                    n = H * i + h
                    if n >= 2:
                        pe.wait_ge(S["pt_act"] if h % 2 == 0 else S["pt_dve"], (n - 2) // 2 + 1)
                    for c in range(i + 1):
                        mm = pe.transpose(ps[:, 4 + h % 2, c * P:(c + 1) * P], z[:, h, c * P:(c + 1) * P], E["ident"][:])
                    mm.then_inc(S["turned"], 1)

                turn(0)
                for h in range(H):
                    if h + 1 < H:
                        turn(h + 1)
                    n = H * i + h
                    pe.wait_ge(S["pt_act"] if h % 2 == 0 else S["pt_dve"], n // 2 + 1)
                    if h % 2 == 0 and i > 0:
                        pe.wait_ge(S["out_copied"], 2 * (i - 1) + h // 2 + 1)
                    o = (h % 2) * HD
                    for c in range(i + 1):
                        mm = pe.matmul(ps[o:o + HD, 6 + h // 2, 0:P], v[:, c, h * HD:(h + 1) * HD],
                                       pT[:, h % 2, c * P:(c + 1) * P], start=(c == 0), stop=(c == i))
                    mm.then_inc(S["out_done"], 1)

        @block.vector
        def _(dve):
            step = stepper(dve, S["dve_step"])
            dve.memset(ones[:], 1.0).then_inc(S["inverse"], 1)
            dve.wait_ge(S["consts"], 16 * n_in)
            for i in range(PT_TILES):
                w = (i + 1) * P
                dve.wait_ge(S["scores_done"], i + 1)
                if i > 0:
                    dve.wait_ge(S["turned"], H * i)
                if window:
                    dve.tensor_tensor(z[:, :, 0:w], ps[:, 0:H, 0:w],
                                      mask[:, SEQ - w:SEQ].unsqueeze(1).to_broadcast([P, H, w]), ALU.add).then_inc(S["z_ready"], 1)
                    dve.wait_ge(S["z_ready"], i + 1)
                    step(dve.tensor_reduce(mx[:], z[:, :, 0:w], AX.X, ALU.max))
                    dve.tensor_scalar(mx[:], mx[:], -1.0, None, ALU.mult).then_inc(S["negated"], 1)
                    dve.wait_ge(S["sums_done"], H * (i + 1))
                    step(dve.reciprocal(total[:], total[:]))
                    dve.tensor_tensor(z[:, :, 0:w], z[:, :, 0:w], total[:].unsqueeze(2).to_broadcast([P, H, w]),
                                      ALU.mult).then_inc(S["a_ready"], 1)
                else:
                    dve.tensor_tensor(z[:, :, 0:w], ps[:, 0:H, 0:w], bias[:, 0:H].unsqueeze(2).to_broadcast([P, H, w]),
                                      ALU.add).then_inc(S["z_ready"], 1)
                    dve.wait_ge(S["z_ready"], i + 1)
                    dve.tensor_tensor(z[:, :, w - P:w], z[:, :, w - P:w], mask[:].unsqueeze(1).to_broadcast([P, H, P]),
                                      ALU.add).then_inc(S["maxima"], 1)
                    dve.wait_ge(S["maxima"], i + 1)
                    dve.wait_ge(S["act_step"], 3 * (i + 1))
                    step(dve.scalar_tensor_tensor(f[:, :, 0:w], z[:, :, 0:w], 0.0, f[:, :, 0:w], ALU.max, ALU.add))
                    for h in range(H):
                        step(dve.tensor_tensor_scan(f[:, h, 0:w][:, ::-1], ones[:, 0:w], f[:, h, 0:w][:, ::-1], 0.0,
                                                    ALU.mult, ALU.add))
                    dve.tensor_tensor(z[:, :, 0:w], z[:, :, 0:w], f[:, :, 0:w], ALU.subtract).then_inc(S["scanned"], 1)
                for h in range(1, H, 2):
                    n = H * i + h
                    dve.wait_ge(S["turned"], n + 1)
                    if n >= 2:
                        dve.wait_ge(S["out_done"], n - 1)
                    dve.tensor_copy(pT[:, 1, 0:w], ps[:, 5, 0:w]).then_inc(S["pt_dve"], 1)

        @block.scalar
        def _(act):
            for i in range(PT_TILES):
                w = (i + 1) * P
                if window:
                    act.wait_ge(S["negated"], i + 1)
                    for h in range(H):
                        act.activation(z[:, h, 0:w], z[:, h, 0:w], ACT.Exp, bias=mx[:, h:h + 1],
                                       accum_out=total[:, h:h + 1]).then_inc(S["sums_done"], 1)
                else:
                    act.wait_ge(S["maxima"], i + 1)
                    act.activation(f[:, :, 0:w], z[:, :, 0:w], ACT.Abs).then_inc(S["act_step"], 1)
                    act.wait_ge(S["act_step"], 3 * i + 1)
                    act.activation(f[:, :, 0:w], f[:, :, 0:w], ACT.Exp, scale=-1.0).then_inc(S["act_step"], 1)
                    act.wait_ge(S["act_step"], 3 * i + 2)
                    act.activation(f[:, :, 0:w], f[:, :, 0:w], ACT.Ln, bias=1.0).then_inc(S["act_step"], 1)
                    act.wait_ge(S["scanned"], i + 1)
                    act.activation(z[:, :, 0:w], z[:, :, 0:w], ACT.Exp).then_inc(S["a_ready"], 1)
                for h in range(0, H, 2):
                    n = H * i + h
                    act.wait_ge(S["turned"], n + 1)
                    if n >= 2:
                        act.wait_ge(S["out_done"], n - 1)
                    act.activation(pT[:, 0, 0:w], ps[:, 4, 0:w], ACT.Copy).then_inc(S["pt_act"], 1)
                for pair in range(2):
                    act.wait_ge(S["out_done"], H * i + 2 * pair + 2)
                    act.activation(M["mixT"][:, chunk + pair, i * P:(i + 1) * P], ps[:, 6 + pair, 0:P],
                                   ACT.Copy).then_inc(S["out_copied"], 1)


def sample_attention(nc, E, M, l, kind, qT, kT, v_new, chunk, I, C):
    window = kind == "window"
    NTL = WIN_TILES if window else N_PAGES
    UT = 4
    chunks = [(c, min(UT, NTL - c)) for c in range(0, NTL, UT)]
    NC = len(chunks)
    KEYS = NTL * P
    units = [(k, j) for k in range(NC) for j in range(SG)]
    SLOTS = 4
    name = "sw" if window else "sd"
    cache_k, cache_v = (I["cache_win_k"], I["cache_win_v"]) if window else (I["cache_sb_k"], I["cache_sb_v"])
    sems = ("consts bias_loaded k0 k1 k2 k3 v0 v1 v2 v3 spread q_ready bias_turned bias_ready turned kt_act kt_dve "
            "scores_done z_ready dve_step act_step negated scanned a_ready pt_turned pt_act pt_dve out_units out_done "
            "rows_ready gathered out_copied")
    with nc.Fori(0, GROUPS) as g:
        with stage(nc, name, sems) as (S, sb, block):
            ps = E["ps"]
            ksem, vsem = (S["k0"], S["k1"], S["k2"], S["k3"]), (S["v0"], S["v1"], S["v2"], S["v3"])
            kn = sb("kn", [P, SLOTS, UT, W4])
            vn = sb("vn", [P, SLOTS, UT, W4])
            kt = sb("kt", [P, 2, 2, UT * P])
            z = sb("z", [P, KEYS + NS])
            f = sb("f", [P, KEYS + NS])
            ones = sb("ones", [P, KEYS + NS])
            pT = sb("pT", [P, 2, UT * P])
            new_mask = sb("new_mask", [P, GROUPS, NS])
            head_cols = sb("head_cols", [P, W4])
            gather = sb("gather", [P, SG * DEC_SEQ])
            pair_head = sb("pair_head", [P, 2, H])
            bias_rows = sb("bias_rows", [H, P])
            b = sb("b", [H, 1])
            bcol = sb("bcol", [P, 1])
            qb = sb("qb", [P, 2, SG, H, DEC_SEQ])
            mx = sb("mx", [P, 1])
            total = sb("total", [P, 1])
            rows = sb("rows", [P, W4])
            n_const = (4 if window else 4) + 1

            def load_window(eng, cache, buf, sems_, u):
                k, j = units[u]
                c0, n = chunks[k]
                rows_ = cache[bass.ds(l, 1), bass.ds(SG * g + j, 1)].rearrange("o r n h d -> (o r n) (h d)")
                for i, t in enumerate(range(c0, c0 + n)):
                    if t < FAR_TILES:
                        src = rows_[t * 2 * P:(t + 1) * 2 * P, :].rearrange("(a b) x -> a b x", b=16)[:, 0:8, :]
                    else:
                        r0 = PAST_LEN - NEAR + (t - FAR_TILES) * P
                        src = rows_[r0:r0 + P, :]
                    eng.dma_start(buf[:, u % SLOTS, i, :], src).then_inc(sems_[u % SLOTS], 16)

            def load_pages(eng, cache, buf, sems_, k, j):
                with eng.Fori(0, UT) as i:
                    page = eng.value_load(E["pages"][0:1, bass.ds(SG * N_PAGES * g + j * N_PAGES + UT * k + i, 1)],
                                          min_val=0, max_val=N_POOL - 1)
                    src = cache[bass.ds(l, 1), bass.ds(page, 1)].rearrange("o q n h d -> (o q n) (h d)")
                    eng.dma_start(buf[:, j, bass.ds(i, 1), :].rearrange("p o x -> p (o x)"), src).then_inc(sems_[j], 16)

            def arrived(eng, sems_, u):
                total_ = sum(chunks[units[x][0]][1] for x in range(u % SLOTS, u + 1, SLOTS))
                eng.wait_ge(sems_[u % SLOTS], 16 * total_)

            @block.sync
            def _(sp):
                sp.dma_start(new_mask[:], C["s_win_new" if window else "s_sb_new"]).then_inc(S["consts"], 16)
                sp.dma_start(head_cols[:], C["head_cols"]).then_inc(S["consts"], 16)
                sp.dma_start(gather[:], C["gather_rows"]).then_inc(S["consts"], 16)
                sp.dma_start(pair_head[:], C["pair_head"]).then_inc(S["consts"], 16)
                if window:
                    sp.dma_start(ones[:, 0:KEYS], C["s_win_mask"]).then_inc(S["consts"], 16)
                else:
                    sp.dma_start(bias_rows[:], C["bias_rows"]).then_inc(S["consts"], 16)
                    sp.dma_start(b[:], layer_col(I["b_sb"], l)).then_inc(S["bias_loaded"], 16)
                if window:
                    for u in range(len(units)):
                        if u >= SLOTS:
                            sp.wait_ge(S["turned"], u - SLOTS + 1)
                        load_window(sp, cache_k, kn, ksem, u)
                        if SLOTS <= u < 2 * SLOTS:
                            load_window(sp, cache_v, vn, vsem, u - SLOTS)
                    for u in range(SLOTS, len(units)):
                        sp.wait_ge(S["out_units"], u - SLOTS + 1)
                        load_window(sp, cache_v, vn, vsem, u)
                else:
                    for j in range(SG):
                        load_pages(sp, cache_k, kn, ksem, 0, j)
                    for j in range(SG):
                        load_pages(sp, cache_v, vn, vsem, 0, j)
                    for k in range(1, NC):
                        for j in range(SG):
                            sp.wait_ge(S["turned"], SG * k + j - SLOTS + 1)
                            load_pages(sp, cache_k, kn, ksem, k, j)
                    for k in range(1, NC):
                        for j in range(SG):
                            sp.wait_ge(S["out_units"], SG * k + j - SLOTS + 1)
                            load_pages(sp, cache_v, vn, vsem, k, j)

            @block.tensor
            def _(pe):
                if not window:
                    pe.wait_ge(S["consts"], 16 * n_const)
                    pe.wait_ge(S["bias_loaded"], 16)
                    pe.matmul(ps[:, 6, 0:1], bias_rows[:], b[:], start=True, stop=True).then_inc(S["bias_turned"], 1)

                def turn(u):
                    k, j = units[u]
                    arrived(pe, ksem, u)
                    if u >= 2:
                        pe.wait_ge(S["kt_act"], u - 1)
                        pe.wait_ge(S["kt_dve"], u - 1)
                    for pair in range(2):
                        for i in range(chunks[k][1]):
                            mm = pe.transpose(ps[:, 2 * (u % 2) + pair, i * P:(i + 1) * P],
                                              kn[:, u % SLOTS, i, pair * P:(pair + 1) * P], E["ident"][:])
                    mm.then_inc(S["turned"], 1)

                def scores(u):
                    k, j = units[u]
                    w = chunks[k][1] * P
                    pe.wait_ge(S["kt_act"], u + 1)
                    pe.wait_ge(S["kt_dve"], u + 1)
                    if j == 0 and k >= 2:
                        pe.wait_ge(S["z_ready"], k - 1)
                    for pair in range(2):
                        mm = pe.matmul(ps[32 * j:32 * j + 32, 4 + k % 2, 0:w],
                                       qb[:, pair, j].rearrange("p h q -> p (h q)"), kt[:, u % 2, pair, 0:w],
                                       start=(pair == 0), stop=(pair == 1), tile_position=(0, 32 * j))
                    mm.then_inc(S["scores_done"], 1)

                turn(0)
                pe.wait_ge(S["q_ready"], 2)
                for u in range(len(units)):
                    if u + 1 < len(units):
                        turn(u + 1)
                    scores(u)
                pe.wait_ge(S["z_ready"], NC - 1 if NC >= 2 else 1)
                for j in range(SG):
                    for pair in range(2):
                        mm = pe.matmul(ps[32 * j:32 * j + 32, 4 + NC % 2, 0:NS],
                                       qb[:, pair, j].rearrange("p h q -> p (h q)"), kT[:, pair, SEQ:NT],
                                       start=(pair == 0), stop=(pair == 1), tile_position=(0, 32 * j))
                mm.then_inc(S["scores_done"], 1)
                pe.wait_ge(S["a_ready"], 1)

                def turn_p(k):
                    c0, n = chunks[k] if k < NC else (NTL, 1)
                    if k >= 2:
                        pe.wait_ge(S["pt_act"] if k % 2 == 0 else S["pt_dve"], (k - 2) // 2 + 1)
                    for i in range(n):
                        cs = slice((c0 + i) * P, (c0 + i) * P + (P if k < NC else NS))
                        mm = pe.transpose(ps[:cs.stop - cs.start, k % 2, i * P:(i + 1) * P], z[:, cs], E["ident"][:])
                    mm.then_inc(S["pt_turned"], 1)

                turn_p(0)
                for k in range(NC):
                    turn_p(k + 1)
                    pe.wait_ge(S["pt_act"] if k % 2 == 0 else S["pt_dve"], k // 2 + 1)
                    for j in range(SG):
                        u = SG * k + j
                        arrived(pe, vsem, u)
                        for i in range(chunks[k][1]):
                            mm = pe.matmul(ps[32 * j:32 * j + 32, 6, 0:W4],
                                           pT[:, k % 2, i * P + 32 * j:i * P + 32 * j + 32], vn[:, u % SLOTS, i, :],
                                           start=(k == 0 and i == 0), stop=False, skip_group_check=True,
                                           tile_position=(0, 32 * j))
                        mm.then_inc(S["out_units"], 1)
                pe.wait_ge(S["pt_act"] if NC % 2 == 0 else S["pt_dve"], NC // 2 + 1)
                pe.matmul(ps[:, 6, 0:W4], pT[:NS, NC % 2, 0:P], v_new, start=False, stop=True,
                          skip_group_check=True).then_inc(S["out_done"], 1)
                pe.wait_ge(S["rows_ready"], 1)
                for pair in range(2):
                    mm = pe.matmul(ps[:, 7, pair * 32:pair * 32 + 32], rows[:, pair * P:(pair + 1) * P], gather[:],
                                   start=True, stop=True)
                mm.then_inc(S["gathered"], 1)

            @block.scalar
            def _(act):
                for u, (k, j) in enumerate(units):
                    w = chunks[k][1] * P
                    act.wait_ge(S["turned"], u + 1)
                    if u >= 2:
                        act.wait_ge(S["scores_done"], u - 1)
                    act.activation(kt[:, u % 2, 0, 0:w], ps[:, 2 * (u % 2), 0:w], ACT.Copy).then_inc(S["kt_act"], 1)
                if window:
                    act.wait_ge(S["negated"], 1)
                    act.activation(z[:], z[:], ACT.Exp, bias=mx[:, 0:1], accum_out=total[:]).then_inc(S["a_ready"], 1)
                else:
                    act.wait_ge(S["z_ready"], NC + 1)
                    act.activation(f[:], z[:], ACT.Abs).then_inc(S["act_step"], 1)
                    act.wait_ge(S["act_step"], 1)
                    act.activation(f[:], f[:], ACT.Exp, scale=-1.0).then_inc(S["act_step"], 1)
                    act.wait_ge(S["act_step"], 2)
                    act.activation(f[:], f[:], ACT.Ln, bias=1.0).then_inc(S["act_step"], 1)
                    act.wait_ge(S["scanned"], 1)
                    act.activation(z[:], z[:], ACT.Exp).then_inc(S["a_ready"], 1)
                for k in range(0, NC + 1, 2):
                    w, r = (chunks[k][1] * P, P) if k < NC else (P, NS)
                    act.wait_ge(S["pt_turned"], k + 1)
                    if k >= 2:
                        act.wait_ge(S["out_units"], SG * (k - 1))
                    act.activation(pT[:r, 0, 0:w], ps[:r, 0, 0:w], ACT.Copy).then_inc(S["pt_act"], 1)
                act.wait_ge(S["gathered"], 1)
                act.activation(M["mixT"][:, chunk:chunk + 2, bass.ds(SEQ + 32 * g, 32)],
                               ps[:, 7, 0:64].rearrange("p (k t) -> p k t", k=2), ACT.Copy).then_inc(S["out_copied"], 1)

            @block.vector
            def _(dve):
                step = stepper(dve, S["dve_step"])
                dve.wait_ge(S["consts"], 16 * n_const)
                for pair in range(2):
                    qv = qT[:, pair, bass.ds(SEQ + 32 * g, 32)].rearrange("p (s q) -> p s q", q=DEC_SEQ)
                    for h in range(H):
                        ins = dve.tensor_scalar(qb[:, pair, :, h, :], qv, pair_head[:, pair, h:h + 1], None, ALU.mult)
                        if h == H - 1:
                            ins.then_inc(S["q_ready"], 1)
                        else:
                            ins.then_inc(S["spread"], 1)
                dve.wait_ge(S["spread"], 2 * (H - 1))
                dve.wait_ge(S["q_ready"], 2)
                if not window:
                    step(dve.memset(ones[:], 1.0))
                    dve.wait_ge(S["bias_turned"], 1)
                    dve.tensor_copy(bcol[:], ps[:, 6, 0:1]).then_inc(S["bias_ready"], 1)
                    dve.wait_ge(S["bias_ready"], 1)

                def take(k):
                    dve.wait_ge(S["scores_done"], SG * (k + 1) if k < NC else SG * NC + 1)
                    if k == NC:
                        src = ps[:, 4 + NC % 2, 0:NS]
                        mk = new_mask[:, bass.ds(g, 1), :].rearrange("p o n -> p (o n)")
                        if window:
                            ins = dve.tensor_tensor(z[:, KEYS:], src, mk, ALU.add)
                        else:
                            ins = dve.scalar_tensor_tensor(z[:, KEYS:], src, bcol[:, 0:1], mk, ALU.add, ALU.add)
                    else:
                        cs = slice(chunks[k][0] * P, (chunks[k][0] + chunks[k][1]) * P)
                        src = ps[:, 4 + k % 2, 0:cs.stop - cs.start]
                        if window:
                            ins = dve.tensor_tensor(z[:, cs], src, ones[:, cs], ALU.add)
                        else:
                            ins = dve.tensor_scalar(z[:, cs], src, bcol[:, 0:1], None, ALU.add)
                    ins.then_inc(S["z_ready"], 1)

                for u, (k, j) in enumerate(units):
                    w = chunks[k][1] * P
                    dve.wait_ge(S["turned"], u + 1)
                    if u >= 2:
                        dve.wait_ge(S["scores_done"], u - 1)
                    dve.tensor_copy(kt[:, u % 2, 1, 0:w], ps[:, 2 * (u % 2) + 1, 0:w]).then_inc(S["kt_dve"], 1)
                    if j == 1 and k >= 1:
                        take(k - 1)
                take(NC - 1)
                take(NC)
                dve.wait_ge(S["z_ready"], NC + 1)
                if window:
                    step(dve.tensor_reduce(mx[:], z[:], AX.X, ALU.max))
                    dve.tensor_scalar(mx[:], mx[:], -1.0, None, ALU.mult).then_inc(S["negated"], 1)
                else:
                    dve.wait_ge(S["act_step"], 3)
                    step(dve.scalar_tensor_tensor(f[:], z[:], 0.0, f[:], ALU.max, ALU.add))
                    step(dve.tensor_tensor_scan(f[:, ::-1], ones[:], f[:, ::-1], 0.0, ALU.mult, ALU.add))
                    dve.tensor_tensor(z[:], z[:], f[:], ALU.subtract).then_inc(S["scanned"], 1)
                for k in range(1, NC + 1, 2):
                    w, r = (chunks[k][1] * P, P) if k < NC else (P, NS)
                    dve.wait_ge(S["pt_turned"], k + 1)
                    if k >= 2:
                        dve.wait_ge(S["out_units"], SG * (k - 1))
                    dve.tensor_copy(pT[:r, 1, 0:w], ps[:r, 1, 0:w]).then_inc(S["pt_dve"], 1)
                dve.wait_ge(S["out_done"], 1)
                if window:
                    dve.wait_ge(S["a_ready"], 1)
                    step(dve.reciprocal(total[:], total[:]))
                    dve.scalar_tensor_tensor(rows[:], ps[:, 6, 0:W4], total[:, 0:1], head_cols[:], ALU.mult,
                                             ALU.mult).then_inc(S["rows_ready"], 1)
                else:
                    dve.tensor_tensor(rows[:], ps[:, 6, 0:W4], head_cols[:], ALU.mult).then_inc(S["rows_ready"], 1)


def output(nc, E, M, l, I):
    with stage(nc, "ou", POST_SEMS) as (S, sb, block):
        B = post_buffers(sb)

        @block.sync
        def _(sp):
            sp.dma_start(B["gain"][:], layer_row(I["g_mix_post"], l)).then_inc(S["post_gain_loaded"], 16)
            post_sync(sp, S, B, I["w_out"], l, KC)

        @block.tensor
        def _(pe):
            post_tensor(pe, E, S, B, M["mixT"], KC)

        @block.scalar
        def _(act):
            post_scalar(act, E, S, B, KC, 1.0)

        @block.vector
        def _(dve):
            post_vector(dve, E, S, B, KC)


def mixing(nc, E, l, I, O, C):
    with ExitStack() as ctx:
        def sb(n, shape, dt=F32):
            return ctx.enter_context(nc.sbuf_tensor(n, shape, dt))

        M = dict(
            TR=sb("TR", [P, 10, NT]), gates=sb("gates", [GATE_ROWS, NT]),
            KA=sb("KA", [P, TILES, W4]), VA=sb("VA", [P, TILES, H, HD + 1]), AO=sb("AO", [P, TILES, W4]),
            CV=sb("CV", [P, TILES, W4]), BVG=sb("BVG", [P, TILES, 2 * W4]), CQK=sb("CQK", [P, TILES, 2 * W4]),
            DKV=sb("DKV", [P, TILES, 2 * W4]), mixT=E["hT"])
        M["CQT"], M["CKT"] = M["TR"][:, AQ:AQ + 2, :], M["TR"][:, AK:AK + 2, :]
        project(nc, E, M, l, I["g_mix_pre"], I["w_in"], O)
        mlstm(nc, E, M, l, I, O, C)
        gla(nc, E, M, l, I, O, C)
        rotary(nc, E, M, l, O, C)
        DQT, DKT = M["TR"][:, DQ:DQ + 2, :], M["TR"][:, DK:DK + 2, :]
        prompt_attention(nc, E, M, l, "window", M["CQT"], M["CKT"], M["CV"], 4, I, C)
        prompt_attention(nc, E, M, l, "stick", DQT, DKT, M["DKV"][:, :, W4:], 6, I, C)
        sample_attention(nc, E, M, l, "window", M["CQT"], M["CKT"], M["CV"][:NS, PT_TILES, :], 4, I, C)
        sample_attention(nc, E, M, l, "stick", DQT, DKT, M["DKV"][:NS, PT_TILES, W4:], 6, I, C)
        output(nc, E, M, l, I)


def program(nc, I, O, C):
    with ExitStack() as ctx:
        def sb(n, shape, dt=F32):
            return ctx.enter_context(nc.sbuf_tensor(n, shape, dt))

        E = dict(
            x=sb("x", [P, TILES, D_MODEL]),
            hT=sb("hT", [P, KC, NT]),
            ident=sb("ident", [P, P]), sumsq=sb("sumsq", [P, TILES]), eps=sb("eps", [P, 2]),
            pages=sb("pages", [1, DEC_BATCH * N_PAGES], I32),
            ps=ctx.enter_context(nc.psum_tensor("ps", [P, 8, 512], F32)))

        with stage(nc, "start", "loaded") as (S, _sb, block):
            @block.sync
            def _(sp):
                sp.dma_start(E["x"][:, 0:PT_TILES, :], I["x_prompt"].rearrange("b (t p) n -> p (b t) n", p=P)).then_inc(S["loaded"], 16)
                sp.dma_start(E["x"][:NS, PT_TILES, :], I["x_sample"].rearrange("b t n -> (b t) n")).then_inc(S["loaded"], 16)
                sp.dma_start(E["ident"][:], C["ident"]).then_inc(S["loaded"], 16)
                sp.dma_start(E["pages"][:], I["page_table"].rearrange("(o b) n -> o (b n)", o=1)).then_inc(S["loaded"], 16)
                sp.wait_ge(S["loaded"], 64)

            @block.vector
            def _(dve):
                dve.memset(E["sumsq"][:], 0.0)
                dve.memset(E["eps"][:, 0:1], EPS)
                dve.memset(E["eps"][:, 1:2], 4 * EPS)

        with nc.Fori(0, DEPTH) as l:
            ffn(nc, E, l, "f1", I["g_ffn1_pre"], I["w_ffn1_in"], I["w_ffn1_out"], I["g_ffn1_post"])
            mixing(nc, E, l, I, O, C)
            ffn(nc, E, l, "f2", I["g_ffn2_pre"], I["w_ffn2_in"], I["w_ffn2_out"], I["g_ffn2_post"])

        with stage(nc, "end", "stored") as (S, _sb, block):
            @block.sync
            def _(sp):
                sp.dma_start(O["y_prompt"].rearrange("b (t p) n -> p (b t) n", p=P), E["x"][:, 0:PT_TILES, :]).then_inc(S["stored"], 16)
                sp.dma_start(O["y_sample"].rearrange("b t n -> (b t) n"), E["x"][:NS, PT_TILES, :]).then_inc(S["stored"], 16)
                sp.wait_ge(S["stored"], 32)


INPUTS = ("x_prompt", "x_sample", "cache_sb_k", "cache_sb_v", "page_table", "cache_win_k", "cache_win_v",
          "state_mlstm_c", "state_mlstm_n", "state_mlstm_m", "state_gla_s",
          "g_ffn1_pre", "w_ffn1_in", "w_ffn1_out", "g_ffn1_post", "g_mix_pre", "w_in", "b_ig", "b_fg",
          "g_head_a", "w_gla_a2", "b_gla_a", "g_head_b", "b_sb", "w_out", "g_mix_post",
          "g_ffn2_pre", "w_ffn2_in", "w_ffn2_out", "g_ffn2_post")
OUTPUTS = {
    "y_prompt": (1, SEQ, D_MODEL), "y_sample": (DEC_BATCH, DEC_SEQ, D_MODEL),
    "p_sb_k": (DEPTH, 1, SEQ, H, HD), "p_sb_v": (DEPTH, 1, SEQ, H, HD),
    "p_win_k": (DEPTH, 1, SEQ, H, HD), "p_win_v": (DEPTH, 1, SEQ, H, HD),
    "p_mlstm_c": (DEPTH, 1, H, HD, HD), "p_mlstm_n": (DEPTH, 1, H, HD), "p_mlstm_m": (DEPTH, 1, H),
    "p_gla_s": (DEPTH, 1, H, DK_B, HD),
    "s_sb_k": (DEPTH, DEC_BATCH, DEC_SEQ, H, HD), "s_sb_v": (DEPTH, DEC_BATCH, DEC_SEQ, H, HD),
    "s_win_k": (DEPTH, DEC_BATCH, DEC_SEQ, H, HD), "s_win_v": (DEPTH, DEC_BATCH, DEC_SEQ, H, HD),
    "s_mlstm_c": (DEPTH, DEC_BATCH, H, HD, HD), "s_mlstm_n": (DEPTH, DEC_BATCH, H, HD),
    "s_mlstm_m": (DEPTH, DEC_BATCH, H), "s_gla_s": (DEPTH, DEC_BATCH, H, DK_B, HD),
}


def kernel(**inputs):
    import concourse.bacc as _bacc
    from concourse.bass_utils import run_bass_kernel_spmd as _run

    nc = _bacc.Bacc("TRN2", target_bir_lowering=False, num_devices=1)
    arrays, I, O, C = {}, {}, {}, {}
    for name in INPUTS:
        a = np.ascontiguousarray(inputs[name])
        arrays[f"in_{name}"] = a
        I[name] = nc.dram_tensor(f"in_{name}", a.shape, mybir.dt.from_np(a.dtype), kind="ExternalInput").ap()
    for name, a in constants().items():
        arrays[f"const_{name}"] = a
        C[name] = nc.dram_tensor(f"const_{name}", a.shape, F32, kind="ExternalInput").ap()
    for name, shape in OUTPUTS.items():
        O[name] = nc.dram_tensor(f"out_{name}", shape, F32, kind="ExternalOutput").ap()
    program(nc, I, O, C)
    r = _run(nc, [arrays], core_ids=[0])
    return tuple(r.results[0][f"out_{name}"] for name in OUTPUTS)
```

```python
from contextlib import ExitStack, contextmanager

import numpy as np
import concourse.bass as bass
from concourse import mybir

ALU = mybir.AluOpType
ACT = mybir.ActivationFunctionType
AX = mybir.AxisListType
F32 = mybir.dt.float32
I32 = mybir.dt.int32
F32R = mybir.dt.float32r

D_MODEL = 1024
SEQ = 512
DEPTH = 2
DEC_BATCH = 8
DEC_SEQ = 8
PAST_LEN = 2048
PAGE = 128
N_PAGES = PAST_LEN // PAGE
N_POOL = DEC_BATCH * N_PAGES * 5 // 4
HD = 64
H = 4
DK_B = HD // 2
RANK = 16
TAU = 16.0
CHUNK = 64
D_FF = 2 * D_MODEL
EPS = 1e-6
ROPE_HALF = HD // 8
THETA = 500000.0
DILATIONS = ((128, 1), (512, 4), (2048, 16))
NEG = -1e30

P = 128
KC = D_MODEL // P
W4 = H * HD
NS = DEC_BATCH * DEC_SEQ
NT = SEQ + NS
PT_TILES = SEQ // P
TILES = PT_TILES + 1
ROWS = [P] * PT_TILES + [NS]
HALF = NT // 2
FF = D_FF // P

SIZES = (W4, W4, W4, H, H, W4, H * DK_B, H * DK_B, W4, W4, RANK, W4, W4, W4, W4, W4, W4)
NAMES = ("aq", "ak", "av", "ai", "af", "ao", "bq", "bk", "bv", "bg", "blr", "cq", "ck", "cv", "dq", "dk", "dv")
COL = {n: sum(SIZES[:i]) for i, n in enumerate(NAMES)}
N_IN = sum(SIZES)

NEAR = DILATIONS[1][0]
FAR_TILES = (PAST_LEN - NEAR) // (2 * P)
WIN_TILES = FAR_TILES + NEAR // P
SG = 4
GROUPS = DEC_BATCH // SG


def tok(t):
    return slice(t * P, t * P + ROWS[t])


PARTS = ((slice(0, P), slice(0, PT_TILES)), (slice(0, NS), slice(PT_TILES, TILES)))


def constants():
    f = np.float32
    c = {}
    c["ident"] = np.eye(P, dtype=f)
    p = np.arange(P)
    u = np.arange(SEQ)

    def log_count(delta):
        n = sum(((delta >= 0) & (delta <= w) & (delta % d == 0)).astype(np.int64) for w, d in DILATIONS)
        return np.where(n > 0, np.log(np.maximum(n, 1)), NEG).astype(f)

    c["win_mask"] = log_count(p[:, None] + (SEQ - P) - u[None, :])
    c["strict_mask"] = np.where(p[:, None] > p[None, :], 0, NEG).astype(f)
    c["turned_mask"] = np.where(p[None, :] >= p[:, None], 0, NEG).astype(f)
    c["gla_mask"] = ((p[None, :] >= p[:, None]) & (p[None, :] // CHUNK == p[:, None] // CHUNK)).astype(f)
    s = np.arange(NS)
    same = s[:, None] // DEC_SEQ == s[None, :] // DEC_SEQ
    ok = same & (s[None, :] >= s[:, None])
    c["s_turned_mask"] = np.where(ok, 0, NEG).astype(f)
    c["s_gla_mask"] = ok.astype(f)
    rs, rh, rq = p // (H * DEC_SEQ), p // DEC_SEQ % H, p % DEC_SEQ
    row = np.zeros((P, WIN_TILES * P), f)
    for t in range(WIN_TILES):
        if t < FAR_TILES:
            pos = t * 2 * P + (np.arange(P) // 8) * 16 + np.arange(P) % 8
        else:
            pos = PAST_LEN - NEAR + (t - FAR_TILES) * P + np.arange(P)
        row[:, t * P:(t + 1) * P] = log_count(PAST_LEN + rq[:, None] - pos[None, :])
    c["s_win_mask"] = row
    g = np.arange(GROUPS)
    mine = (g[:, None, None] * SG + rs[None, :, None]) == (s // DEC_SEQ)[None, None, :]
    delta = (rq[:, None] - (s % DEC_SEQ)[None, :])[None]
    c["s_win_new"] = np.where(mine, log_count(delta), NEG).astype(f).transpose(1, 0, 2).copy()
    c["s_sb_new"] = np.where(mine & (delta > 0), 0, NEG).astype(f).transpose(1, 0, 2).copy()
    c["head_cols"] = np.repeat((rh[:, None] == np.arange(H)[None, :]), HD, axis=1).astype(f)
    c["gather_rows"] = ((rs * DEC_SEQ + rq)[:, None] == np.arange(SG * DEC_SEQ)[None, :]).astype(f)
    c["pair_head"] = np.stack([(np.arange(H)[None, :] == 2 * pr + (p // HD)[:, None]) for pr in range(2)],
                              1).astype(f)
    c["bias_rows"] = (np.arange(H)[:, None] == rh[None, :]).astype(f)
    c["head_rows"] = np.repeat(np.eye(H, dtype=f)[:, :, None], P, axis=2)
    first = (np.arange(NT) >= SEQ) & ((np.arange(NT) - SEQ) % DEC_SEQ == 0)
    c["keep_a"] = np.repeat(np.where(first, 0, 1)[None], H, 0).astype(f)
    c["cut_a"] = np.repeat(np.where(first, NEG, 0)[None], H, 0).astype(f)
    start = first | ((np.arange(NT) < SEQ) & (np.arange(NT) % CHUNK == 0))
    c["keep_b"] = np.repeat(np.where(start, 0, 1)[None], P, 0).astype(f)
    q = np.arange(DEC_BATCH // 2)
    req = 2 * q[None, :] + (p // HD)[:, None]
    c["pair_tokens"] = (req[:, :, None] == (s // DEC_SEQ)[None, None, :]).astype(f)
    c["pair_last"] = ((req.T[None] * DEC_SEQ + DEC_SEQ - 1) == s[:, None, None]).astype(f)
    c["token_request"] = ((s // DEC_SEQ)[:, None] == np.arange(DEC_BATCH)[None, :]).astype(f)
    c["request_tokens"] = np.repeat(c["token_request"].T[None], P, 0).copy()
    c["gla_head"] = ((p // DK_B)[:, None] == np.arange(H)[None, :]).astype(f)
    c["gla_cols"] = np.repeat(c["gla_head"], HD, axis=1)
    inv = np.float32(THETA) ** (-np.arange(ROPE_HALF, dtype=f) / np.float32(ROPE_HALF))
    pos = np.concatenate([np.arange(SEQ), PAST_LEN + np.arange(NS) % DEC_SEQ, np.zeros(P - NS)]).astype(f)
    ang = (pos[:, None] * inv[None, :].astype(f)).astype(f)
    for name, fn in (("cos", np.cos), ("sin", np.sin)):
        c[name] = fn(ang).astype(f).reshape(TILES, P, ROPE_HALF).transpose(1, 0, 2).copy()
    return c


RESIDENT = ("ident",)


@contextmanager
def stage(nc, name, sems):
    with ExitStack() as st:
        S = dict(**{s: st.enter_context(nc.semaphore(f"{name}_{s}")) for s in sems.split()})
        st2 = ExitStack()

        def sb(n, shape, dt=F32):
            return st.enter_context(nc.sbuf_tensor(f"{name}_{n}", shape, dt))

        with st2:
            block = st2.enter_context(nc.Block())
            yield S, sb, block
        nums = sorted(s.num for s in S.values())
        while nums:
            run = 1
            while run < len(nums) and nums[run] == nums[0] + run:
                run += 1
            nc.all_engine_barrier(sems_to_clear=range(nums[0], nums[0] + run))
            nums = nums[run:]


def stepper(eng, sem):
    n = [0]

    def step(ins):
        n[0] += 1
        ins.then_inc(sem, 1)
        eng.wait_ge(sem, n[0])
    return step


def layer_row(w, l):
    return w[bass.ds(l, 1), :].rearrange("o n -> (o n)").partition_broadcast(P)


def layer_col(w, l):
    return w[bass.ds(l, 1), :].rearrange("o n -> n o")


SLOT = 2048


def split_products(pe, out, stat_hi, stat_lo, mov_hi, mov_lo, start, stop):
    pe.matmul(out, stat_hi, mov_hi, start=start, stop=False, skip_group_check=True)
    pe.matmul(out, stat_hi, mov_lo, start=False, stop=False, skip_group_check=True)
    return pe.matmul(out, stat_lo, mov_hi, start=False, stop=stop, skip_group_check=True)


WEIGHT_SEMS = "raw_loaded0 raw_loaded1 w_hi w_lo chunk_done "


def weight_buffers(sb, raw=None):
    return dict(raw=raw if raw is not None else sb("w_raw", [P, 2, SLOT]),
                hi=sb("w_hi", [P, 2, SLOT], F32R), lo=sb("w_lo", [P, 2, SLOT], F32R))


def raw_sem(S, slot):
    return (S["raw_loaded0"], S["raw_loaded1"])[slot]


def weight_room(sp, S, n):
    sp.wait_ge(S["w_lo"], n - 1)


def split_scalar(act, S, W, slot, n, turn, reused):
    act.wait_ge(raw_sem(S, slot), 32 * turn + 32)
    if reused:
        act.wait_ge(S["chunk_done"], n - 1)
    act.activation(W["hi"][:, slot], W["raw"][:, slot], ACT.Copy).then_inc(S["w_hi"], 1)


def split_vector(dve, S, W, slot, n):
    dve.wait_ge(S["w_hi"], n + 1)
    dve.tensor_tensor(W["lo"][:, slot], W["raw"][:, slot], W["hi"][:, slot].bitcast(F32),
                      ALU.subtract).then_inc(S["w_lo"], 1)


PRE_SEMS = "pre_gain_loaded squares_done rms_done inv_done normed turned h_hi h_lo "


def pre_buffers(sb, work):
    return dict(scratch=work[:, 2 * D_MODEL:3 * D_MODEL], gain=sb("gain", [P, D_MODEL]),
                rms=sb("pre_rms", [P, TILES]), inv=sb("pre_inv", [P, TILES]),
                normed=work[:, 0:2 * D_MODEL].rearrange("p (s n) -> p s n", s=2),
                hi=sb("h_hi", [P, KC, NT], F32R), lo=sb("h_lo", [P, KC, NT], F32R))


def pre_view(x, t, half):
    return x[:, 4 * half:4 * half + 4, tok(t)]


def pre_bank(E, t, half):
    return E["ps"][:, 2 * (t % 2) + half, 0:4 * ROWS[t]].rearrange("p (c r) -> p c r", c=4)


def pre_scalar(act, E, S, B):
    for t, r in enumerate(ROWS):
        if t > 0:
            act.wait_ge(S["squares_done"], t)
        act.activation(B["scratch"][:r, :], E["x"][:r, t, :], ACT.Square,
                       accum_out=E["sumsq"][:r, t:t + 1]).then_inc(S["squares_done"], 1)
    act.wait_ge(S["squares_done"], TILES)
    act.activation(B["rms"][:, :], E["sumsq"][:, :], ACT.Sqrt, bias=E["eps"][:, 0:1],
                   scale=1.0 / D_MODEL).then_inc(S["rms_done"], 1)
    for t in range(TILES):
        for half in range(2):
            act.wait_ge(S["turned"], 2 * t + half + 1)
            act.activation(pre_view(B["hi"], t, half), pre_bank(E, t, half), ACT.Copy).then_inc(S["h_hi"], 1)


def pre_vector(dve, E, S, B):
    dve.wait_ge(S["rms_done"], 1)
    dve.reciprocal(B["inv"][:, :], B["rms"][:, :]).then_inc(S["inv_done"], 1)
    dve.wait_ge(S["inv_done"], 1)
    dve.wait_ge(S["pre_gain_loaded"], 16)
    for t in range(TILES + 1):
        if t < TILES:
            r = ROWS[t]
            if t == TILES - 1:
                dve.wait_ge(S["squares_done"], TILES)
            dve.scalar_tensor_tensor(B["normed"][:r, t % 2, :], E["x"][:r, t, :], B["inv"][:r, t:t + 1],
                                     B["gain"][:r, :], ALU.mult, ALU.mult).then_inc(S["normed"], 1)
        if t > 0:
            for half in range(2):
                dve.wait_ge(S["h_hi"], 2 * (t - 1) + half + 1)
                dve.tensor_tensor(pre_view(B["lo"], t - 1, half), pre_bank(E, t - 1, half),
                                  pre_view(B["hi"], t - 1, half).bitcast(F32), ALU.subtract).then_inc(S["h_lo"], 1)


def pre_tensor(pe, E, S, B):
    for t, r in enumerate(ROWS):
        pe.wait_ge(S["normed"], t + 1)
        for half in range(2):
            if t >= 2:
                pe.wait_ge(S["h_lo"], 2 * (t - 2) + half + 1)
            for c in range(4):
                mm = pe.transpose(E["ps"][:, 2 * (t % 2) + half, c * r:(c + 1) * r],
                                  B["normed"][:r, t % 2, (4 * half + c) * P:(4 * half + c + 1) * P],
                                  E["ident"][:r, :r])
            mm.then_inc(S["turned"], 1)
    pe.wait_ge(S["h_lo"], 2 * TILES)


POST_SEMS = "post_gain_loaded half_done y_act y_dve y_squares y_rms y_inv scaled added "


def post_chunks(nk):
    return [(h, k) for h in range(2) for k in range(0, nk, 4)]


def post_sync(sp, S, W, w, l, nk, base):
    wv = w[bass.ds(l, 1)].rearrange("o (k p) n -> p (o k) n", p=P)
    for q, (h, k) in enumerate(post_chunks(nk)):
        n = base + q
        if n >= 2:
            weight_room(sp, S, n)
        dst = W["raw"][:, n % 2].rearrange("p (k n) -> p k n", k=4)
        for i in range(0, 4, 2):
            sp.dma_start(dst[:, i:i + 2], wv[:, k + i:k + i + 2, h * 512:(h + 1) * 512]).then_inc(
                raw_sem(S, n % 2), 16)


def post_tensor(pe, E, S, W, a_hi, a_lo, nk, base):
    for q, (h, k) in enumerate(post_chunks(nk)):
        n = base + q
        pe.wait_ge(S["w_lo"], n + 1)
        hi, lo = (W[x][:, n % 2].rearrange("p (k n) -> p k n", k=4) for x in ("hi", "lo"))
        for kk in range(4):
            for t, r in enumerate(ROWS):
                if h == 1 and k + kk == 0:
                    pe.wait_ge(S["y_act"] if t % 2 == 0 else S["y_dve"], t // 2 + 1)
                mm = split_products(pe, E["ps"][:r, t, 0:512], a_hi[:, k + kk, tok(t)], a_lo[:, k + kk, tok(t)],
                                    hi[:, kk], lo[:, kk], k + kk == 0, k + kk == nk - 1)
                if k + kk == nk - 1 and t < TILES - 1:
                    mm.then_inc(S["half_done"], 1)
        mm.then_inc(S["chunk_done"], 1)


def post_split_scalar(act, S, W, nk, base, h):
    total = base + len(post_chunks(nk))
    per = nk // 4
    for q in range(h * per, (h + 1) * per):
        n = base + q + 2
        if n < total:
            split_scalar(act, S, W, n % 2, n, n // 2, True)


def post_split_vector(dve, S, W, nk, base, h):
    total = base + len(post_chunks(nk))
    per = nk // 4
    for q in range(h * per, (h + 1) * per):
        n = base + q + 2
        if n < total:
            split_vector(dve, S, W, n % 2, n)


def post_wait(eng, S, h, t, nk, base):
    if t < TILES - 1:
        eng.wait_ge(S["half_done"], (TILES - 1) * h + t + 1)
    else:
        eng.wait_ge(S["chunk_done"], base + (h + 1) * nk // 4)


def post_scalar(act, E, S, W, y, scratch, rms, nk, base, weight):
    for h in range(2):
        post_split_scalar(act, S, W, nk, base, h)
        for t in range(0, TILES, 2):
            post_wait(act, S, h, t, nk, base)
            act.activation(y[:ROWS[t], h, t * 512:(t + 1) * 512], E["ps"][:ROWS[t], t, 0:512],
                           ACT.Copy).then_inc(S["y_act"], 1)
    act.wait_ge(S["y_act"], 2 * 3)
    act.wait_ge(S["y_dve"], 2 * 2)
    for t, r in enumerate(ROWS):
        if t > 0:
            act.wait_ge(S["y_squares"], t)
        act.activation(scratch[:r].rearrange("p (h n) -> p h n", h=2), y[:r, :, t * 512:(t + 1) * 512], ACT.Square,
                       accum_out=E["sumsq"][:r, t:t + 1]).then_inc(S["y_squares"], 1)
    act.wait_ge(S["y_squares"], TILES)
    act.activation(rms[:, :], E["sumsq"][:, :], ACT.Sqrt, bias=E["eps"][:, 1:2] if weight == 0.5 else E["eps"][:, 0:1],
                   scale=1.0 / D_MODEL / weight ** 2).then_inc(S["y_rms"], 1)


def post_vector(dve, E, S, W, y, gain, rms, inv, nk, base):
    for h in range(2):
        post_split_vector(dve, S, W, nk, base, h)
        for t in range(1, TILES, 2):
            post_wait(dve, S, h, t, nk, base)
            dve.tensor_copy(y[:ROWS[t], h, t * 512:(t + 1) * 512], E["ps"][:ROWS[t], t, 0:512]).then_inc(S["y_dve"], 1)
    dve.wait_ge(S["y_rms"], 1)
    dve.reciprocal(inv[:, :], rms[:, :]).then_inc(S["y_inv"], 1)
    dve.wait_ge(S["y_inv"], 1)
    dve.wait_ge(S["post_gain_loaded"], 16)
    for t, r in enumerate(ROWS):
        yt = y[:r, :, t * 512:(t + 1) * 512]
        dve.scalar_tensor_tensor(yt, yt, inv[:r, t:t + 1], gain[:r, :].rearrange("p (h n) -> p h n", h=2),
                                 ALU.mult, ALU.mult).then_inc(S["scaled"], 1)
    for t, r in enumerate(ROWS):
        dve.wait_ge(S["scaled"], t + 1)
        xt = E["x"][:r, t, :].rearrange("p (h n) -> p h n", h=2)
        dve.tensor_tensor(xt, xt, y[:r, :, t * 512:(t + 1) * 512], ALU.add).then_inc(S["added"], 1)


def ffn(nc, E, l, name, g_pre, w_in, w_out, g_post):
    sems = PRE_SEMS + POST_SEMS + WEIGHT_SEMS + "unit_done silu_done a_done a_hi a_lo"
    WORK = 3 * D_MODEL
    with stage(nc, name, sems) as (S, sb, block):
        room = sb("room", [P, WORK + 2 * SLOT])
        B = pre_buffers(sb, room[:, 0:WORK])
        W = weight_buffers(sb, room[:, WORK:].rearrange("p (s n) -> p s n", s=2))
        y = room[:, 0:2 * WORK].rearrange("p (h n) -> p h n", h=2)
        y_scratch = room[:, WORK + TILES * 512:WORK + TILES * 512 + D_MODEL]
        a_hi = sb("a_hi", [P, FF, NT], F32R)
        a_lo = sb("a_lo", [P, FF, NT], F32R)
        gate = sb("gate", [P, 4, HALF])
        w_v = w_in[bass.ds(l, 1)].rearrange("o (c p) (b f) -> p b (o c) f", p=P, b=2)

        @block.sync
        def _(sp):
            sp.dma_start(B["gain"][:], layer_row(g_pre, l)).then_inc(S["pre_gain_loaded"], 16)

            def load(slot, n):
                dst = W["raw"][:, slot].rearrange("p (b c f) -> p b c f", b=2, c=KC)
                for b in range(2):
                    sp.dma_start(dst[:, b], w_v[:, b, :, bass.ds(n * P, P)]).then_inc(raw_sem(S, slot), 16)

            load(0, 0)
            load(1, 1)
            with sp.Fori(1, FF // 2) as i:
                for slot in range(2):
                    weight_room(sp, S, 2 * i + slot)
                    load(slot, 2 * i + slot)
            sp.wait_ge(S["normed"], TILES)
            sp.dma_start(B["gain"][:], layer_row(g_post, l)).then_inc(S["post_gain_loaded"], 16)
            post_sync(sp, S, W, w_out, l, FF, FF)

        @block.tensor
        def _(pe):
            pre_tensor(pe, E, S, B)

            def two_chunks(i, first):
                for slot in range(2):
                    n = 2 * i + slot
                    pe.wait_ge(S["w_lo"], n + 1)
                    hi, lo = (W[x][:, slot].rearrange("p (b c f) -> p b c f", b=2, c=KC) for x in ("hi", "lo"))
                    for half in range(2):
                        k = 2 * slot + half
                        if not first:
                            pe.wait_ge(S["a_done"], 4 * i + k - 3)
                        hs = slice(half * HALF, (half + 1) * HALF)
                        for b in range(2):
                            for c in range(KC):
                                mm = split_products(pe, E["ps"][:, 2 * k + b, 0:HALF], hi[:, b, c], lo[:, b, c],
                                                    B["hi"][:, c, hs], B["lo"][:, c, hs], c == 0, c == KC - 1)
                        if half == 0:
                            mm.then_inc(S["unit_done"], 1)
                    mm.then_inc(S["chunk_done"], 1)

            two_chunks(0, True)
            with pe.Fori(1, FF // 2) as i:
                two_chunks(i, False)
            pe.wait_ge(S["a_lo"], 2 * FF)
            post_tensor(pe, E, S, W, a_hi, a_lo, FF, FF)

        def a_part(x, i, k):
            return x[:, bass.ds(2 * i + k // 2, 1), (k % 2) * HALF:(k % 2 + 1) * HALF].rearrange("p o n -> p (o n)")

        @block.scalar
        def _(act):
            split_scalar(act, S, W, 0, 0, 0, False)
            split_scalar(act, S, W, 1, 1, 0, False)
            pre_scalar(act, E, S, B)

            def two_chunks(i, first):
                for slot in range(2):
                    for half in range(2):
                        k = 2 * slot + half
                        if half == 0:
                            act.wait_ge(S["unit_done"], 2 * i + slot + 1)
                        else:
                            act.wait_ge(S["chunk_done"], 2 * i + slot + 1)
                        if not first:
                            act.wait_ge(S["a_lo"], 4 * i + k - 3)
                        act.activation(gate[:, k, :], E["ps"][:, 2 * k, 0:HALF], ACT.Silu).then_inc(S["silu_done"], 1)
                        act.wait_ge(S["a_done"], 4 * i + k + 1)
                        act.activation(a_part(a_hi, i, k), gate[:, k, :], ACT.Copy).then_inc(S["a_hi"], 1)
                    split_scalar(act, S, W, slot, 2 * i + slot + 2, i + 1, True)

            two_chunks(0, True)
            with act.Fori(1, FF // 2) as i:
                two_chunks(i, False)
            post_scalar(act, E, S, W, y, y_scratch, B["rms"], FF, FF, 0.5)

        @block.vector
        def _(dve):
            split_vector(dve, S, W, 0, 0)
            split_vector(dve, S, W, 1, 1)
            pre_vector(dve, E, S, B)
            with dve.Fori(0, FF // 2) as i:
                for slot in range(2):
                    for half in range(2):
                        k = 2 * slot + half
                        dve.wait_ge(S["silu_done"], 4 * i + k + 1)
                        dve.tensor_tensor(gate[:, k, :], gate[:, k, :], E["ps"][:, 2 * k + 1, 0:HALF],
                                          ALU.mult).then_inc(S["a_done"], 1)
                        dve.wait_ge(S["a_hi"], 4 * i + k + 1)
                        dve.tensor_tensor(a_part(a_lo, i, k), gate[:, k, :], a_part(a_hi, i, k).bitcast(F32),
                                          ALU.subtract).then_inc(S["a_lo"], 1)
                    split_vector(dve, S, W, slot, 2 * i + slot + 2)
            post_vector(dve, E, S, W, y, B["gain"], B["rms"], B["inv"], FF, FF)


BLOCKS = (
    ("turned", ((0, COL["aq"], 2 * W4),)),
    ("turned", ((0, COL["bq"], W4),)),
    ("turned", ((0, COL["dq"], 2 * W4),)),
    ("rows", ((0, COL["ak"], 2 * W4),)),
    ("rows", ((0, COL["ao"], W4), (W4, COL["cv"], W4))),
    ("rows", ((0, COL["bv"], 2 * W4),)),
    ("rows", ((0, COL["cq"], 2 * W4),)),
    ("rows", ((0, COL["dk"], 2 * W4),)),
)
AQ, AK, BQ, BK, DQ, DK = 0, 2, 4, 5, 6, 8
GATE_I, GATE_F, LOWRANK = 0, 32, 64
GATE_ROWS = LOWRANK + RANK
QK_SCALE = HD ** -0.5


def project(nc, E, M, l, g_pre, w_in, O):
    sems = PRE_SEMS + WEIGHT_SEMS + "unit_done act_out dve_out ones_set stored"
    KH = KC // 2
    GATE_COL = W4
    with stage(nc, "pr", sems) as (S, sb, block):
        B = pre_buffers(sb, sb("work", [P, 3 * D_MODEL]))
        W = weight_buffers(sb)
        w_v = w_in[bass.ds(l, 1)].rearrange("o (c p) f -> p (o c) f", p=P)

        units = []
        for b, (kind, parts) in enumerate(BLOCKS):
            if kind == "turned":
                width = sum(n for _, _, n in parts)
                units += [(b, kind, m, half) for m in range(width // P) for half in range(2)]
                if b == 1:
                    units += [(b, "gates", 0, half) for half in range(2)]
            else:
                units += [(b, kind, t, 0) for t in range(TILES)]
        first_tile = {0: AQ, 1: BQ, 2: DQ}
        numbers = [[n for n, u in enumerate(units) if u[0] == b] for b in range(len(BLOCKS))]
        chunks = 2 * len(BLOCKS)

        @block.sync
        def _(sp):
            sp.dma_start(B["gain"][:], layer_row(g_pre, l)).then_inc(S["pre_gain_loaded"], 16)
            for b, (kind, parts) in enumerate(BLOCKS):
                for hc in range(2):
                    n = 2 * b + hc
                    if n >= 2:
                        weight_room(sp, S, n)
                    dst = W["raw"][:, hc].rearrange("p (c f) -> p c f", c=KH)
                    cs = slice(KH * hc, KH * hc + KH)
                    if b == 1:
                        (at, src, width), = parts
                        sp.dma_start(dst[:, :, at:at + width], w_v[:, cs, src:src + width]).then_inc(raw_sem(S, hc), 16)
                        for row, part, width in ((GATE_I, "ai", H), (GATE_F, "af", H), (LOWRANK, "blr", RANK)):
                            at = GATE_COL + row
                            sp.dma_start(dst[:, :, at:at + width], w_v[:, cs, COL[part]:COL[part] + width]).then_inc(
                                raw_sem(S, hc), 16)
                    else:
                        if len(parts) == 1:
                            (at, src, width), = parts
                            parts = ((at, src, width // 2), (at + width // 2, src + width // 2, width // 2))
                        for at, src, width in parts:
                            sp.dma_start(dst[:, :, at:at + width], w_v[:, cs, src:src + width]).then_inc(
                                raw_sem(S, hc), 16)
            sp.wait_ge(S["act_out"], (len(units) + 1) // 2)
            sp.wait_ge(S["dve_out"], len(units) // 2)
            n = 0
            for src, pn, sn in ((M["DKV"][:, :, 0:W4], "p_sb_k", "s_sb_k"), (M["DKV"][:, :, W4:], "p_sb_v", "s_sb_v"),
                                (M["CV"][:], "p_win_v", "s_win_v")):
                po = O[pn][bass.ds(l, 1)].rearrange("o b (t p) h d -> p (o b t) (h d)", p=P)
                so = O[sn][bass.ds(l, 1)].rearrange("o b t h d -> (o b t) (h d)")
                sp.dma_start(po, src[:, 0:PT_TILES, :]).then_inc(S["stored"], 16)
                sp.dma_start(so, src[:NS, PT_TILES, :]).then_inc(S["stored"], 16)
                n += 2
            sp.wait_ge(S["stored"], 16 * n)

        def raw_count(n):
            return 16 * sum(4 if b == 1 else 2 for b in range(n // 2 + 1))

        @block.tensor
        def _(pe):
            pre_tensor(pe, E, S, B)
            for n in range(chunks):
                b, hc = n // 2, n % 2
                pe.wait_ge(S["w_lo"], n + 1)
                hi, lo = (W[x][:, hc].rearrange("p (c f) -> p c f", c=KH) for x in ("hi", "lo"))
                for u in numbers[b]:
                    _, kind, m, half = units[u]
                    if hc == 0 and u >= 8:
                        pe.wait_ge(S["act_out"] if u % 2 == 0 else S["dve_out"], (u - 8) // 2 + 1)
                    hs = slice(half * HALF, (half + 1) * HALF)
                    for c in range(KH):
                        cc = KH * hc + c
                        if kind == "rows":
                            out = E["ps"][:ROWS[m], u % 8, 0:512]
                            ops = (B["hi"][:, cc, tok(m)], B["lo"][:, cc, tok(m)], hi[:, c, :], lo[:, c, :])
                        else:
                            cols = slice(m * P, (m + 1) * P)
                            if kind == "gates":
                                cols = slice(GATE_COL, GATE_COL + GATE_ROWS)
                            out = E["ps"][:cols.stop - cols.start, u % 8, 0:HALF]
                            ops = (hi[:, c, cols], lo[:, c, cols], B["hi"][:, cc, hs], B["lo"][:, cc, hs])
                        mm = split_products(pe, out, *ops, cc == 0, cc == KC - 1)
                    if hc == 1 and u != numbers[b][-1]:
                        mm.then_inc(S["unit_done"], 1)
                mm.then_inc(S["chunk_done"], 1)

        def unit_wait(eng, u):
            b = units[u][0]
            if u == numbers[b][-1]:
                eng.wait_ge(S["chunk_done"], 2 * b + 2)
            else:
                eng.wait_ge(S["unit_done"], u + 1 - b)

        def copies(n):
            b, kind, m, half = units[n]
            hs = slice(half * HALF, (half + 1) * HALF)
            bank = E["ps"][:, n % 8, :]
            if kind == "turned":
                tile = first_tile[b] + m
                scale = {AK: QK_SCALE, AK + 1: QK_SCALE, BQ: DK_B ** -0.5, DQ: QK_SCALE, DQ + 1: QK_SCALE}.get(tile, 1.0)
                return [(M["TR"][:, tile, hs], bank[:, 0:HALF], scale)]
            if kind == "gates":
                return [(M["gates"][:, hs], bank[:GATE_ROWS, 0:HALF], 1.0)]
            r = ROWS[m]
            lo, hi = bank[:r, 0:W4], bank[:r, W4:512]
            if b == 3:
                return [(M["KA"][:r, m, :], lo, QK_SCALE),
                        (M["VA"][:r, m, :, 0:HD], hi.rearrange("p (h d) -> p h d", h=H), 1.0)]
            if b == 4:
                return [(M["AO"][:r, m, :], lo, 1.0), (M["CV"][:r, m, :], hi, 1.0)]
            whole = {5: M["BVG"], 6: M["CQK"], 7: M["DKV"]}[b]
            return [(whole[:r, m, :], bank[:r, :], 1.0)]

        @block.scalar
        def _(act):
            for n in range(2):
                act.wait_ge(raw_sem(S, n), raw_count(n))
                act.activation(W["hi"][:, n], W["raw"][:, n], ACT.Copy).then_inc(S["w_hi"], 1)
            pre_scalar(act, E, S, B)
            for n in range(2, chunks + 2):
                if n < chunks:
                    act.wait_ge(raw_sem(S, n % 2), raw_count(n))
                    act.wait_ge(S["chunk_done"], n - 1)
                    act.activation(W["hi"][:, n % 2], W["raw"][:, n % 2], ACT.Copy).then_inc(S["w_hi"], 1)
                if n % 2 == 1:
                    for u in numbers[(n - 2) // 2]:
                        if u % 2 == 0:
                            unit_wait(act, u)
                            for out, src, scale in copies(u):
                                ins = act.activation(out, src, ACT.Copy, scale=scale)
                            ins.then_inc(S["act_out"], 1)

        @block.vector
        def _(dve):
            dve.memset(M["VA"][:, :, :, HD:HD + 1], 1.0).then_inc(S["ones_set"], 1)
            split_vector(dve, S, W, 0, 0)
            split_vector(dve, S, W, 1, 1)
            pre_vector(dve, E, S, B)
            for n in range(2, chunks + 2):
                if n < chunks:
                    split_vector(dve, S, W, n % 2, n)
                if n % 2 == 1:
                    for u in numbers[(n - 2) // 2]:
                        if u % 2 == 1:
                            unit_wait(dve, u)
                            for out, src, scale in copies(u):
                                if scale == 1.0:
                                    ins = dve.tensor_copy(out, src)
                                else:
                                    ins = dve.tensor_scalar(out, src, scale, None, ALU.mult)
                            ins.then_inc(S["dve_out"], 1)


HEAD_SEMS = "squared ssq_done root_done root_inv_done head_scaled head_gated head_turned head_out "


def head_vector(dve, S, B, h, gate):
    n = len(PARTS)
    for rs, ts in PARTS:
        dve.tensor_tensor(B["sq"][rs, ts], h[rs, ts], h[rs, ts], ALU.mult).then_inc(S["squared"], 1)
    dve.wait_ge(S["squared"], n)
    for rs, ts in PARTS:
        dve.tensor_reduce(B["ssq"][rs, ts, :], B["sq"][rs, ts].rearrange("p t (h d) -> p t h d", h=H), AX.X,
                          ALU.add).then_inc(S["ssq_done"], 1)
    dve.wait_ge(S["root_done"], n)
    for rs, ts in PARTS:
        dve.reciprocal(B["ssq"][rs, ts, :], B["ssq"][rs, ts, :]).then_inc(S["root_inv_done"], 1)
    dve.wait_ge(S["root_inv_done"], n)
    for rs, ts in PARTS:
        hv = h[rs, ts].rearrange("p t (h d) -> p t h d", h=H)
        dve.tensor_tensor(hv, hv, B["ssq"][rs, ts, :].unsqueeze(3).to_broadcast(list(hv.shape)),
                          ALU.mult).then_inc(S["head_scaled"], 1)
    dve.wait_ge(S["head_scaled"], n)
    for rs, ts in PARTS:
        dve.tensor_tensor(h[rs, ts], h[rs, ts], gate[rs, ts], ALU.mult).then_inc(S["head_gated"], 1)


def head_scalar_root(act, E, S, B):
    act.wait_ge(S["ssq_done"], len(PARTS))
    for rs, ts in PARTS:
        act.activation(B["ssq"][rs, ts, :], B["ssq"][rs, ts, :], ACT.Sqrt, bias=E["eps"][rs, 0:1],
                       scale=1.0 / HD).then_inc(S["root_done"], 1)


def head_tensor(pe, E, S, h, bank):
    pe.wait_ge(S["head_gated"], len(PARTS))
    for t, r in enumerate(ROWS):
        for pair in range(2):
            n = 2 * t + pair
            if n >= 2:
                pe.wait_ge(S["head_out"], n - 1)
            pe.transpose(E["ps"][:, bank + n % 2, 0:r], h[:r, t, pair * P:(pair + 1) * P],
                         E["ident"][:r, :r]).then_inc(S["head_turned"], 1)


def head_scalar_out(act, E, M, S, chunk, bank):
    for t, r in enumerate(ROWS):
        for pair in range(2):
            n = 2 * t + pair
            act.wait_ge(S["head_turned"], n + 1)
            act.activation(M["mixT"][:, chunk + pair, tok(t)], E["ps"][:, bank + n % 2, 0:r], ACT.Copy).then_inc(S["head_out"], 1)


def head_buffers(sb):
    return dict(sq=sb("sq", [P, TILES, W4]), ssq=sb("ssq", [P, TILES, H]))


def mlstm(nc, E, M, l, I, O, C):
    sems = HEAD_SEMS + ("consts state bias gains dve_step act_step pe_step dve_to_act act_to_dve dve_to_pe "
                        "exps_done cols_turned cols_copied decay_copied n0_turned states_whole "
                        "query_bcast query_ready keys_ready bcast_done scores_done weights_done probs_done "
                        "out_whole out_copied p_state_done s_state_done s_state_added p_state_copied "
                        "n_turned n_copied stored gate_done")
    with stage(nc, "ml", sems) as (S, sb, block):
        HB = head_buffers(sb)
        sel = sb("sel", [H, H, P])
        mask = sb("mask", [P, P])
        s_mask = sb("s_mask", [NS, NS])
        keep = sb("keep", [H, NT])
        cut = sb("cut", [H, NT])
        pair_tok = sb("pair_tok", [P, DEC_BATCH // 2, NS])
        pair_last = sb("pair_last", [NS, DEC_BATCH // 2, P])
        tok_req = sb("tok_req", [NS, DEC_BATCH])
        b_i = sb("b_i", [H, 1])
        b_f = sb("b_f", [P, 1])
        m0 = sb("m0", [H, DEC_BATCH])
        n0 = sb("n0", [4 * H, P])
        gain = sb("gain", [P, W4])
        c0 = sb("c0", [P, 4, H, HD + 1])
        ig = sb("ig", [H, NT])
        fy = sb("fy", [H, NT])
        sp_ = sb("softplus", [H, NT])
        lf = sb("lf", [H, NT])
        lfc = sb("lf_cut", [H, NT])
        floor = sb("floor", [H, NT])
        st0 = sb("start", [H, DEC_BATCH])
        bsum = sb("bsum", [H, NT])
        m = sb("m", [H, NT])
        a = sb("a", [H, NT])
        wrow = sb("wrow", [H, NT])
        ws = sb("ws", [H, NT])
        em = sb("em", [H, NT])
        ea = sb("ea", [H, NS])
        cols = sb("cols", [P, 3, TILES, H])
        ea_col = sb("ea_col", [NS, H])
        decay = sb("decay", [P, 4, H])
        qd = sb("qd", [P, H, NS])
        qm = sb("qm", [P, H, 4, NS])
        km = sb("km", [NS, H, DEC_BATCH, HD])
        ex = sb("ex", [P, 2, SEQ])
        pr = sb("pr", [P, 2, SEQ])
        oc = sb("oc", [P, H, TILES, HD + 1])
        den = sb("den", [P, TILES, H])
        den2 = sb("den2", [P, TILES, H])
        hA = sb("hA", [P, TILES, W4])
        pc = sb("pc", [HD, H, HD + 1])
        pn = sb("pn", [4 * H, P])
        np_ = sb("np", [H, HD])
        ps = E["ps"]
        first = SEQ
        last = SEQ + DEC_SEQ - 1

        def s_rows(x):
            return x[:, first:NT].rearrange("p (r t) -> p r t", t=DEC_SEQ)

        @block.sync
        def _(sp):
            for dst, n in ((sel, "head_rows"), (mask, "turned_mask"), (s_mask, "s_turned_mask"), (keep, "keep_a"),
                           (cut, "cut_a"), (pair_tok, "pair_tokens"), (pair_last, "pair_last"),
                           (tok_req, "token_request")):
                sp.dma_start(dst[:], C[n]).then_inc(S["consts"], 16)
            sp.dma_start(b_i[:], layer_col(I["b_ig"], l)).then_inc(S["bias"], 16)
            sp.dma_start(b_f[GATE_F:GATE_F + H, :], layer_col(I["b_fg"], l)).then_inc(S["bias"], 16)
            with nc.allow_non_contiguous_dma(reason="32 stabilisers"):
                sp.dma_start(m0[:], I["state_mlstm_m"][bass.ds(l, 1)].rearrange("o r h -> h (o r)")).then_inc(S["bias"], 16)
            sp.dma_start(gain[:], layer_row(I["g_head_a"], l)).then_inc(S["gains"], 16)
            nv = I["state_mlstm_n"][bass.ds(l, 1)].rearrange("o (q j) h d -> q h (o j) d", j=2)
            for q in range(4):
                sp.dma_start(n0[H * q:H * q + H, :].rearrange("p (j d) -> p j d", j=2), nv[q]).then_inc(S["state"], 16)
            cv = I["state_mlstm_c"][bass.ds(l, 1)].rearrange("o (q j) h d e -> j h (o d) q e", j=2)
            for j in range(2):
                for h in range(H):
                    sp.dma_start(c0[j * HD:(j + 1) * HD, :, h, 0:HD], cv[j, h]).then_inc(S["state"], 16)
            n = 0
            sp.wait_ge(S["p_state_copied"], 1)
            sp.dma_start(O["p_mlstm_c"][bass.ds(l, 1)].rearrange("o b h d e -> d (o b h) e"), pc[:, :, 0:HD]).then_inc(S["stored"], 16)
            n += 1
            with nc.allow_non_contiguous_dma(reason="the last stabilisers"):
                sp.dma_start(O["p_mlstm_m"][bass.ds(l, 1)].rearrange("o b h -> h (o b)"), m[:, SEQ - 1:SEQ]).then_inc(S["stored"], 16)
                sp.dma_start(O["s_mlstm_m"][bass.ds(l, 1)].rearrange("o r h -> h (o r)"),
                             m[:, last:NT:DEC_SEQ]).then_inc(S["stored"], 16)
            n += 2
            sp.wait_ge(S["s_state_added"], 2 * H)
            cw = O["s_mlstm_c"][bass.ds(l, 1)].rearrange("o (q j) h d e -> j h (o d) q e", j=2)
            for j in range(2):
                for h in range(H):
                    sp.dma_start(cw[j, h], c0[j * HD:(j + 1) * HD, :, h, 0:HD]).then_inc(S["stored"], 16)
                    n += 1
            sp.wait_ge(S["n_copied"], 2)
            sp.dma_start(O["p_mlstm_n"][bass.ds(l, 1)].rearrange("o b h d -> (o b h) d"), np_[:]).then_inc(S["stored"], 16)
            nw = O["s_mlstm_n"][bass.ds(l, 1)].rearrange("o (q j) h d -> q h (o j) d", j=2)
            for q in range(4):
                sp.dma_start(nw[q], pn[H * q:H * q + H, :].rearrange("p (j d) -> p j d", j=2)).then_inc(S["stored"], 16)
            n += 5
            sp.wait_ge(S["stored"], 16 * n)

        units = [(h, c) for h in range(H) for c in range(TILES)]

        def width(c):
            return SEQ - c * P if c < PT_TILES else NS

        def queries(c):
            return slice(c * P, SEQ) if c < PT_TILES else slice(SEQ, NT)

        @block.vector
        def _(dve):
            step = stepper(dve, S["dve_step"])
            dve.wait_ge(S["bias"], 48)
            dve.wait_ge(S["consts"], 16 * 8)
            step(dve.tensor_scalar(ig[:], M["gates"][GATE_I:GATE_I + H, :], b_i[:, 0:1], None, ALU.add))
            dve.tensor_scalar(fy[:], M["gates"][GATE_F:GATE_F + H, :], b_f[GATE_F:GATE_F + H, 0:1], None,
                              ALU.add).then_inc(S["dve_to_act"], 1)
            dve.wait_ge(S["dve_to_act"], 1)
            dve.wait_ge(S["act_to_dve"], 3)
            step(dve.scalar_tensor_tensor(lf[:], fy[:], 0.0, sp_[:], ALU.min, ALU.subtract))
            step(dve.tensor_tensor_scan(bsum[:], keep[:], lf[:], 0.0, ALU.mult, ALU.add))
            step(dve.tensor_tensor(lfc[:], lf[:], cut[:], ALU.add))
            step(dve.tensor_copy(floor[:], ig[:]))
            step(dve.tensor_tensor(st0[:], lf[:, first:NT:DEC_SEQ], m0[:], ALU.add))
            step(dve.tensor_tensor(floor[:, first:NT:DEC_SEQ], ig[:, first:NT:DEC_SEQ], st0[:], ALU.max))
            step(dve.tensor_tensor_scan(m[:], lfc[:], floor[:], 0.0, ALU.add, ALU.max))
            step(dve.tensor_tensor(a[:], bsum[:], m[:], ALU.subtract))
            step(dve.tensor_tensor(wrow[:], ig[:], bsum[:], ALU.subtract))
            step(dve.tensor_scalar(ws[:, 0:SEQ], wrow[:, 0:SEQ], a[:, SEQ - 1:SEQ], None, ALU.add))
            step(dve.tensor_tensor(s_rows(ws), s_rows(wrow),
                                   a[:, last:NT:DEC_SEQ].unsqueeze(2).to_broadcast([H, DEC_BATCH, DEC_SEQ]), ALU.add))
            dve.tensor_tensor(ea[:].rearrange("p (r t) -> p r t", t=DEC_SEQ), s_rows(a),
                              m0[:].unsqueeze(2).to_broadcast([H, DEC_BATCH, DEC_SEQ]), ALU.add).then_inc(S["dve_to_act"], 1)

            dve.wait_ge(S["cols_turned"], 1)
            n = TILES * H
            cps = ps[:, 7, 0:3 * n].rearrange("p (k t h) -> p k t h", k=3, t=TILES)
            for rs, ts in PARTS:
                step(dve.tensor_copy(cols[rs, :, ts, :], cps[rs, :, ts, :]))
            dve.tensor_copy(ea_col[:], ps[:NS, 7, 3 * n:3 * n + H]).then_inc(S["cols_copied"], 1)
            dve.wait_ge(S["n0_turned"], 1)
            dve.wait_ge(S["state"], 16 * 12)
            step(dve.tensor_copy(decay[:], ps[:, 7, 0:16].rearrange("p (q h) -> p q h", q=4)))
            step(dve.tensor_copy(c0[:, :, :, HD], ps[:, 7, 16:32].rearrange("p (q h) -> p q h", q=4)))

            dve.wait_ge(S["query_bcast"], 1)
            for h in range(H):
                o = (h % 2) * HD
                for j in range(2):
                    step(dve.tensor_tensor(qd[j * HD:(j + 1) * HD, h, :], M["TR"][o:o + HD, AQ + h // 2, SEQ:NT],
                                           ps[j * HD:(j + 1) * HD, 6, h * NS:(h + 1) * NS], ALU.mult))
            for h in range(H):
                dve.tensor_tensor(qm[:, h], pair_tok[:], qd[:, h, :].unsqueeze(1).to_broadcast([P, 4, NS]),
                                  ALU.mult).then_inc(S["query_ready"], 1)
            for rs, ts in PARTS:
                kv = M["KA"][rs, ts, :].rearrange("p t (h d) -> p t h d", h=H)
                step(dve.tensor_tensor(kv, kv, cols[rs, 1, ts, :].unsqueeze(3).to_broadcast(list(kv.shape)), ALU.mult))
            for h in range(H):
                dve.tensor_tensor(km[:, h], M["KA"][:NS, PT_TILES, h * HD:(h + 1) * HD].unsqueeze(1).to_broadcast(
                    [NS, DEC_BATCH, HD]), tok_req[:].unsqueeze(2).to_broadcast([NS, DEC_BATCH, HD]),
                    ALU.mult).then_inc(S["keys_ready"], 1)
            for u, (h, c) in enumerate(units):
                dve.wait_ge(S["weights_done"], u + 1)
                dve.wait_ge(S["scores_done"], u + 1)
                r, w = ROWS[c], width(c)
                if u >= 2:
                    dve.wait_ge(S["pe_step"], u - 1)
                dve.tensor_tensor(pr[:r, u % 2, 0:w], ex[:r, u % 2, 0:w], ps[:r, 2 + u % 2, 0:w],
                                  ALU.mult).then_inc(S["probs_done"], 1)
            dve.wait_ge(S["p_state_done"], 1)
            dve.tensor_copy(pc[:], ps[:HD, 6, 0:H * (HD + 1)].rearrange("p (h e) -> p h e", h=H)).then_inc(S["p_state_copied"], 1)
            for h in range(H):
                dve.wait_ge(S["out_copied"], H)
                dve.tensor_tensor(c0[:, :, h, :], c0[:, :, h, :],
                                  decay[:, :, h].unsqueeze(2).to_broadcast([P, 4, HD + 1]), ALU.mult).then_inc(S["s_state_added"], 1)
                dve.wait_ge(S["s_state_added"], 2 * h + 1)
                dve.wait_ge(S["s_state_done"], h + 1)
                dve.tensor_tensor(c0[:, :, h, :], c0[:, :, h, :],
                                  ps[:, h % 2, 0:4 * (HD + 1)].rearrange("p (q e) -> p q e", q=4), ALU.add).then_inc(S["s_state_added"], 1)
            for rs, ts in PARTS:
                dv = oc[rs, :, ts, HD].rearrange("p h t -> p t h")
                step(dve.tensor_copy(den[rs, ts], dv))
                step(dve.scalar_tensor_tensor(den2[rs, ts], den[rs, ts], -1.0, den[rs, ts], ALU.mult, ALU.max))
                step(dve.tensor_tensor(den2[rs, ts], den2[rs, ts], cols[rs, 2, ts, :], ALU.max))
                step(dve.reciprocal(den2[rs, ts], den2[rs, ts]))
                for h in range(H):
                    nt = ts.stop - ts.start
                    step(dve.tensor_tensor(hA[rs, ts, h * HD:(h + 1) * HD], oc[rs, h, ts, 0:HD],
                                           den2[rs, ts, h].unsqueeze(2).to_broadcast([rs.stop, nt, HD]), ALU.mult))
            dve.wait_ge(S["gains"], 16)
            dve.wait_ge(S["gate_done"], 2)
            for rs, ts in PARTS:
                nt = ts.stop - ts.start
                step(dve.tensor_tensor(M["AO"][rs, ts, :], M["AO"][rs, ts, :],
                                       gain[rs].unsqueeze(1).to_broadcast([rs.stop, nt, W4]), ALU.mult))
            head_vector(dve, S, HB, hA, M["AO"])

        @block.scalar
        def _(act):
            act.wait_ge(S["dve_to_act"], 1)
            act.activation(sp_[:], fy[:], ACT.Abs).then_inc(S["act_to_dve"], 1)
            act.wait_ge(S["act_to_dve"], 1)
            act.activation(sp_[:], sp_[:], ACT.Exp, scale=-1.0).then_inc(S["act_to_dve"], 1)
            act.wait_ge(S["act_to_dve"], 2)
            act.activation(sp_[:], sp_[:], ACT.Ln, bias=1.0).then_inc(S["act_to_dve"], 1)
            act.wait_ge(S["dve_to_act"], 2)
            act.activation(ws[:], ws[:], ACT.Exp).then_inc(S["exps_done"], 1)
            act.activation(em[:], m[:], ACT.Exp, scale=-1.0).then_inc(S["exps_done"], 1)
            act.activation(ea[:], ea[:], ACT.Exp).then_inc(S["exps_done"], 1)
            act.wait_ge(S["cols_copied"], 1)
            for u, (h, c) in enumerate(units):
                act.wait_ge(S["bcast_done"], u + 1)
                r, w = ROWS[c], width(c)
                if u >= 2:
                    act.wait_ge(S["probs_done"], u - 1)
                act.activation(ex[:r, u % 2, 0:w], ps[:r, u % 2, 0:w], ACT.Exp,
                               bias=cols[:r, 0, c, h:h + 1]).then_inc(S["weights_done"], 1)
                if c == TILES - 1:
                    act.wait_ge(S["out_whole"], h + 1)
                    act.activation(oc[:, h, 0:PT_TILES, :],
                                   ps[:, 4 + h % 2, 0:PT_TILES * (HD + 1)].rearrange("p (t e) -> p t e", t=PT_TILES),
                                   ACT.Copy)
                    act.activation(oc[:NS, h, PT_TILES, :],
                                   ps[:NS, 4 + h % 2, PT_TILES * (HD + 1):TILES * (HD + 1)], ACT.Copy).then_inc(S["out_copied"], 1)
            for rs, ts in PARTS:
                act.activation(M["AO"][rs, ts, :], M["AO"][rs, ts, :], ACT.Sigmoid).then_inc(S["gate_done"], 1)
            head_scalar_root(act, E, S, HB)
            head_scalar_out(act, E, M, S, 0, 2)
            act.wait_ge(S["n_turned"], 1)
            act.activation(np_[:], ps[:H, 4, 0:HD], ACT.Copy).then_inc(S["n_copied"], 1)
            act.activation(pn[:], ps[:4 * H, 4, P:2 * P], ACT.Copy).then_inc(S["n_copied"], 1)

        @block.tensor
        def _(pe):
            pe.wait_ge(S["exps_done"], 3)
            n = TILES * H
            for k, row in enumerate((wrow, ws, em)):
                for t, r in enumerate(ROWS):
                    pe.transpose(ps[:r, 7, k * n + t * H:k * n + (t + 1) * H], row[:, tok(t)], E["ident"][:H, :H])
            pe.transpose(ps[:NS, 7, 3 * n:3 * n + H], ea[:], E["ident"][:H, :H]).then_inc(S["cols_turned"], 1)
            pe.wait_ge(S["consts"], 16 * 8)
            for h in range(H):
                mm = pe.matmul(ps[:, 6, h * NS:(h + 1) * NS], sel[:, h, :], ea[:], start=True, stop=True)
            mm.then_inc(S["query_bcast"], 1)
            pe.wait_ge(S["cols_copied"], 1)
            pe.wait_ge(S["state"], 16 * 12)
            for q in range(4):
                pe.matmul(ps[:, 7, q * H:(q + 1) * H], pair_last[:, q, :], ea_col[:], start=True, stop=True)
            pe.transpose(ps[:, 7, 16:32], n0[:], E["ident"][:4 * H, :4 * H]).then_inc(S["n0_turned"], 1)

            def scores(u):
                h, c = units[u]
                r, w, o = ROWS[c], width(c), (h % 2) * HD
                qs = queries(c)
                if u >= 2:
                    pe.wait_ge(S["weights_done"], u - 1)
                    pe.wait_ge(S["probs_done"], u - 1)
                pe.matmul(ps[:r, u % 2, 0:r], E["ident"][:r, :r], (mask if c < PT_TILES else s_mask)[:r, :r],
                          start=True, stop=False, skip_group_check=True)
                pe.matmul(ps[:r, u % 2, 0:w], sel[:, h, 0:r], a[:, qs], start=False, stop=True,
                          skip_group_check=True).then_inc(S["bcast_done"], 1)
                pe.matmul(ps[:r, 2 + u % 2, 0:w], M["TR"][o:o + HD, AK + h // 2, tok(c)],
                          M["TR"][o:o + HD, AQ + h // 2, qs], start=True, stop=True).then_inc(S["scores_done"], 1)

            def outputs(u):
                h, c = units[u]
                r = ROWS[c]
                pe.wait_ge(S["probs_done"], u + 1)
                if c == 0 and h >= 2:
                    pe.wait_ge(S["out_copied"], h - 1)
                if c < PT_TILES:
                    for t in range(c, PT_TILES):
                        mm = pe.matmul(ps[:, 4 + h % 2, t * (HD + 1):(t + 1) * (HD + 1)],
                                       pr[:r, u % 2, (t - c) * P:(t - c + 1) * P], M["VA"][:r, c, h, :],
                                       start=(c == 0 and t == 0), stop=(c == t), skip_group_check=True)
                    mm.then_inc(S["pe_step"], 1)
                else:
                    out = ps[:NS, 4 + h % 2, PT_TILES * (HD + 1):TILES * (HD + 1)]
                    pe.matmul(out, pr[:NS, u % 2, 0:NS], M["VA"][:NS, c, h, :], start=False, stop=False,
                              skip_group_check=True).then_inc(S["pe_step"], 1)
                    for q in range(4):
                        mm = pe.matmul(out, qm[:, h, q, :], c0[:, q, h, :], start=False, stop=(q == 3),
                                       skip_group_check=True)
                    mm.then_inc(S["out_whole"], 1)

            pe.wait_ge(S["query_ready"], H)
            for u in range(len(units) + 1):
                if u < len(units):
                    scores(u)
                if u >= 1:
                    outputs(u - 1)
            pe.wait_ge(S["keys_ready"], H)
            for h in range(H):
                for t in range(PT_TILES):
                    mm = pe.matmul(ps[:HD, 6, h * (HD + 1):(h + 1) * (HD + 1)], M["KA"][:, t, h * HD:(h + 1) * HD],
                                   M["VA"][:, t, h, :], start=(h == 0 and t == 0), stop=(t == PT_TILES - 1),
                                   skip_group_check=True)
            mm.then_inc(S["p_state_done"], 1)
            pe.wait_ge(S["weights_done"], len(units))
            for h in range(H):
                if h >= 2:
                    pe.wait_ge(S["s_state_added"], 2 * (h - 1))
                for q in range(4):
                    mm = pe.matmul(ps[:, h % 2, q * (HD + 1):(q + 1) * (HD + 1)],
                                   km[:, h, 2 * q:2 * q + 2, :].rearrange("p j d -> p (j d)"),
                                   M["VA"][:NS, PT_TILES, h, :], start=True, stop=True)
                mm.then_inc(S["s_state_done"], 1)
            pe.wait_ge(S["p_state_copied"], 1)
            pe.wait_ge(S["s_state_added"], 2 * H)
            pe.wait_ge(S["out_copied"], H)
            pe.transpose(ps[:H, 4, 0:HD], pc[:, :, HD], E["ident"][:HD, :HD])
            pe.transpose(ps[:4 * H, 4, P:2 * P], c0[:, :, :, HD].rearrange("p q h -> p (q h)"), E["ident"][:]).then_inc(S["n_turned"], 1)
            head_tensor(pe, E, S, hA, 2)


def gla(nc, E, M, l, I, O, C):
    NCH = SEQ // CHUNK
    sems = HEAD_SEMS + ("consts params states cleared dve_step low_ready pre_done pre_out y_ready act_to_dve "
                        "sums_ready exps_done factors_ready query_ready att_done att_ready keys_turned keys_ready "
                        "update_done state_new out_done out_copied s_query_ready s_keys_ready s_update_done "
                        "s_state_new gate_done stored")
    with stage(nc, "gl", sems) as (S, sb, block):
        HB = head_buffers(sb)
        keep = sb("keep", [P, NT])
        mask = sb("mask", [P, P])
        s_mask = sb("s_mask", [NS, NS])
        head = sb("head", [P, H])
        head_cols = sb("head_cols", [P, W4])
        req_tok = sb("req_tok", [P, DEC_BATCH, NS])
        tok_req = sb("tok_req", [NS, DEC_BATCH])
        w2 = sb("w2", [RANK, P])
        bias = sb("bias", [P, 1])
        gain = sb("gain", [P, W4])
        low = sb("low", [RANK, NT])
        y = sb("y", [P, NT])
        sp_ = sb("softplus", [P, NT])
        bsum = sb("bsum", [P, NT])
        mid = sb("mid", [P, NT])
        rest = sb("rest", [P, NT])
        e1 = sb("e1", [P, NT])
        whole = sb("whole", [P, NCH + DEC_BATCH])
        state = sb("state", [P, NCH + 1, W4])
        s_state = sb("s_state", [P, DEC_BATCH, W4])
        upd = sb("upd", [P, W4])
        qq = sb("qq", [P, NT])
        qi = sb("qi", [P, NT])
        kk = sb("kk", [P, NT])
        kd = sb("kd", [P, NT])
        qh = sb("qh", [P, 2, H, P])
        att = sb("att", [P, 2, H, P])
        kdt = sb("kdt", [P, TILES, P])
        s_qi = sb("s_qi", [P, DEC_BATCH, NS])
        s_kd = sb("s_kd", [NS, DEC_BATCH, P])
        hB = sb("hB", [P, TILES, W4])
        ps = E["ps"]

        def chunks(x):
            return (x[:, 0:SEQ].rearrange("p (c t) -> p c t", t=CHUNK),
                    x[:, SEQ:NT].rearrange("p (c t) -> p c t", t=DEC_SEQ))

        @block.sync
        def _(sp):
            for dst, n in ((keep, "keep_b"), (mask, "gla_mask"), (s_mask, "s_gla_mask"), (head, "gla_head"),
                           (head_cols, "gla_cols"), (req_tok, "request_tokens"), (tok_req, "token_request")):
                sp.dma_start(dst[:], C[n]).then_inc(S["consts"], 16)
            sp.dma_start(w2[:], I["w_gla_a2"][bass.ds(l, 1)].rearrange("o r n -> (o r) n")).then_inc(S["params"], 16)
            sp.dma_start(bias[:], layer_col(I["b_gla_a"], l)).then_inc(S["params"], 16)
            sp.dma_start(gain[:], layer_row(I["g_head_b"], l)).then_inc(S["params"], 16)
            sp.wait_ge(S["cleared"], 2)
            for h in range(H):
                sp.dma_start(s_state[h * DK_B:(h + 1) * DK_B, :, h * HD:(h + 1) * HD],
                             I["state_gla_s"][bass.ds(l, 1), :, h].rearrange("o r d e -> d (o r) e")).then_inc(S["states"], 16)
            n = 0
            sp.wait_ge(S["state_new"], NCH)
            for h in range(H):
                sp.dma_start(O["p_gla_s"][bass.ds(l, 1), 0, h].rearrange("o d e -> (o d) e"),
                             state[h * DK_B:(h + 1) * DK_B, NCH, h * HD:(h + 1) * HD]).then_inc(S["stored"], 16)
            sp.wait_ge(S["s_state_new"], DEC_BATCH)
            for h in range(H):
                sp.dma_start(O["s_gla_s"][bass.ds(l, 1), :, h].rearrange("o r d e -> d (o r) e"),
                             s_state[h * DK_B:(h + 1) * DK_B, :, h * HD:(h + 1) * HD]).then_inc(S["stored"], 16)
            sp.wait_ge(S["stored"], 16 * 2 * H)

        @block.vector
        def _(dve):
            step = stepper(dve, S["dve_step"])
            dve.memset(state[:, 0, :], 0.0).then_inc(S["cleared"], 1)
            dve.memset(s_state[:], 0.0).then_inc(S["cleared"], 1)
            dve.tensor_copy(low[:], M["gates"][LOWRANK:LOWRANK + RANK, :]).then_inc(S["low_ready"], 1)
            dve.wait_ge(S["params"], 48)
            dve.wait_ge(S["consts"], 16 * 7)
            dve.wait_ge(S["pre_done"], 1)
            for half in range(2):
                dve.tensor_scalar(y[:, half * HALF:(half + 1) * HALF], ps[:, half, 0:HALF], bias[:, 0:1], None,
                                  ALU.add).then_inc(S["y_ready"], 1)
            dve.wait_ge(S["y_ready"], 2)
            dve.wait_ge(S["act_to_dve"], 3)
            step(dve.scalar_tensor_tensor(y[:], y[:], 0.0, sp_[:], ALU.min, ALU.subtract))
            step(dve.tensor_scalar(y[:], y[:], 1.0 / TAU, None, ALU.mult))
            step(dve.tensor_tensor_scan(bsum[:], keep[:], y[:], 0.0, ALU.mult, ALU.add))
            for v, mv, rv, size in ((chunks(bsum)[0], chunks(mid)[0], chunks(rest)[0], CHUNK),
                                    (chunks(bsum)[1], chunks(mid)[1], chunks(rest)[1], DEC_SEQ)):
                shape = [P, v.shape[1], size]
                step(dve.tensor_tensor(mv, v, v[:, :, size // 2 - 1:size // 2].to_broadcast(shape), ALU.subtract))
                step(dve.tensor_tensor(rv, v[:, :, size - 1:size].to_broadcast(shape), v, ALU.subtract))
            step(dve.tensor_copy(whole[:, 0:NCH], bsum[:, CHUNK - 1:SEQ:CHUNK]))
            dve.tensor_copy(whole[:, NCH:], bsum[:, SEQ + DEC_SEQ - 1:NT:DEC_SEQ]).then_inc(S["sums_ready"], 1)
            for n, (dst, x, e) in enumerate(((qi, BQ, y), (qq, BQ, e1), (kk, BK, mid), (kd, BK, rest))):
                dve.wait_ge(S["exps_done"], n + 1)
                dve.tensor_tensor(dst[:], M["TR"][:, x, :], e[:], ALU.mult).then_inc(S["factors_ready"], 1)
            dve.wait_ge(S["factors_ready"], 4)
            dve.wait_ge(S["exps_done"], 5)
            dve.wait_ge(S["states"], 16 * H)

            def spread_query(t):
                r = ROWS[t]
                if t >= 2:
                    dve.wait_ge(S["att_done"], t - 1)
                dve.tensor_tensor(qh[:, t % 2, :, 0:r], qq[:, tok(t)].unsqueeze(1).to_broadcast([P, H, r]),
                                  head[:].unsqueeze(2).to_broadcast([P, H, r]), ALU.mult).then_inc(S["query_ready"], 1)

            spread_query(0)
            for t, r in enumerate(ROWS):
                if t + 1 < TILES:
                    spread_query(t + 1)
                dve.wait_ge(S["att_done"], t + 1)
                if t >= 2:
                    dve.wait_ge(S["out_done"], t - 1)
                mk = (mask if t < PT_TILES else s_mask)[:r, :r]
                dve.tensor_tensor(att[:r, t % 2, :, 0:r], ps[:r, t % 2, 0:H * r].rearrange("p (h t) -> p h t", h=H),
                                  mk.unsqueeze(1).to_broadcast([r, H, r]), ALU.mult).then_inc(S["att_ready"], 1)
                dve.wait_ge(S["keys_turned"], t + 1)
                dve.tensor_copy(kdt[:r, t, :], ps[:r, 2 + t % 2, 0:P]).then_inc(S["keys_ready"], 1)
                if t < PT_TILES:
                    for j in range(2):
                        c = 2 * t + j
                        dve.wait_ge(S["update_done"], c + 1)
                        step(dve.tensor_tensor(upd[:], ps[:, 4 + j, 0:W4], head_cols[:], ALU.mult))
                        dve.scalar_tensor_tensor(state[:, c + 1, :], state[:, c, :], whole[:, c:c + 1], upd[:],
                                                 ALU.mult, ALU.add).then_inc(S["state_new"], 1)
                        dve.wait_ge(S["state_new"], c + 1)
            dve.tensor_tensor(s_qi[:], qi[:, SEQ:NT].unsqueeze(1).to_broadcast([P, DEC_BATCH, NS]), req_tok[:],
                              ALU.mult).then_inc(S["s_query_ready"], 1)
            dve.wait_ge(S["keys_ready"], TILES)
            dve.tensor_tensor(s_kd[:], kdt[:NS, PT_TILES, :].unsqueeze(1).to_broadcast([NS, DEC_BATCH, P]),
                              tok_req[:].unsqueeze(2).to_broadcast([NS, DEC_BATCH, P]), ALU.mult).then_inc(S["s_keys_ready"], 1)
            dve.wait_ge(S["out_done"], TILES)
            for s in range(DEC_BATCH):
                dve.wait_ge(S["s_update_done"], s + 1)
                step(dve.tensor_tensor(upd[:], ps[:, 4 + s % 2, 0:W4], head_cols[:], ALU.mult))
                dve.scalar_tensor_tensor(s_state[:, s, :], s_state[:, s, :], whole[:, NCH + s:NCH + s + 1], upd[:],
                                         ALU.mult, ALU.add).then_inc(S["s_state_new"], 1)
                dve.wait_ge(S["s_state_new"], s + 1)
            dve.wait_ge(S["gate_done"], 2)
            for rs, ts in PARTS:
                nt = ts.stop - ts.start
                step(dve.tensor_tensor(M["BVG"][rs, ts, W4:], M["BVG"][rs, ts, W4:],
                                       gain[rs].unsqueeze(1).to_broadcast([rs.stop, nt, W4]), ALU.mult))
            dve.wait_ge(S["out_copied"], TILES)
            head_vector(dve, S, HB, hB, M["BVG"][:, :, W4:])

        @block.scalar
        def _(act):
            for rs, ts in PARTS:
                act.activation(M["BVG"][rs, ts, W4:], M["BVG"][rs, ts, W4:], ACT.Silu).then_inc(S["gate_done"], 1)
            act.wait_ge(S["y_ready"], 2)
            act.activation(sp_[:], y[:], ACT.Abs).then_inc(S["act_to_dve"], 1)
            act.wait_ge(S["act_to_dve"], 1)
            act.activation(sp_[:], sp_[:], ACT.Exp, scale=-1.0).then_inc(S["act_to_dve"], 1)
            act.wait_ge(S["act_to_dve"], 2)
            act.activation(sp_[:], sp_[:], ACT.Ln, bias=1.0).then_inc(S["act_to_dve"], 1)
            act.wait_ge(S["sums_ready"], 1)
            act.activation(y[:], bsum[:], ACT.Exp).then_inc(S["exps_done"], 1)
            act.activation(e1[:], mid[:], ACT.Exp).then_inc(S["exps_done"], 1)
            act.wait_ge(S["exps_done"], 2)
            act.activation(mid[:], mid[:], ACT.Exp, scale=-1.0).then_inc(S["exps_done"], 1)
            act.activation(rest[:], rest[:], ACT.Exp).then_inc(S["exps_done"], 1)
            act.activation(whole[:], whole[:], ACT.Exp).then_inc(S["exps_done"], 1)
            for t, r in enumerate(ROWS):
                act.wait_ge(S["out_done"], t + 1)
                act.activation(hB[:r, t, :], ps[:r, 6 + t % 2, 0:W4], ACT.Copy).then_inc(S["out_copied"], 1)
            head_scalar_root(act, E, S, HB)
            head_scalar_out(act, E, M, S, 2, 2)

        @block.tensor
        def _(pe):
            pe.wait_ge(S["params"], 48)
            pe.wait_ge(S["low_ready"], 1)
            for half in range(2):
                mm = pe.matmul(ps[:, half, 0:HALF], w2[:], low[:, half * HALF:(half + 1) * HALF], start=True, stop=True)
            mm.then_inc(S["pre_done"], 1)
            pe.wait_ge(S["factors_ready"], 4)

            def inside(t):
                r = ROWS[t]
                if t >= 2:
                    pe.wait_ge(S["att_ready"], t - 1)
                    pe.wait_ge(S["keys_ready"], t - 1)
                pe.wait_ge(S["query_ready"], t + 1)
                rhs = qh[:, t % 2, :, 0:r]
                out = ps[:r, t % 2, 0:H * r].rearrange("p (h t) -> p h t", h=H)
                pe.matmul(out, kk[:, tok(t)], rhs, start=True, stop=True).then_inc(S["att_done"], 1)
                pe.transpose(ps[:r, 2 + t % 2, 0:P], kd[:, tok(t)], E["ident"][:]).then_inc(S["keys_turned"], 1)

            inside(0)
            for t, r in enumerate(ROWS):
                if t + 1 < TILES:
                    inside(t + 1)
                pe.wait_ge(S["keys_ready"], t + 1)
                if t < PT_TILES:
                    for j in range(2):
                        c = 2 * t + j
                        if c >= 2:
                            pe.wait_ge(S["state_new"], c - 1)
                        pe.matmul(ps[:, 4 + j, 0:W4], kdt[j * CHUNK:(j + 1) * CHUNK, t, :],
                                  M["BVG"][j * CHUNK:(j + 1) * CHUNK, t, 0:W4], start=True, stop=True).then_inc(S["update_done"], 1)
                pe.wait_ge(S["att_ready"], t + 1)
                if t >= 2:
                    pe.wait_ge(S["out_copied"], t - 1)
                for h in range(H):
                    pe.matmul(ps[:r, 6 + t % 2, h * HD:(h + 1) * HD], att[:r, t % 2, h, 0:r],
                              M["BVG"][:r, t, h * HD:(h + 1) * HD], start=(h == 0), stop=False, skip_group_check=True)
                if t < PT_TILES:
                    for j in range(2):
                        c = 2 * t + j
                        if c >= 1:
                            pe.wait_ge(S["state_new"], c)
                        else:
                            pe.wait_ge(S["cleared"], 1)
                        mm = pe.matmul(ps[j * CHUNK:(j + 1) * CHUNK, 6 + t % 2, 0:W4], qi[:, c * CHUNK:(c + 1) * CHUNK],
                                       state[:, c, :], start=False, stop=True, skip_group_check=True)
                else:
                    pe.wait_ge(S["s_query_ready"], 1)
                    pe.wait_ge(S["states"], 16 * H)
                    for s in range(DEC_BATCH):
                        mm = pe.matmul(ps[:NS, 6 + t % 2, 0:W4], s_qi[:, s, :], s_state[:, s, :], start=False,
                                       stop=(s == DEC_BATCH - 1), skip_group_check=True)
                mm.then_inc(S["out_done"], 1)
            pe.wait_ge(S["s_keys_ready"], 1)
            pe.wait_ge(S["state_new"], NCH)
            for s in range(DEC_BATCH):
                if s >= 2:
                    pe.wait_ge(S["s_state_new"], s - 1)
                pe.matmul(ps[:, 4 + s % 2, 0:W4], s_kd[:, s, :], M["BVG"][:NS, PT_TILES, 0:W4], start=True,
                          stop=True).then_inc(S["s_update_done"], 1)
            head_tensor(pe, E, S, hB, 2)


def rotary(nc, E, M, l, O, C):
    with stage(nc, "ro", "consts dve_step turned_q turned_k act_out dve_out stored rotated") as (S, sb, block):
        cos = sb("cos", [P, TILES, ROPE_HALF])
        sin = sb("sin", [P, TILES, ROPE_HALF])
        tmp = sb("tmp", [P, 4, TILES, 2 * H, ROPE_HALF])

        @block.sync
        def _(sp):
            sp.dma_start(cos[:], C["cos"]).then_inc(S["consts"], 16)
            sp.dma_start(sin[:], C["sin"]).then_inc(S["consts"], 16)
            sp.wait_ge(S["rotated"], 4)
            sp.dma_start(O["p_win_k"][bass.ds(l, 1)].rearrange("o b (t p) h d -> p (o b t) (h d)", p=P),
                         M["CQK"][:, 0:PT_TILES, W4:]).then_inc(S["stored"], 16)
            sp.dma_start(O["s_win_k"][bass.ds(l, 1)].rearrange("o b t h d -> (o b t) (h d)"),
                         M["CQK"][:NS, PT_TILES, W4:]).then_inc(S["stored"], 16)
            sp.wait_ge(S["stored"], 32)

        @block.vector
        def _(dve):
            step = stepper(dve, S["dve_step"])
            dve.wait_ge(S["consts"], 32)
            for rs, ts in PARTS:
                for t in range(ts.start, ts.stop):
                    v = M["CQK"][rs, t, :].rearrange("p (h d) -> p h d", h=2 * H)
                    shape = [rs.stop, 2 * H, ROPE_HALF]
                    x1, x2 = v[:, :, 0:ROPE_HALF], v[:, :, ROPE_HALF:2 * ROPE_HALF]
                    for k, (x, f) in enumerate(((x1, cos), (x2, sin), (x1, sin), (x2, cos))):
                        ins = dve.tensor_tensor(tmp[rs, k, t], x, f[rs, t, :].unsqueeze(1).to_broadcast(shape), ALU.mult)
                        if k == 3:
                            step(ins)
                        else:
                            ins.then_inc(S["dve_out"], 1)
            dve.wait_ge(S["dve_out"], 3 * TILES)
            for rs, ts in PARTS:
                for a, b, o, op in ((0, 1, 0, ALU.subtract), (2, 3, ROPE_HALF, ALU.add)):
                    v = M["CQK"][rs, ts, :].rearrange("p t (h d) -> p t h d", h=2 * H)[:, :, :, o:o + ROPE_HALF]
                    dve.tensor_tensor(v, tmp[rs, a, ts], tmp[rs, b, ts], op).then_inc(S["rotated"], 1)
            for n in range(2 * TILES):
                t, pair = n // 2, n % 2
                dve.wait_ge(S["turned_k"], n + 1)
                dve.tensor_copy(M["CKT"][:, pair, tok(t)], E["ps"][:, 2 + n % 2, 0:ROWS[t]]).then_inc(S["dve_out"], 1)

        @block.scalar
        def _(act):
            for n in range(2 * TILES):
                t, pair = n // 2, n % 2
                act.wait_ge(S["turned_q"], n + 1)
                act.activation(M["CQT"][:, pair, tok(t)], E["ps"][:, n % 2, 0:ROWS[t]], ACT.Copy,
                               scale=QK_SCALE).then_inc(S["act_out"], 1)

        @block.tensor
        def _(pe):
            pe.wait_ge(S["rotated"], 4)
            for n in range(2 * TILES):
                t, pair = n // 2, n % 2
                r = ROWS[t]
                if n >= 2:
                    pe.wait_ge(S["act_out"], n - 1)
                    pe.wait_ge(S["dve_out"], 3 * TILES + n - 1)
                pe.transpose(E["ps"][:, n % 2, 0:r], M["CQK"][:r, t, pair * P:(pair + 1) * P],
                             E["ident"][:r, :r]).then_inc(S["turned_q"], 1)
                pe.transpose(E["ps"][:, 2 + n % 2, 0:r], M["CQK"][:r, t, W4 + pair * P:W4 + (pair + 1) * P],
                             E["ident"][:r, :r]).then_inc(S["turned_k"], 1)


def prompt_attention(nc, E, M, l, kind, qT, kT, v, chunk, I, C):
    sems = ("consts scores_done z_ready maxima negated sums_done inverse act_step dve_step scanned a_ready "
            "turned pt_act pt_dve out_done out_copied")
    window = kind == "window"
    with stage(nc, "pw" if window else "pd", sems) as (S, sb, block):
        ps = E["ps"]
        mask = sb("mask", [P, SEQ if window else P])
        z = sb("z", [P, H, SEQ])
        f = sb("f", [P, H, SEQ])
        ones = sb("ones", [P, SEQ])
        mx = sb("mx", [P, H])
        total = sb("total", [P, H])
        bias = sb("bias", [P, H])
        pT = sb("pT", [P, 2, SEQ])
        n_in = 1 if window else 2

        @block.sync
        def _(sp):
            sp.dma_start(mask[:], C["win_mask" if window else "strict_mask"]).then_inc(S["consts"], 16)
            if not window:
                sp.dma_start(bias[:], layer_row(I["b_sb"], l)).then_inc(S["consts"], 16)

        @block.tensor
        def _(pe):
            for i in range(PT_TILES):
                w = (i + 1) * P
                if i > 0:
                    pe.wait_ge(S["z_ready"], i)
                for h in range(H):
                    o = (h % 2) * HD
                    mm = pe.matmul(ps[:, h, 0:w], qT[o:o + HD, h // 2, i * P:(i + 1) * P],
                                   kT[o:o + HD, h // 2, 0:w], start=True, stop=True)
                mm.then_inc(S["scores_done"], 1)
                pe.wait_ge(S["a_ready"], i + 1)

                def turn(h):
                    n = H * i + h
                    if n >= 2:
                        pe.wait_ge(S["pt_act"] if h % 2 == 0 else S["pt_dve"], (n - 2) // 2 + 1)
                    for c in range(i + 1):
                        mm = pe.transpose(ps[:, 4 + h % 2, c * P:(c + 1) * P], z[:, h, c * P:(c + 1) * P], E["ident"][:])
                    mm.then_inc(S["turned"], 1)

                turn(0)
                for h in range(H):
                    if h + 1 < H:
                        turn(h + 1)
                    n = H * i + h
                    pe.wait_ge(S["pt_act"] if h % 2 == 0 else S["pt_dve"], n // 2 + 1)
                    if h % 2 == 0 and i > 0:
                        pe.wait_ge(S["out_copied"], 2 * (i - 1) + h // 2 + 1)
                    o = (h % 2) * HD
                    for c in range(i + 1):
                        mm = pe.matmul(ps[o:o + HD, 6 + h // 2, 0:P], v[:, c, h * HD:(h + 1) * HD],
                                       pT[:, h % 2, c * P:(c + 1) * P], start=(c == 0), stop=(c == i))
                    mm.then_inc(S["out_done"], 1)

        @block.vector
        def _(dve):
            step = stepper(dve, S["dve_step"])
            dve.memset(ones[:], 1.0).then_inc(S["inverse"], 1)
            dve.wait_ge(S["consts"], 16 * n_in)
            for i in range(PT_TILES):
                w = (i + 1) * P
                dve.wait_ge(S["scores_done"], i + 1)
                if i > 0:
                    dve.wait_ge(S["turned"], H * i)
                if window:
                    dve.tensor_tensor(z[:, :, 0:w], ps[:, 0:H, 0:w],
                                      mask[:, SEQ - w:SEQ].unsqueeze(1).to_broadcast([P, H, w]), ALU.add).then_inc(S["z_ready"], 1)
                    dve.wait_ge(S["z_ready"], i + 1)
                    step(dve.tensor_reduce(mx[:], z[:, :, 0:w], AX.X, ALU.max))
                    dve.tensor_scalar(mx[:], mx[:], -1.0, None, ALU.mult).then_inc(S["negated"], 1)
                    dve.wait_ge(S["sums_done"], H * (i + 1))
                    step(dve.reciprocal(total[:], total[:]))
                    dve.tensor_tensor(z[:, :, 0:w], z[:, :, 0:w], total[:].unsqueeze(2).to_broadcast([P, H, w]),
                                      ALU.mult).then_inc(S["a_ready"], 1)
                else:
                    dve.tensor_tensor(z[:, :, 0:w], ps[:, 0:H, 0:w], bias[:, 0:H].unsqueeze(2).to_broadcast([P, H, w]),
                                      ALU.add).then_inc(S["z_ready"], 1)
                    dve.wait_ge(S["z_ready"], i + 1)
                    dve.tensor_tensor(z[:, :, w - P:w], z[:, :, w - P:w], mask[:].unsqueeze(1).to_broadcast([P, H, P]),
                                      ALU.add).then_inc(S["maxima"], 1)
                    dve.wait_ge(S["maxima"], i + 1)
                    dve.wait_ge(S["act_step"], 3 * (i + 1))
                    step(dve.scalar_tensor_tensor(f[:, :, 0:w], z[:, :, 0:w], 0.0, f[:, :, 0:w], ALU.max, ALU.add))
                    for h in range(H):
                        step(dve.tensor_tensor_scan(f[:, h, 0:w][:, ::-1], ones[:, 0:w], f[:, h, 0:w][:, ::-1], 0.0,
                                                    ALU.mult, ALU.add))
                    dve.tensor_tensor(z[:, :, 0:w], z[:, :, 0:w], f[:, :, 0:w], ALU.subtract).then_inc(S["scanned"], 1)
                for h in range(1, H, 2):
                    n = H * i + h
                    dve.wait_ge(S["turned"], n + 1)
                    if n >= 2:
                        dve.wait_ge(S["out_done"], n - 1)
                    dve.tensor_copy(pT[:, 1, 0:w], ps[:, 5, 0:w]).then_inc(S["pt_dve"], 1)

        @block.scalar
        def _(act):
            for i in range(PT_TILES):
                w = (i + 1) * P
                if window:
                    act.wait_ge(S["negated"], i + 1)
                    for h in range(H):
                        act.activation(z[:, h, 0:w], z[:, h, 0:w], ACT.Exp, bias=mx[:, h:h + 1],
                                       accum_out=total[:, h:h + 1]).then_inc(S["sums_done"], 1)
                else:
                    act.wait_ge(S["maxima"], i + 1)
                    act.activation(f[:, :, 0:w], z[:, :, 0:w], ACT.Abs).then_inc(S["act_step"], 1)
                    act.wait_ge(S["act_step"], 3 * i + 1)
                    act.activation(f[:, :, 0:w], f[:, :, 0:w], ACT.Exp, scale=-1.0).then_inc(S["act_step"], 1)
                    act.wait_ge(S["act_step"], 3 * i + 2)
                    act.activation(f[:, :, 0:w], f[:, :, 0:w], ACT.Ln, bias=1.0).then_inc(S["act_step"], 1)
                    act.wait_ge(S["scanned"], i + 1)
                    act.activation(z[:, :, 0:w], z[:, :, 0:w], ACT.Exp).then_inc(S["a_ready"], 1)
                for h in range(0, H, 2):
                    n = H * i + h
                    act.wait_ge(S["turned"], n + 1)
                    if n >= 2:
                        act.wait_ge(S["out_done"], n - 1)
                    act.activation(pT[:, 0, 0:w], ps[:, 4, 0:w], ACT.Copy).then_inc(S["pt_act"], 1)
                for pair in range(2):
                    act.wait_ge(S["out_done"], H * i + 2 * pair + 2)
                    act.activation(M["mixT"][:, chunk + pair, i * P:(i + 1) * P], ps[:, 6 + pair, 0:P],
                                   ACT.Copy).then_inc(S["out_copied"], 1)


def sample_attention(nc, E, M, l, kind, qT, kT, v_new, chunk, I, C):
    window = kind == "window"
    NTL = WIN_TILES if window else N_PAGES
    UT = 4
    chunks = [(c, min(UT, NTL - c)) for c in range(0, NTL, UT)]
    NC = len(chunks)
    KEYS = NTL * P
    units = [(k, j) for k in range(NC) for j in range(SG)]
    SLOTS = 4
    name = "sw" if window else "sd"
    cache_k, cache_v = (I["cache_win_k"], I["cache_win_v"]) if window else (I["cache_sb_k"], I["cache_sb_v"])
    sems = ("consts bias_loaded k0 k1 k2 k3 v0 v1 v2 v3 spread q_ready bias_turned bias_ready turned kt_act kt_dve "
            "scores_done z_ready dve_step act_step negated scanned a_ready pt_turned pt_act pt_dve out_units out_done "
            "rows_ready gathered out_copied")
    with nc.Fori(0, GROUPS) as g:
        with stage(nc, name, sems) as (S, sb, block):
            ps = E["ps"]
            ksem, vsem = (S["k0"], S["k1"], S["k2"], S["k3"]), (S["v0"], S["v1"], S["v2"], S["v3"])
            kn = sb("kn", [P, SLOTS, UT, W4])
            vn = sb("vn", [P, SLOTS, UT, W4])
            kt = sb("kt", [P, 2, 2, UT * P])
            z = sb("z", [P, KEYS + NS])
            f = sb("f", [P, KEYS + NS])
            ones = sb("ones", [P, KEYS + NS])
            pT = sb("pT", [P, 2, UT * P])
            new_mask = sb("new_mask", [P, GROUPS, NS])
            head_cols = sb("head_cols", [P, W4])
            gather = sb("gather", [P, SG * DEC_SEQ])
            pair_head = sb("pair_head", [P, 2, H])
            bias_rows = sb("bias_rows", [H, P])
            b = sb("b", [H, 1])
            bcol = sb("bcol", [P, 1])
            qb = sb("qb", [P, 2, SG, H, DEC_SEQ])
            mx = sb("mx", [P, 1])
            total = sb("total", [P, 1])
            rows = sb("rows", [P, W4])
            n_const = (4 if window else 4) + 1

            def load_window(eng, cache, buf, sems_, u):
                k, j = units[u]
                c0, n = chunks[k]
                rows_ = cache[bass.ds(l, 1), bass.ds(SG * g + j, 1)].rearrange("o r n h d -> (o r n) (h d)")
                for i, t in enumerate(range(c0, c0 + n)):
                    if t < FAR_TILES:
                        src = rows_[t * 2 * P:(t + 1) * 2 * P, :].rearrange("(a b) x -> a b x", b=16)[:, 0:8, :]
                    else:
                        r0 = PAST_LEN - NEAR + (t - FAR_TILES) * P
                        src = rows_[r0:r0 + P, :]
                    eng.dma_start(buf[:, u % SLOTS, i, :], src).then_inc(sems_[u % SLOTS], 16)

            def load_pages(eng, cache, buf, sems_, k, j, room=None):
                _, pages = nc.values_load_multi_w_load_instructions(
                    E["pages"][0:1, bass.ds(SG * N_PAGES * g + j * N_PAGES + UT * k, UT)], engines=(eng.engine,),
                    min_val=0, max_val=N_POOL - 1,
                    skip_runtime_bounds_check_because="the page table numbers pages of the pool")
                if room is not None:
                    eng.wait_ge(*room)
                for i, page in enumerate(pages):
                    src = cache[bass.ds(l, 1), bass.ds(page, 1)].rearrange("o q n h d -> (o q n) (h d)")
                    eng.dma_start(buf[:, j, i, :], src).then_inc(sems_[j], 16)

            def arrived(eng, sems_, u):
                total_ = sum(chunks[units[x][0]][1] for x in range(u % SLOTS, u + 1, SLOTS))
                eng.wait_ge(sems_[u % SLOTS], 16 * total_)

            @block.sync
            def _(sp):
                sp.dma_start(new_mask[:], C["s_win_new" if window else "s_sb_new"]).then_inc(S["consts"], 16)
                sp.dma_start(head_cols[:], C["head_cols"]).then_inc(S["consts"], 16)
                sp.dma_start(gather[:], C["gather_rows"]).then_inc(S["consts"], 16)
                sp.dma_start(pair_head[:], C["pair_head"]).then_inc(S["consts"], 16)
                if window:
                    sp.dma_start(ones[:, 0:KEYS], C["s_win_mask"]).then_inc(S["consts"], 16)
                else:
                    sp.dma_start(bias_rows[:], C["bias_rows"]).then_inc(S["consts"], 16)
                    sp.dma_start(b[:], layer_col(I["b_sb"], l)).then_inc(S["bias_loaded"], 16)
                if window:
                    for u in range(len(units)):
                        if u >= SLOTS:
                            sp.wait_ge(S["turned"], u - SLOTS + 1)
                        load_window(sp, cache_k, kn, ksem, u)
                        if SLOTS <= u < 2 * SLOTS:
                            load_window(sp, cache_v, vn, vsem, u - SLOTS)
                    for u in range(SLOTS, len(units)):
                        sp.wait_ge(S["out_units"], u - SLOTS + 1)
                        load_window(sp, cache_v, vn, vsem, u)
                else:
                    for j in range(SG):
                        load_pages(sp, cache_k, kn, ksem, 0, j)
                    for j in range(SG):
                        load_pages(sp, cache_v, vn, vsem, 0, j)
                    with sp.Fori(1, NC) as k:
                        for j in range(SG):
                            load_pages(sp, cache_k, kn, ksem, k, j, (S["turned"], SG * k + (j - SLOTS + 1)))
                    with sp.Fori(1, NC) as k:
                        for j in range(SG):
                            load_pages(sp, cache_v, vn, vsem, k, j, (S["out_units"], SG * k + (j - SLOTS + 1)))

            @block.tensor
            def _(pe):
                if not window:
                    pe.wait_ge(S["consts"], 16 * n_const)
                    pe.wait_ge(S["bias_loaded"], 16)
                    pe.matmul(ps[:, 6, 0:1], bias_rows[:], b[:], start=True, stop=True).then_inc(S["bias_turned"], 1)

                def turn(u):
                    k, j = units[u]
                    arrived(pe, ksem, u)
                    if u >= 2:
                        pe.wait_ge(S["kt_act"], u - 1)
                        pe.wait_ge(S["kt_dve"], u - 1)
                    for pair in range(2):
                        for i in range(chunks[k][1]):
                            mm = pe.transpose(ps[:, 2 * (u % 2) + pair, i * P:(i + 1) * P],
                                              kn[:, u % SLOTS, i, pair * P:(pair + 1) * P], E["ident"][:])
                    mm.then_inc(S["turned"], 1)

                def scores(u):
                    k, j = units[u]
                    w = chunks[k][1] * P
                    pe.wait_ge(S["kt_act"], u + 1)
                    pe.wait_ge(S["kt_dve"], u + 1)
                    if j == 0 and k >= 2:
                        pe.wait_ge(S["z_ready"], k - 1)
                    for pair in range(2):
                        mm = pe.matmul(ps[32 * j:32 * j + 32, 4 + k % 2, 0:w],
                                       qb[:, pair, j].rearrange("p h q -> p (h q)"), kt[:, u % 2, pair, 0:w],
                                       start=(pair == 0), stop=(pair == 1), tile_position=(0, 32 * j))
                    mm.then_inc(S["scores_done"], 1)

                turn(0)
                pe.wait_ge(S["q_ready"], 2)
                for u in range(len(units)):
                    if u + 1 < len(units):
                        turn(u + 1)
                    scores(u)
                pe.wait_ge(S["z_ready"], NC - 1 if NC >= 2 else 1)
                for j in range(SG):
                    for pair in range(2):
                        mm = pe.matmul(ps[32 * j:32 * j + 32, 4 + NC % 2, 0:NS],
                                       qb[:, pair, j].rearrange("p h q -> p (h q)"), kT[:, pair, SEQ:NT],
                                       start=(pair == 0), stop=(pair == 1), tile_position=(0, 32 * j))
                mm.then_inc(S["scores_done"], 1)
                pe.wait_ge(S["a_ready"], 1)

                def turn_p(k):
                    c0, n = chunks[k] if k < NC else (NTL, 1)
                    if k >= 2:
                        pe.wait_ge(S["pt_act"] if k % 2 == 0 else S["pt_dve"], (k - 2) // 2 + 1)
                    for i in range(n):
                        cs = slice((c0 + i) * P, (c0 + i) * P + (P if k < NC else NS))
                        mm = pe.transpose(ps[:cs.stop - cs.start, k % 2, i * P:(i + 1) * P], z[:, cs], E["ident"][:])
                    mm.then_inc(S["pt_turned"], 1)

                turn_p(0)
                for k in range(NC):
                    turn_p(k + 1)
                    pe.wait_ge(S["pt_act"] if k % 2 == 0 else S["pt_dve"], k // 2 + 1)
                    for j in range(SG):
                        u = SG * k + j
                        arrived(pe, vsem, u)
                        for i in range(chunks[k][1]):
                            mm = pe.matmul(ps[32 * j:32 * j + 32, 6, 0:W4],
                                           pT[:, k % 2, i * P + 32 * j:i * P + 32 * j + 32], vn[:, u % SLOTS, i, :],
                                           start=(k == 0 and i == 0), stop=False, skip_group_check=True,
                                           tile_position=(0, 32 * j))
                        mm.then_inc(S["out_units"], 1)
                pe.wait_ge(S["pt_act"] if NC % 2 == 0 else S["pt_dve"], NC // 2 + 1)
                pe.matmul(ps[:, 6, 0:W4], pT[:NS, NC % 2, 0:P], v_new, start=False, stop=True,
                          skip_group_check=True).then_inc(S["out_done"], 1)
                pe.wait_ge(S["rows_ready"], 1)
                for pair in range(2):
                    mm = pe.matmul(ps[:, 7, pair * 32:pair * 32 + 32], rows[:, pair * P:(pair + 1) * P], gather[:],
                                   start=True, stop=True)
                mm.then_inc(S["gathered"], 1)

            @block.scalar
            def _(act):
                for u, (k, j) in enumerate(units):
                    w = chunks[k][1] * P
                    act.wait_ge(S["turned"], u + 1)
                    if u >= 2:
                        act.wait_ge(S["scores_done"], u - 1)
                    act.activation(kt[:, u % 2, 0, 0:w], ps[:, 2 * (u % 2), 0:w], ACT.Copy).then_inc(S["kt_act"], 1)
                if window:
                    act.wait_ge(S["negated"], 1)
                    act.activation(z[:], z[:], ACT.Exp, bias=mx[:, 0:1], accum_out=total[:]).then_inc(S["a_ready"], 1)
                else:
                    act.wait_ge(S["z_ready"], NC + 1)
                    act.activation(f[:], z[:], ACT.Abs).then_inc(S["act_step"], 1)
                    act.wait_ge(S["act_step"], 1)
                    act.activation(f[:], f[:], ACT.Exp, scale=-1.0).then_inc(S["act_step"], 1)
                    act.wait_ge(S["act_step"], 2)
                    act.activation(f[:], f[:], ACT.Ln, bias=1.0).then_inc(S["act_step"], 1)
                    act.wait_ge(S["scanned"], 1)
                    act.activation(z[:], z[:], ACT.Exp).then_inc(S["a_ready"], 1)
                for k in range(0, NC + 1, 2):
                    w, r = (chunks[k][1] * P, P) if k < NC else (P, NS)
                    act.wait_ge(S["pt_turned"], k + 1)
                    if k >= 2:
                        act.wait_ge(S["out_units"], SG * (k - 1))
                    act.activation(pT[:r, 0, 0:w], ps[:r, 0, 0:w], ACT.Copy).then_inc(S["pt_act"], 1)
                act.wait_ge(S["gathered"], 1)
                act.activation(M["mixT"][:, chunk:chunk + 2, bass.ds(SEQ + 32 * g, 32)],
                               ps[:, 7, 0:64].rearrange("p (k t) -> p k t", k=2), ACT.Copy).then_inc(S["out_copied"], 1)

            @block.vector
            def _(dve):
                step = stepper(dve, S["dve_step"])
                dve.wait_ge(S["consts"], 16 * n_const)
                for pair in range(2):
                    qv = qT[:, pair, bass.ds(SEQ + 32 * g, 32)].rearrange("p (s q) -> p s q", q=DEC_SEQ)
                    for h in range(H):
                        ins = dve.tensor_scalar(qb[:, pair, :, h, :], qv, pair_head[:, pair, h:h + 1], None, ALU.mult)
                        if h == H - 1:
                            ins.then_inc(S["q_ready"], 1)
                        else:
                            ins.then_inc(S["spread"], 1)
                dve.wait_ge(S["spread"], 2 * (H - 1))
                dve.wait_ge(S["q_ready"], 2)
                if not window:
                    step(dve.memset(ones[:], 1.0))
                    dve.wait_ge(S["bias_turned"], 1)
                    dve.tensor_copy(bcol[:], ps[:, 6, 0:1]).then_inc(S["bias_ready"], 1)
                    dve.wait_ge(S["bias_ready"], 1)

                def take(k):
                    dve.wait_ge(S["scores_done"], SG * (k + 1) if k < NC else SG * NC + 1)
                    if k == NC:
                        src = ps[:, 4 + NC % 2, 0:NS]
                        mk = new_mask[:, bass.ds(g, 1), :].rearrange("p o n -> p (o n)")
                        if window:
                            ins = dve.tensor_tensor(z[:, KEYS:], src, mk, ALU.add)
                        else:
                            ins = dve.scalar_tensor_tensor(z[:, KEYS:], src, bcol[:, 0:1], mk, ALU.add, ALU.add)
                    else:
                        cs = slice(chunks[k][0] * P, (chunks[k][0] + chunks[k][1]) * P)
                        src = ps[:, 4 + k % 2, 0:cs.stop - cs.start]
                        if window:
                            ins = dve.tensor_tensor(z[:, cs], src, ones[:, cs], ALU.add)
                        else:
                            ins = dve.tensor_scalar(z[:, cs], src, bcol[:, 0:1], None, ALU.add)
                    ins.then_inc(S["z_ready"], 1)

                for u, (k, j) in enumerate(units):
                    w = chunks[k][1] * P
                    dve.wait_ge(S["turned"], u + 1)
                    if u >= 2:
                        dve.wait_ge(S["scores_done"], u - 1)
                    dve.tensor_copy(kt[:, u % 2, 1, 0:w], ps[:, 2 * (u % 2) + 1, 0:w]).then_inc(S["kt_dve"], 1)
                    if j == 1 and k >= 1:
                        take(k - 1)
                take(NC - 1)
                take(NC)
                dve.wait_ge(S["z_ready"], NC + 1)
                if window:
                    step(dve.tensor_reduce(mx[:], z[:], AX.X, ALU.max))
                    dve.tensor_scalar(mx[:], mx[:], -1.0, None, ALU.mult).then_inc(S["negated"], 1)
                else:
                    dve.wait_ge(S["act_step"], 3)
                    step(dve.scalar_tensor_tensor(f[:], z[:], 0.0, f[:], ALU.max, ALU.add))
                    step(dve.tensor_tensor_scan(f[:, ::-1], ones[:], f[:, ::-1], 0.0, ALU.mult, ALU.add))
                    dve.tensor_tensor(z[:], z[:], f[:], ALU.subtract).then_inc(S["scanned"], 1)
                for k in range(1, NC + 1, 2):
                    w, r = (chunks[k][1] * P, P) if k < NC else (P, NS)
                    dve.wait_ge(S["pt_turned"], k + 1)
                    if k >= 2:
                        dve.wait_ge(S["out_units"], SG * (k - 1))
                    dve.tensor_copy(pT[:r, 1, 0:w], ps[:r, 1, 0:w]).then_inc(S["pt_dve"], 1)
                dve.wait_ge(S["out_done"], 1)
                if window:
                    dve.wait_ge(S["a_ready"], 1)
                    step(dve.reciprocal(total[:], total[:]))
                    dve.scalar_tensor_tensor(rows[:], ps[:, 6, 0:W4], total[:, 0:1], head_cols[:], ALU.mult,
                                             ALU.mult).then_inc(S["rows_ready"], 1)
                else:
                    dve.tensor_tensor(rows[:], ps[:, 6, 0:W4], head_cols[:], ALU.mult).then_inc(S["rows_ready"], 1)


def output(nc, E, M, l, I):
    with stage(nc, "ou", POST_SEMS + WEIGHT_SEMS + "mix_hi mix_lo") as (S, sb, block):
        W = weight_buffers(sb)
        hi = sb("mix_hi", [P, KC, NT], F32R)
        lo = sb("mix_lo", [P, KC, NT], F32R)
        gain = sb("gain", [P, D_MODEL])
        rms = sb("rms", [P, TILES])
        inv = sb("inv", [P, TILES])
        y = M["TR"][:].rearrange("p m n -> p (m n)")[:, 0:2 * TILES * 512].rearrange("p (h n) -> p h n", h=2)
        y_scratch = W["raw"][:, 0, 0:D_MODEL]

        @block.sync
        def _(sp):
            sp.dma_start(gain[:], layer_row(I["g_mix_post"], l)).then_inc(S["post_gain_loaded"], 16)
            post_sync(sp, S, W, I["w_out"], l, KC, 0)

        @block.tensor
        def _(pe):
            pe.wait_ge(S["mix_lo"], KC)
            post_tensor(pe, E, S, W, hi, lo, KC, 0)

        @block.scalar
        def _(act):
            split_scalar(act, S, W, 0, 0, 0, False)
            split_scalar(act, S, W, 1, 1, 0, False)
            for c in range(KC):
                act.activation(hi[:, c], M["mixT"][:, c], ACT.Copy).then_inc(S["mix_hi"], 1)
            post_scalar(act, E, S, W, y, y_scratch, rms, KC, 0, 1.0)

        @block.vector
        def _(dve):
            split_vector(dve, S, W, 0, 0)
            split_vector(dve, S, W, 1, 1)
            for c in range(KC):
                dve.wait_ge(S["mix_hi"], c + 1)
                dve.tensor_tensor(lo[:, c], M["mixT"][:, c], hi[:, c].bitcast(F32), ALU.subtract).then_inc(S["mix_lo"], 1)
            post_vector(dve, E, S, W, y, gain, rms, inv, KC, 0)


def mixing(nc, E, l, I, O, C):
    with ExitStack() as ctx:
        def sb(n, shape, dt=F32):
            return ctx.enter_context(nc.sbuf_tensor(n, shape, dt))

        M = dict(
            TR=sb("TR", [P, 10, NT]), gates=sb("gates", [GATE_ROWS, NT]),
            KA=sb("KA", [P, TILES, W4]), VA=sb("VA", [P, TILES, H, HD + 1]), AO=sb("AO", [P, TILES, W4]),
            CV=sb("CV", [P, TILES, W4]), BVG=sb("BVG", [P, TILES, 2 * W4]), CQK=sb("CQK", [P, TILES, 2 * W4]),
            DKV=sb("DKV", [P, TILES, 2 * W4]))
        M["CQT"], M["CKT"] = M["TR"][:, AQ:AQ + 2, :], M["TR"][:, AK:AK + 2, :]
        project(nc, E, M, l, I["g_mix_pre"], I["w_in"], O)
        M["mixT"] = sb("mixT", [P, KC, NT])
        mlstm(nc, E, M, l, I, O, C)
        gla(nc, E, M, l, I, O, C)
        rotary(nc, E, M, l, O, C)
        DQT, DKT = M["TR"][:, DQ:DQ + 2, :], M["TR"][:, DK:DK + 2, :]
        prompt_attention(nc, E, M, l, "window", M["CQT"], M["CKT"], M["CV"], 4, I, C)
        prompt_attention(nc, E, M, l, "stick", DQT, DKT, M["DKV"][:, :, W4:], 6, I, C)
        sample_attention(nc, E, M, l, "window", M["CQT"], M["CKT"], M["CV"][:NS, PT_TILES, :], 4, I, C)
        sample_attention(nc, E, M, l, "stick", DQT, DKT, M["DKV"][:NS, PT_TILES, W4:], 6, I, C)
        output(nc, E, M, l, I)



def program(nc, I, O, C):
    with ExitStack() as ctx:
        def sb(n, shape, dt=F32):
            return ctx.enter_context(nc.sbuf_tensor(n, shape, dt))

        E = dict(
            x=sb("x", [P, TILES, D_MODEL]),
            ident=sb("ident", [P, P]), sumsq=sb("sumsq", [P, TILES]), eps=sb("eps", [P, 2]),
            pages=sb("pages", [1, DEC_BATCH * N_PAGES], I32),
            ps=ctx.enter_context(nc.psum_tensor("ps", [P, 8, 512], F32)))

        with stage(nc, "start", "loaded") as (S, _sb, block):
            @block.sync
            def _(sp):
                sp.dma_start(E["x"][:, 0:PT_TILES, :], I["x_prompt"].rearrange("b (t p) n -> p (b t) n", p=P)).then_inc(S["loaded"], 16)
                sp.dma_start(E["x"][:NS, PT_TILES, :], I["x_sample"].rearrange("b t n -> (b t) n")).then_inc(S["loaded"], 16)
                sp.dma_start(E["ident"][:], C["ident"]).then_inc(S["loaded"], 16)
                sp.dma_start(E["pages"][:], I["page_table"].rearrange("(o b) n -> o (b n)", o=1)).then_inc(S["loaded"], 16)
                sp.wait_ge(S["loaded"], 64)

            @block.vector
            def _(dve):
                dve.memset(E["sumsq"][:], 0.0)
                dve.memset(E["eps"][:, 0:1], EPS)
                dve.memset(E["eps"][:, 1:2], 4 * EPS)

        with nc.Fori(0, DEPTH) as l:
            ffn(nc, E, l, "f1", I["g_ffn1_pre"], I["w_ffn1_in"], I["w_ffn1_out"], I["g_ffn1_post"])
            mixing(nc, E, l, I, O, C)
            ffn(nc, E, l, "f2", I["g_ffn2_pre"], I["w_ffn2_in"], I["w_ffn2_out"], I["g_ffn2_post"])

        with stage(nc, "end", "stored") as (S, _sb, block):
            @block.sync
            def _(sp):
                sp.dma_start(O["y_prompt"].rearrange("b (t p) n -> p (b t) n", p=P), E["x"][:, 0:PT_TILES, :]).then_inc(S["stored"], 16)
                sp.dma_start(O["y_sample"].rearrange("b t n -> (b t) n"), E["x"][:NS, PT_TILES, :]).then_inc(S["stored"], 16)
                sp.wait_ge(S["stored"], 32)


INPUTS = ("x_prompt", "x_sample", "cache_sb_k", "cache_sb_v", "page_table", "cache_win_k", "cache_win_v",
          "state_mlstm_c", "state_mlstm_n", "state_mlstm_m", "state_gla_s",
          "g_ffn1_pre", "w_ffn1_in", "w_ffn1_out", "g_ffn1_post", "g_mix_pre", "w_in", "b_ig", "b_fg",
          "g_head_a", "w_gla_a2", "b_gla_a", "g_head_b", "b_sb", "w_out", "g_mix_post",
          "g_ffn2_pre", "w_ffn2_in", "w_ffn2_out", "g_ffn2_post")
OUTPUTS = {
    "y_prompt": (1, SEQ, D_MODEL), "y_sample": (DEC_BATCH, DEC_SEQ, D_MODEL),
    "p_sb_k": (DEPTH, 1, SEQ, H, HD), "p_sb_v": (DEPTH, 1, SEQ, H, HD),
    "p_win_k": (DEPTH, 1, SEQ, H, HD), "p_win_v": (DEPTH, 1, SEQ, H, HD),
    "p_mlstm_c": (DEPTH, 1, H, HD, HD), "p_mlstm_n": (DEPTH, 1, H, HD), "p_mlstm_m": (DEPTH, 1, H),
    "p_gla_s": (DEPTH, 1, H, DK_B, HD),
    "s_sb_k": (DEPTH, DEC_BATCH, DEC_SEQ, H, HD), "s_sb_v": (DEPTH, DEC_BATCH, DEC_SEQ, H, HD),
    "s_win_k": (DEPTH, DEC_BATCH, DEC_SEQ, H, HD), "s_win_v": (DEPTH, DEC_BATCH, DEC_SEQ, H, HD),
    "s_mlstm_c": (DEPTH, DEC_BATCH, H, HD, HD), "s_mlstm_n": (DEPTH, DEC_BATCH, H, HD),
    "s_mlstm_m": (DEPTH, DEC_BATCH, H), "s_gla_s": (DEPTH, DEC_BATCH, H, DK_B, HD),
}


def kernel(**inputs):
    import concourse.bacc as _bacc
    from concourse.bass_utils import run_bass_kernel_spmd as _run

    nc = _bacc.Bacc("TRN2", target_bir_lowering=False, num_devices=1)
    arrays, I, O, C = {}, {}, {}, {}
    for name in INPUTS:
        a = np.ascontiguousarray(inputs[name])
        arrays[f"in_{name}"] = a
        I[name] = nc.dram_tensor(f"in_{name}", a.shape, mybir.dt.from_np(a.dtype), kind="ExternalInput").ap()
    for name, a in constants().items():
        arrays[f"const_{name}"] = a
        C[name] = nc.dram_tensor(f"const_{name}", a.shape, F32, kind="ExternalInput").ap()
    for name, shape in OUTPUTS.items():
        O[name] = nc.dram_tensor(f"out_{name}", shape, F32, kind="ExternalOutput").ap()
    program(nc, I, O, C)
    r = _run(nc, [arrays], core_ids=[0])
    return tuple(r.results[0][f"out_{name}"] for name in OUTPUTS)
```

```python
from contextlib import ExitStack, contextmanager

import numpy as np
import concourse.bass as bass
from concourse import mybir

ALU = mybir.AluOpType
ACT = mybir.ActivationFunctionType
AX = mybir.AxisListType
F32 = mybir.dt.float32
I32 = mybir.dt.int32
F32R = mybir.dt.float32r

D_MODEL = 1024
SEQ = 512
DEPTH = 2
DEC_BATCH = 8
DEC_SEQ = 8
PAST_LEN = 2048
PAGE = 128
N_PAGES = PAST_LEN // PAGE
N_POOL = DEC_BATCH * N_PAGES * 5 // 4
HD = 64
H = 4
DK_B = HD // 2
RANK = 16
TAU = 16.0
CHUNK = 64
D_FF = 2 * D_MODEL
EPS = 1e-6
ROPE_HALF = HD // 8
THETA = 500000.0
DILATIONS = ((128, 1), (512, 4), (2048, 16))
NEG = -1e30

P = 128
KC = D_MODEL // P
W4 = H * HD
NS = DEC_BATCH * DEC_SEQ
NT = SEQ + NS
PT_TILES = SEQ // P
TILES = PT_TILES + 1
ROWS = [P] * PT_TILES + [NS]
HALF = NT // 2
FF = D_FF // P

SIZES = (W4, W4, W4, H, H, W4, H * DK_B, H * DK_B, W4, W4, RANK, W4, W4, W4, W4, W4, W4)
NAMES = ("aq", "ak", "av", "ai", "af", "ao", "bq", "bk", "bv", "bg", "blr", "cq", "ck", "cv", "dq", "dk", "dv")
COL = {n: sum(SIZES[:i]) for i, n in enumerate(NAMES)}
N_IN = sum(SIZES)

NEAR = DILATIONS[1][0]
FAR_TILES = (PAST_LEN - NEAR) // (2 * P)
WIN_TILES = FAR_TILES + NEAR // P
UT = 4
SG = 4
GROUPS = DEC_BATCH // SG


def tok(t):
    return slice(t * P, t * P + ROWS[t])


PARTS = ((slice(0, P), slice(0, PT_TILES)), (slice(0, NS), slice(PT_TILES, TILES)))


def constants():
    f = np.float32
    c = {}
    c["ident"] = np.eye(P, dtype=f)
    p = np.arange(P)
    u = np.arange(SEQ)

    def log_count(delta):
        n = sum(((delta >= 0) & (delta <= w) & (delta % d == 0)).astype(np.int64) for w, d in DILATIONS)
        return np.where(n > 0, np.log(np.maximum(n, 1)), NEG).astype(f)

    c["win_mask"] = log_count(p[:, None] + (SEQ - P) - u[None, :])
    c["strict_mask"] = np.where(p[:, None] > p[None, :], 0, NEG).astype(f)
    c["turned_mask"] = np.where(p[None, :] >= p[:, None], 0, NEG).astype(f)
    c["gla_mask"] = ((p[None, :] >= p[:, None]) & (p[None, :] // CHUNK == p[:, None] // CHUNK)).astype(f)
    s = np.arange(NS)
    same = s[:, None] // DEC_SEQ == s[None, :] // DEC_SEQ
    ok = same & (s[None, :] >= s[:, None])
    c["s_turned_mask"] = np.where(ok, 0, NEG).astype(f)
    c["s_gla_mask"] = ok.astype(f)
    rs, rh, rq = p // (H * DEC_SEQ), p // DEC_SEQ % H, p % DEC_SEQ
    row = np.zeros((P, WIN_TILES * P), f)
    for t in range(WIN_TILES):
        c0 = t // UT * UT
        nt = min(UT, WIN_TILES - c0)
        far = max(0, min(FAR_TILES - c0, nt))
        if t < FAR_TILES:
            pos = c0 * 2 * P + p // (8 // far) * 16 + p % (8 // far) * far + (t - c0)
        else:
            pos = PAST_LEN - NEAR + (c0 + far - FAR_TILES) * P + p * (nt - far) + (t - c0 - far)
        row[:, t * P:(t + 1) * P] = log_count(PAST_LEN + rq[:, None] - pos[None, :])
    c["s_win_mask"] = row
    g = np.arange(GROUPS)
    mine = (g[:, None, None] * SG + rs[None, :, None]) == (s // DEC_SEQ)[None, None, :]
    delta = (rq[:, None] - (s % DEC_SEQ)[None, :])[None]
    c["s_win_new"] = np.where(mine, log_count(delta), NEG).astype(f).transpose(1, 0, 2).copy()
    c["s_sb_new"] = np.where(mine & (delta > 0), 0, NEG).astype(f).transpose(1, 0, 2).copy()
    c["head_cols"] = np.repeat((rh[:, None] == np.arange(H)[None, :]), HD, axis=1).astype(f)
    c["gather_rows"] = ((rs * DEC_SEQ + rq)[:, None] == np.arange(SG * DEC_SEQ)[None, :]).astype(f)
    c["pair_head"] = np.stack([(np.arange(H)[None, :] == 2 * pr + (p // HD)[:, None]) for pr in range(2)],
                              1).astype(f)
    c["bias_rows"] = (np.arange(H)[:, None] == rh[None, :]).astype(f)
    c["head_rows"] = np.repeat(np.eye(H, dtype=f)[:, :, None], P, axis=2)
    first = (np.arange(NT) >= SEQ) & ((np.arange(NT) - SEQ) % DEC_SEQ == 0)
    c["keep_a"] = np.repeat(np.where(first, 0, 1)[None], H, 0).astype(f)
    c["cut_a"] = np.repeat(np.where(first, NEG, 0)[None], H, 0).astype(f)
    start = first | ((np.arange(NT) < SEQ) & (np.arange(NT) % CHUNK == 0))
    c["keep_b"] = np.repeat(np.where(start, 0, 1)[None], P, 0).astype(f)
    q = np.arange(DEC_BATCH // 2)
    req = 2 * q[None, :] + (p // HD)[:, None]
    c["pair_tokens"] = (req[:, :, None] == (s // DEC_SEQ)[None, None, :]).astype(f)
    c["pair_last"] = ((req.T[None] * DEC_SEQ + DEC_SEQ - 1) == s[:, None, None]).astype(f)
    c["token_request"] = ((s // DEC_SEQ)[:, None] == np.arange(DEC_BATCH)[None, :]).astype(f)
    c["request_tokens"] = np.repeat(c["token_request"].T[None], P, 0).copy()
    c["gla_head"] = ((p // DK_B)[:, None] == np.arange(H)[None, :]).astype(f)
    c["gla_cols"] = np.repeat(c["gla_head"], HD, axis=1)
    inv = np.float32(THETA) ** (-np.arange(ROPE_HALF, dtype=f) / np.float32(ROPE_HALF))
    pos = np.concatenate([np.arange(SEQ), PAST_LEN + np.arange(NS) % DEC_SEQ, np.zeros(P - NS)]).astype(f)
    ang = (pos[:, None] * inv[None, :].astype(f)).astype(f)
    for name, fn in (("cos", np.cos), ("sin", np.sin)):
        c[name] = fn(ang).astype(f).reshape(TILES, P, ROPE_HALF).transpose(1, 0, 2).copy()
    return c


RESIDENT = ("ident",)


@contextmanager
def stage(nc, name, sems):
    with ExitStack() as st:
        S = dict(**{s: st.enter_context(nc.semaphore(f"{name}_{s}")) for s in sems.split()})
        st2 = ExitStack()

        def sb(n, shape, dt=F32):
            return st.enter_context(nc.sbuf_tensor(f"{name}_{n}", shape, dt))

        with st2:
            block = st2.enter_context(nc.Block())
            yield S, sb, block
        nums = sorted(s.num for s in S.values())
        while nums:
            run = 1
            while run < len(nums) and nums[run] == nums[0] + run:
                run += 1
            nc.all_engine_barrier(sems_to_clear=range(nums[0], nums[0] + run))
            nums = nums[run:]


def stepper(eng, sem):
    n = [0]

    def step(ins):
        n[0] += 1
        ins.then_inc(sem, 1)
        eng.wait_ge(sem, n[0])
    return step


def layer_row(w, l):
    return w[bass.ds(l, 1), :].rearrange("o n -> (o n)").partition_broadcast(P)


def layer_col(w, l):
    return w[bass.ds(l, 1), :].rearrange("o n -> n o")


SLOT = 2048


def split_products(pe, out, stat_hi, stat_lo, mov_hi, mov_lo, start, stop):
    pe.matmul(out, stat_hi, mov_hi, start=start, stop=False, skip_group_check=True)
    pe.matmul(out, stat_hi, mov_lo, start=False, stop=False, skip_group_check=True)
    return pe.matmul(out, stat_lo, mov_hi, start=False, stop=stop, skip_group_check=True)


WEIGHT_SEMS = "raw_loaded0 raw_loaded1 w_hi w_lo chunk_done "


def weight_buffers(sb, raw=None):
    return dict(raw=raw if raw is not None else sb("w_raw", [P, 2, SLOT]),
                hi=sb("w_hi", [P, 2, SLOT], F32R), lo=sb("w_lo", [P, 2, SLOT], F32R))


def raw_sem(S, slot):
    return (S["raw_loaded0"], S["raw_loaded1"])[slot]


def weight_room(sp, S, n):
    sp.wait_ge(S["w_lo"], n - 1)


def split_scalar(act, S, W, slot, n, turn, reused):
    act.wait_ge(raw_sem(S, slot), 32 * turn + 32)
    if reused:
        act.wait_ge(S["chunk_done"], n - 1)
    act.activation(W["hi"][:, slot], W["raw"][:, slot], ACT.Copy).then_inc(S["w_hi"], 1)


def split_vector(dve, S, W, slot, n):
    dve.wait_ge(S["w_hi"], n + 1)
    dve.tensor_tensor(W["lo"][:, slot], W["raw"][:, slot], W["hi"][:, slot].bitcast(F32),
                      ALU.subtract).then_inc(S["w_lo"], 1)


PRE_SEMS = "pre_gain_loaded rms_done inv_done normed turned h_hi h_lo "


def pre_buffers(sb, work):
    return dict(gain=sb("gain", [P, D_MODEL]), rms=sb("pre_rms", [P, TILES]), inv=sb("pre_inv", [P, TILES]),
                normed=work.rearrange("p (s n) -> p s n", s=2),
                hi=sb("h_hi", [P, KC, NT], F32R), lo=sb("h_lo", [P, KC, NT], F32R))


def pre_view(x, t, half):
    return x[:, 4 * half:4 * half + 4, tok(t)]


def pre_bank(E, t, half):
    return E["ps"][:, 2 * (t % 2) + half, 0:4 * ROWS[t]].rearrange("p (c r) -> p c r", c=4)


WEIGHTS_AFTER = {1: 0, 3: 1}


def pre_scalar(act, E, S, B, split):
    act.activation(B["rms"][:, :], E["sumsq"][:, :], ACT.Sqrt, bias=E["eps"][:, 0:1],
                   scale=1.0 / D_MODEL).then_inc(S["rms_done"], 1)
    for t in range(TILES):
        for half in range(2):
            act.wait_ge(S["turned"], 2 * t + half + 1)
            act.activation(pre_view(B["hi"], t, half), pre_bank(E, t, half), ACT.Copy).then_inc(S["h_hi"], 1)
        if t in WEIGHTS_AFTER:
            split(WEIGHTS_AFTER[t])


def pre_vector(dve, E, S, W, B):
    dve.wait_ge(S["rms_done"], 1)
    dve.reciprocal(B["inv"][:, :], B["rms"][:, :]).then_inc(S["inv_done"], 1)
    dve.wait_ge(S["inv_done"], 1)
    dve.wait_ge(S["pre_gain_loaded"], 16)
    for t in range(TILES + 1):
        if t < TILES:
            r = ROWS[t]
            if t >= 2:
                dve.wait_ge(S["turned"], 2 * t - 2)
            dve.scalar_tensor_tensor(B["normed"][:r, t % 2, :], E["x"][:r, t, :], B["inv"][:r, t:t + 1],
                                     B["gain"][:r, :], ALU.mult, ALU.mult).then_inc(S["normed"], 1)
        if t > 0:
            for half in range(2):
                dve.wait_ge(S["h_hi"], 2 * (t - 1) + half + 1)
                dve.tensor_tensor(pre_view(B["lo"], t - 1, half), pre_bank(E, t - 1, half),
                                  pre_view(B["hi"], t - 1, half).bitcast(F32), ALU.subtract).then_inc(S["h_lo"], 1)
            if t - 1 in WEIGHTS_AFTER:
                n = WEIGHTS_AFTER[t - 1]
                split_vector(dve, S, W, n, n)


def pre_tensor(pe, E, S, B):
    for t, r in enumerate(ROWS):
        pe.wait_ge(S["normed"], t + 1)
        for half in range(2):
            if t >= 2:
                pe.wait_ge(S["h_lo"], 2 * (t - 2) + half + 1)
            for c in range(4):
                mm = pe.transpose(E["ps"][:, 2 * (t % 2) + half, c * r:(c + 1) * r],
                                  B["normed"][:r, t % 2, (4 * half + c) * P:(4 * half + c + 1) * P],
                                  E["ident"][:r, :r])
            mm.then_inc(S["turned"], 1)
    pe.wait_ge(S["h_lo"], 2 * TILES)


POST_SEMS = "post_gain_loaded half_done y_squares y_gained y_base y_rms y_inv added x_squares "


def post_chunks(nk):
    return [(h, k) for h in range(2) for k in range(0, nk, 4)]


def post_sync(sp, S, W, w, l, nk, base):
    wv = w[bass.ds(l, 1)].rearrange("o (k p) n -> p (o k) n", p=P)
    for q, (h, k) in enumerate(post_chunks(nk)):
        n = base + q
        if n >= 2:
            weight_room(sp, S, n)
        dst = W["raw"][:, n % 2].rearrange("p (k n) -> p k n", k=4)
        for i in range(0, 4, 2):
            sp.dma_start(dst[:, i:i + 2], wv[:, k + i:k + i + 2, h * 512:(h + 1) * 512]).then_inc(
                raw_sem(S, n % 2), 16)


def post_tensor(pe, E, S, W, a_hi, a_lo, nk, base):
    for q, (h, k) in enumerate(post_chunks(nk)):
        n = base + q
        pe.wait_ge(S["w_lo"], n + 1)
        hi, lo = (W[x][:, n % 2].rearrange("p (k n) -> p k n", k=4) for x in ("hi", "lo"))
        last = k + 4 == nk
        order = [(kk, t) for t in range(TILES) for kk in range(4)] if last else [
            (kk, t) for kk in range(4) for t in range(TILES)]
        for kk, t in order:
            r = ROWS[t]
            if h == 1 and k + kk == 0:
                pe.wait_ge(S["y_gained"], t + 1)
            mm = split_products(pe, E["ps"][:r, t, 0:512], a_hi[:, k + kk, tok(t)], a_lo[:, k + kk, tok(t)],
                                hi[:, kk], lo[:, kk], k + kk == 0, k + kk == nk - 1)
            if k + kk == nk - 1 and t < TILES - 1:
                mm.then_inc(S["half_done"], 1)
        mm.then_inc(S["chunk_done"], 1)


def post_splits(nk, base, h, late):
    per = nk // 4
    qs = range((h + 1) * per - 1, (h + 1) * per) if late else range(h * per, (h + 1) * per - 1)
    return [base + q + 2 for q in qs if q + 2 < len(post_chunks(nk))]


def post_wait(eng, S, h, t, nk, base):
    if t < TILES - 1:
        eng.wait_ge(S["half_done"], (TILES - 1) * h + t + 1)
    else:
        eng.wait_ge(S["chunk_done"], base + (h + 1) * nk // 4)


def post_buffers(sb):
    return dict(squares=sb("y_squares", [P, 2, TILES]), base=sb("y_base", [P, TILES]), rms=sb("y_rms", [P, TILES]),
                inv=sb("y_inv", [P, TILES]))


def post_scalar(act, E, S, W, Y, scratch, x_scratch, nk, base):
    def x_squares(t):
        r = ROWS[t]
        act.wait_ge(S["added"], t + 1)
        if t > 0:
            act.wait_ge(S["x_squares"], t)
        act.activation(x_scratch[:r], E["x"][:r, t, :], ACT.Square,
                       accum_out=E["sumsq"][:r, t:t + 1]).then_inc(S["x_squares"], 1)

    for h in range(2):
        for n in post_splits(nk, base, h, False):
            split_scalar(act, S, W, n % 2, n, n // 2, True)
        for t, r in enumerate(ROWS):
            post_wait(act, S, h, t, nk, base)
            if h + t > 0:
                act.wait_ge(S["y_squares"], TILES * h + t)
            act.activation(scratch[:r], E["ps"][:r, t, 0:512], ACT.Square,
                           accum_out=Y["squares"][:r, h, t:t + 1]).then_inc(S["y_squares"], 1)
            if h == 1:
                act.wait_ge(S["y_squares"], TILES + t + 1)
                act.wait_ge(S["y_base"], 1)
                act.activation(Y["rms"][:r, t:t + 1], Y["squares"][:r, 1, t:t + 1], ACT.Sqrt, bias=Y["base"][:r, t:t + 1],
                               scale=Y["scale"]).then_inc(S["y_rms"], 1)
                if t > 0:
                    x_squares(t - 1)
        for n in post_splits(nk, base, h, True):
            split_scalar(act, S, W, n % 2, n, n // 2, True)
    x_squares(TILES - 1)


def post_vector(dve, E, S, W, Y, y, gain, nk, base):
    for h in range(2):
        for n in post_splits(nk, base, h, False):
            split_vector(dve, S, W, n % 2, n)
        if h == 0:
            dve.wait_ge(S["post_gain_loaded"], 16)
        for t, r in enumerate(ROWS):
            dve.wait_ge(S["y_squares"], TILES * h + t + 1)
            dve.tensor_tensor(y[:r, h, t * 512:(t + 1) * 512], E["ps"][:r, t, 0:512], gain[:r, h * 512:(h + 1) * 512],
                              ALU.mult).then_inc(S["y_gained"], 1)
            if h == 1:
                dve.wait_ge(S["y_rms"], t + 1)
                dve.reciprocal(Y["inv"][:r, t:t + 1], Y["rms"][:r, t:t + 1]).then_inc(S["y_inv"], 1)
                dve.wait_ge(S["y_inv"], t + 1)
                dve.wait_ge(S["y_gained"], TILES + t + 1)
                xt = E["x"][:r, t, :].rearrange("p (h n) -> p h n", h=2)
                dve.scalar_tensor_tensor(xt, y[:r, :, t * 512:(t + 1) * 512], Y["inv"][:r, t:t + 1], xt,
                                         ALU.mult, ALU.add).then_inc(S["added"], 1)
        if h == 0:
            dve.wait_ge(S["y_squares"], TILES)
            for t, r in enumerate(ROWS):
                ins = dve.tensor_scalar(Y["base"][:r, t:t + 1], Y["squares"][:r, 0, t:t + 1], Y["scale"], Y["eps"],
                                        ALU.mult, ALU.add)
            ins.then_inc(S["y_base"], 1)
        for n in post_splits(nk, base, h, True):
            split_vector(dve, S, W, n % 2, n)


def ffn(nc, E, l, name, g_pre, w_in, w_out, g_post):
    sems = PRE_SEMS + POST_SEMS + WEIGHT_SEMS + "unit_done silu_done a_done a_hi a_lo"
    WORK = 3 * D_MODEL
    with stage(nc, name, sems) as (S, sb, block):
        room = sb("room", [P, WORK + 2 * SLOT])
        B = pre_buffers(sb, room[:, 0:2 * D_MODEL])
        Y = post_buffers(sb)
        Y["scale"], Y["eps"] = 4.0 / D_MODEL, 4.0 * EPS
        W = weight_buffers(sb, room[:, WORK:].rearrange("p (s n) -> p s n", s=2))
        y = room[:, 0:2 * WORK].rearrange("p (h n) -> p h n", h=2)
        y_scratch = room[:, TILES * 512:WORK]
        x_scratch = room[:, WORK + TILES * 512:WORK + TILES * 512 + D_MODEL]
        a_hi = sb("a_hi", [P, FF, NT], F32R)
        a_lo = sb("a_lo", [P, FF, NT], F32R)
        gate = sb("gate", [P, 4, HALF])
        w_v = w_in[bass.ds(l, 1)].rearrange("o (c p) (b f) -> p b (o c) f", p=P, b=2)

        @block.sync
        def _(sp):
            sp.dma_start(B["gain"][:], layer_row(g_pre, l)).then_inc(S["pre_gain_loaded"], 16)

            def load(slot, n):
                dst = W["raw"][:, slot].rearrange("p (b c f) -> p b c f", b=2, c=KC)
                for b in range(2):
                    sp.dma_start(dst[:, b], w_v[:, b, :, bass.ds(n * P, P)]).then_inc(raw_sem(S, slot), 16)

            load(0, 0)
            load(1, 1)
            with sp.Fori(1, FF // 2) as i:
                for slot in range(2):
                    weight_room(sp, S, 2 * i + slot)
                    load(slot, 2 * i + slot)
            sp.wait_ge(S["normed"], TILES)
            sp.dma_start(B["gain"][:], layer_row(g_post, l)).then_inc(S["post_gain_loaded"], 16)
            post_sync(sp, S, W, w_out, l, FF, FF)

        @block.tensor
        def _(pe):
            pre_tensor(pe, E, S, B)

            def two_chunks(i, first):
                for slot in range(2):
                    n = 2 * i + slot
                    pe.wait_ge(S["w_lo"], n + 1)
                    hi, lo = (W[x][:, slot].rearrange("p (b c f) -> p b c f", b=2, c=KC) for x in ("hi", "lo"))
                    for half in range(2):
                        k = 2 * slot + half
                        if not first:
                            pe.wait_ge(S["a_done"], 4 * i + k - 3)
                        hs = slice(half * HALF, (half + 1) * HALF)
                        for b in range(2):
                            for c in range(KC):
                                mm = split_products(pe, E["ps"][:, 2 * k + b, 0:HALF], hi[:, b, c], lo[:, b, c],
                                                    B["hi"][:, c, hs], B["lo"][:, c, hs], c == 0, c == KC - 1)
                        if half == 0:
                            mm.then_inc(S["unit_done"], 1)
                    mm.then_inc(S["chunk_done"], 1)

            two_chunks(0, True)
            with pe.Fori(1, FF // 2) as i:
                two_chunks(i, False)
            pe.wait_ge(S["a_lo"], 2 * FF)
            post_tensor(pe, E, S, W, a_hi, a_lo, FF, FF)

        def a_part(x, i, k):
            return x[:, bass.ds(2 * i + k // 2, 1), (k % 2) * HALF:(k % 2 + 1) * HALF].rearrange("p o n -> p (o n)")

        @block.scalar
        def _(act):
            pre_scalar(act, E, S, B, lambda n: split_scalar(act, S, W, n, n, 0, False))

            def two_chunks(i, first):
                for slot in range(2):
                    for half in range(2):
                        k = 2 * slot + half
                        if half == 0:
                            act.wait_ge(S["unit_done"], 2 * i + slot + 1)
                        else:
                            act.wait_ge(S["chunk_done"], 2 * i + slot + 1)
                        if not first:
                            act.wait_ge(S["a_lo"], 4 * i + k - 3)
                        act.activation(gate[:, k, :], E["ps"][:, 2 * k, 0:HALF], ACT.Silu).then_inc(S["silu_done"], 1)
                        act.wait_ge(S["a_done"], 4 * i + k + 1)
                        act.activation(a_part(a_hi, i, k), gate[:, k, :], ACT.Copy).then_inc(S["a_hi"], 1)
                    split_scalar(act, S, W, slot, 2 * i + slot + 2, i + 1, True)

            two_chunks(0, True)
            with act.Fori(1, FF // 2) as i:
                two_chunks(i, False)
            post_scalar(act, E, S, W, Y, y_scratch, x_scratch, FF, FF)

        @block.vector
        def _(dve):
            pre_vector(dve, E, S, W, B)
            with dve.Fori(0, FF // 2) as i:
                for slot in range(2):
                    for half in range(2):
                        k = 2 * slot + half
                        dve.wait_ge(S["silu_done"], 4 * i + k + 1)
                        dve.tensor_tensor(gate[:, k, :], gate[:, k, :], E["ps"][:, 2 * k + 1, 0:HALF],
                                          ALU.mult).then_inc(S["a_done"], 1)
                        dve.wait_ge(S["a_hi"], 4 * i + k + 1)
                        dve.tensor_tensor(a_part(a_lo, i, k), gate[:, k, :], a_part(a_hi, i, k).bitcast(F32),
                                          ALU.subtract).then_inc(S["a_lo"], 1)
                    split_vector(dve, S, W, slot, 2 * i + slot + 2)
            post_vector(dve, E, S, W, Y, y, B["gain"], FF, FF)


BLOCKS = (
    ("turned", ((0, COL["aq"], 2 * W4),)),
    ("turned", ((0, COL["bq"], W4),)),
    ("turned", ((0, COL["dq"], 2 * W4),)),
    ("rows", ((0, COL["ak"], 2 * W4),)),
    ("rows", ((0, COL["ao"], W4), (W4, COL["cv"], W4))),
    ("rows", ((0, COL["bv"], 2 * W4),)),
    ("rows", ((0, COL["cq"], 2 * W4),)),
    ("rows", ((0, COL["dk"], 2 * W4),)),
)
AQ, AK, BQ, BK, DQ, DK = 0, 2, 4, 5, 6, 8
GATE_I, GATE_F, LOWRANK = 0, 32, 64
GATE_ROWS = LOWRANK + RANK
QK_SCALE = HD ** -0.5


def project(nc, E, M, l, g_pre, w_in, O):
    sems = PRE_SEMS + WEIGHT_SEMS + "unit_done act_out dve_out ones_set"
    KH = KC // 2
    GATE_COL = W4
    with stage(nc, "pr", sems) as (S, sb, block):
        B = pre_buffers(sb, sb("work", [P, 2 * D_MODEL])[:])
        W = weight_buffers(sb)
        w_v = w_in[bass.ds(l, 1)].rearrange("o (c p) f -> p (o c) f", p=P)

        units = []
        for b, (kind, parts) in enumerate(BLOCKS):
            if kind == "turned":
                width = sum(n for _, _, n in parts)
                units += [(b, kind, m, half) for m in range(width // P) for half in range(2)]
                if b == 1:
                    units += [(b, "gates", 0, half) for half in range(2)]
            else:
                units += [(b, kind, t, 0) for t in range(TILES)]
        first_tile = {0: AQ, 1: BQ, 2: DQ}
        numbers = [[n for n, u in enumerate(units) if u[0] == b] for b in range(len(BLOCKS))]
        chunks = 2 * len(BLOCKS)

        @block.sync
        def _(sp):
            sp.dma_start(B["gain"][:], layer_row(g_pre, l)).then_inc(S["pre_gain_loaded"], 16)
            for b, (kind, parts) in enumerate(BLOCKS):
                for hc in range(2):
                    n = 2 * b + hc
                    if n >= 2:
                        weight_room(sp, S, n)
                    dst = W["raw"][:, hc].rearrange("p (c f) -> p c f", c=KH)
                    cs = slice(KH * hc, KH * hc + KH)
                    if b == 1:
                        (at, src, width), = parts
                        sp.dma_start(dst[:, :, at:at + width], w_v[:, cs, src:src + width]).then_inc(raw_sem(S, hc), 16)
                        for row, part, width in ((GATE_I, "ai", H), (GATE_F, "af", H), (LOWRANK, "blr", RANK)):
                            at = GATE_COL + row
                            sp.dma_start(dst[:, :, at:at + width], w_v[:, cs, COL[part]:COL[part] + width]).then_inc(
                                raw_sem(S, hc), 16)
                    else:
                        if len(parts) == 1:
                            (at, src, width), = parts
                            parts = ((at, src, width // 2), (at + width // 2, src + width // 2, width // 2))
                        for at, src, width in parts:
                            sp.dma_start(dst[:, :, at:at + width], w_v[:, cs, src:src + width]).then_inc(
                                raw_sem(S, hc), 16)

        def raw_count(n):
            return 16 * sum(4 if b == 1 else 2 for b in range(n // 2 + 1))

        @block.tensor
        def _(pe):
            pre_tensor(pe, E, S, B)
            for n in range(chunks):
                b, hc = n // 2, n % 2
                pe.wait_ge(S["w_lo"], n + 1)
                hi, lo = (W[x][:, hc].rearrange("p (c f) -> p c f", c=KH) for x in ("hi", "lo"))
                for u in numbers[b]:
                    _, kind, m, half = units[u]
                    if hc == 0 and u >= 8:
                        pe.wait_ge(S["act_out"] if u % 2 == 0 else S["dve_out"], (u - 8) // 2 + 1)
                    hs = slice(half * HALF, (half + 1) * HALF)
                    for c in range(KH):
                        cc = KH * hc + c
                        if kind == "rows":
                            out = E["ps"][:ROWS[m], u % 8, 0:512]
                            ops = (B["hi"][:, cc, tok(m)], B["lo"][:, cc, tok(m)], hi[:, c, :], lo[:, c, :])
                        else:
                            cols = slice(m * P, (m + 1) * P)
                            if kind == "gates":
                                cols = slice(GATE_COL, GATE_COL + GATE_ROWS)
                            out = E["ps"][:cols.stop - cols.start, u % 8, 0:HALF]
                            ops = (hi[:, c, cols], lo[:, c, cols], B["hi"][:, cc, hs], B["lo"][:, cc, hs])
                        mm = split_products(pe, out, *ops, cc == 0, cc == KC - 1)
                    if hc == 1 and u != numbers[b][-1]:
                        mm.then_inc(S["unit_done"], 1)
                mm.then_inc(S["chunk_done"], 1)

        def unit_wait(eng, u):
            b = units[u][0]
            if u == numbers[b][-1]:
                eng.wait_ge(S["chunk_done"], 2 * b + 2)
            else:
                eng.wait_ge(S["unit_done"], u + 1 - b)

        def copies(n):
            b, kind, m, half = units[n]
            hs = slice(half * HALF, (half + 1) * HALF)
            bank = E["ps"][:, n % 8, :]
            if kind == "turned":
                tile = first_tile[b] + m
                scale = {AK: QK_SCALE, AK + 1: QK_SCALE, BQ: DK_B ** -0.5, DQ: QK_SCALE, DQ + 1: QK_SCALE}.get(tile, 1.0)
                return [(M["TR"][:, tile, hs], bank[:, 0:HALF], scale)]
            if kind == "gates":
                return [(M["gates"][:, hs], bank[:GATE_ROWS, 0:HALF], 1.0)]
            r = ROWS[m]
            lo, hi = bank[:r, 0:W4], bank[:r, W4:512]
            if b == 3:
                return [(M["KA"][:r, m, :], lo, QK_SCALE),
                        (M["VA"][:r, m, :, 0:HD], hi.rearrange("p (h d) -> p h d", h=H), 1.0)]
            if b == 4:
                return [(M["AO"][:r, m, :], lo, 1.0), (M["CV"][:r, m, :], hi, 1.0)]
            whole = {5: M["BVG"], 6: M["CQK"], 7: M["DKV"]}[b]
            return [(whole[:r, m, :], bank[:r, :], 1.0)]

        @block.scalar
        def _(act):
            def split(n):
                act.wait_ge(raw_sem(S, n), raw_count(n))
                act.activation(W["hi"][:, n], W["raw"][:, n], ACT.Copy).then_inc(S["w_hi"], 1)

            pre_scalar(act, E, S, B, split)
            for n in range(2, chunks + 2):
                if n < chunks:
                    act.wait_ge(raw_sem(S, n % 2), raw_count(n))
                    act.wait_ge(S["chunk_done"], n - 1)
                    act.activation(W["hi"][:, n % 2], W["raw"][:, n % 2], ACT.Copy).then_inc(S["w_hi"], 1)
                if n % 2 == 1:
                    for u in numbers[(n - 2) // 2]:
                        if u % 2 == 0:
                            unit_wait(act, u)
                            for out, src, scale in copies(u):
                                ins = act.activation(out, src, ACT.Copy, scale=scale)
                            ins.then_inc(S["act_out"], 1)

        @block.vector
        def _(dve):
            dve.memset(M["VA"][:, :, :, HD:HD + 1], 1.0).then_inc(S["ones_set"], 1)
            pre_vector(dve, E, S, W, B)
            for n in range(2, chunks + 2):
                if n < chunks:
                    split_vector(dve, S, W, n % 2, n)
                if n % 2 == 1:
                    for u in numbers[(n - 2) // 2]:
                        if u % 2 == 1:
                            unit_wait(dve, u)
                            for out, src, scale in copies(u):
                                if scale == 1.0:
                                    ins = dve.tensor_copy(out, src)
                                else:
                                    ins = dve.tensor_scalar(out, src, scale, None, ALU.mult)
                            ins.then_inc(S["dve_out"], 1)


HEAD_SEMS = "squared ssq_done root_done root_inv_done head_scaled head_gated head_turned head_out "


def head_vector(dve, S, B, h, gate):
    n = len(PARTS)
    for rs, ts in PARTS:
        dve.tensor_tensor(B["sq"][rs, ts], h[rs, ts], h[rs, ts], ALU.mult).then_inc(S["squared"], 1)
    dve.wait_ge(S["squared"], n)
    for rs, ts in PARTS:
        dve.tensor_reduce(B["ssq"][rs, ts, :], B["sq"][rs, ts].rearrange("p t (h d) -> p t h d", h=H), AX.X,
                          ALU.add).then_inc(S["ssq_done"], 1)
    dve.wait_ge(S["root_done"], n)
    for rs, ts in PARTS:
        dve.reciprocal(B["ssq"][rs, ts, :], B["ssq"][rs, ts, :]).then_inc(S["root_inv_done"], 1)
    dve.wait_ge(S["root_inv_done"], n)
    for rs, ts in PARTS:
        hv = h[rs, ts].rearrange("p t (h d) -> p t h d", h=H)
        dve.tensor_tensor(hv, hv, B["ssq"][rs, ts, :].unsqueeze(3).to_broadcast(list(hv.shape)),
                          ALU.mult).then_inc(S["head_scaled"], 1)
    dve.wait_ge(S["head_scaled"], n)
    for rs, ts in PARTS:
        dve.tensor_tensor(h[rs, ts], h[rs, ts], gate[rs, ts], ALU.mult).then_inc(S["head_gated"], 1)


def head_scalar_root(act, E, S, B):
    act.wait_ge(S["ssq_done"], len(PARTS))
    for rs, ts in PARTS:
        act.activation(B["ssq"][rs, ts, :], B["ssq"][rs, ts, :], ACT.Sqrt, bias=E["eps"][rs, 0:1],
                       scale=1.0 / HD).then_inc(S["root_done"], 1)


def head_tensor(pe, E, S, h, bank):
    pe.wait_ge(S["head_gated"], len(PARTS))
    for t, r in enumerate(ROWS):
        for pair in range(2):
            n = 2 * t + pair
            if n >= 2:
                pe.wait_ge(S["head_out"], n - 1)
            pe.transpose(E["ps"][:, bank + n % 2, 0:r], h[:r, t, pair * P:(pair + 1) * P],
                         E["ident"][:r, :r]).then_inc(S["head_turned"], 1)


def head_scalar_out(act, E, M, S, chunk, bank):
    for t, r in enumerate(ROWS):
        for pair in range(2):
            n = 2 * t + pair
            act.wait_ge(S["head_turned"], n + 1)
            act.activation(M["mixT"][:, chunk + pair, tok(t)], E["ps"][:, bank + n % 2, 0:r], ACT.Copy).then_inc(S["head_out"], 1)


def head_buffers(sb):
    return dict(sq=sb("sq", [P, TILES, W4]), ssq=sb("ssq", [P, TILES, H]))


def mlstm(nc, E, M, l, I, O, C):
    sems = HEAD_SEMS + ("consts state bias gains dve_step act_step pe_step dve_to_act act_to_dve dve_to_pe "
                        "exps_done cols_turned cols_copied decay_copied n0_turned states_whole "
                        "query_bcast query_ready keys_ready bcast_done scores_done weights_done probs_done "
                        "out_whole out_copied p_state_done s_state_done s_state_added p_state_copied "
                        "n_turned n_copied stored gate_done")
    with stage(nc, "ml", sems) as (S, sb, block):
        HB = head_buffers(sb)
        sel = sb("sel", [H, H, P])
        mask = sb("mask", [P, P])
        s_mask = sb("s_mask", [NS, NS])
        keep = sb("keep", [H, NT])
        cut = sb("cut", [H, NT])
        pair_tok = sb("pair_tok", [P, DEC_BATCH // 2, NS])
        pair_last = sb("pair_last", [NS, DEC_BATCH // 2, P])
        tok_req = sb("tok_req", [NS, DEC_BATCH])
        b_i = sb("b_i", [H, 1])
        b_f = sb("b_f", [P, 1])
        m0 = sb("m0", [H, DEC_BATCH])
        n0 = sb("n0", [4 * H, P])
        gain = sb("gain", [P, W4])
        c0 = sb("c0", [P, 4, H, HD + 1])
        ig = sb("ig", [H, NT])
        fy = sb("fy", [H, NT])
        sp_ = sb("softplus", [H, NT])
        lf = sb("lf", [H, NT])
        lfc = sb("lf_cut", [H, NT])
        floor = sb("floor", [H, NT])
        st0 = sb("start", [H, DEC_BATCH])
        bsum = sb("bsum", [H, NT])
        m = sb("m", [H, NT])
        a = sb("a", [H, NT])
        wrow = sb("wrow", [H, NT])
        ws = sb("ws", [H, NT])
        em = sb("em", [H, NT])
        ea = sb("ea", [H, NS])
        cols = sb("cols", [P, 3, TILES, H])
        ea_col = sb("ea_col", [NS, H])
        decay = sb("decay", [P, 4, H])
        qd = sb("qd", [P, H, NS])
        qm = sb("qm", [P, H, 4, NS])
        km = sb("km", [NS, H, DEC_BATCH, HD])
        ex = sb("ex", [P, 2, SEQ])
        pr = sb("pr", [P, 2, SEQ])
        oc = sb("oc", [P, H, TILES, HD + 1])
        den = sb("den", [P, TILES, H])
        den2 = sb("den2", [P, TILES, H])
        hA = sb("hA", [P, TILES, W4])
        pc = sb("pc", [HD, H, HD + 1])
        pn = sb("pn", [4 * H, P])
        np_ = sb("np", [H, HD])
        ps = E["ps"]
        first = SEQ
        last = SEQ + DEC_SEQ - 1

        def s_rows(x):
            return x[:, first:NT].rearrange("p (r t) -> p r t", t=DEC_SEQ)

        @block.sync
        def _(sp):
            for dst, n in ((sel, "head_rows"), (mask, "turned_mask"), (s_mask, "s_turned_mask"), (keep, "keep_a"),
                           (cut, "cut_a"), (pair_tok, "pair_tokens"), (pair_last, "pair_last"),
                           (tok_req, "token_request")):
                sp.dma_start(dst[:], C[n]).then_inc(S["consts"], 16)
            sp.dma_start(b_i[:], layer_col(I["b_ig"], l)).then_inc(S["bias"], 16)
            sp.dma_start(b_f[GATE_F:GATE_F + H, :], layer_col(I["b_fg"], l)).then_inc(S["bias"], 16)
            with nc.allow_non_contiguous_dma(reason="32 stabilisers"):
                sp.dma_start(m0[:], I["state_mlstm_m"][bass.ds(l, 1)].rearrange("o r h -> h (o r)")).then_inc(S["bias"], 16)
            sp.dma_start(gain[:], layer_row(I["g_head_a"], l)).then_inc(S["gains"], 16)
            nv = I["state_mlstm_n"][bass.ds(l, 1)].rearrange("o (q j) h d -> q h (o j) d", j=2)
            for q in range(4):
                sp.dma_start(n0[H * q:H * q + H, :].rearrange("p (j d) -> p j d", j=2), nv[q]).then_inc(S["state"], 16)
            cv = I["state_mlstm_c"][bass.ds(l, 1)].rearrange("o (q j) h d e -> j h (o d) q e", j=2)
            for j in range(2):
                for h in range(H):
                    sp.dma_start(c0[j * HD:(j + 1) * HD, :, h, 0:HD], cv[j, h]).then_inc(S["state"], 16)
            n = 0
            sp.wait_ge(S["p_state_copied"], 1)
            sp.dma_start(O["p_mlstm_c"][bass.ds(l, 1)].rearrange("o b h d e -> d (o b h) e"), pc[:, :, 0:HD]).then_inc(S["stored"], 16)
            n += 1
            with nc.allow_non_contiguous_dma(reason="the last stabilisers"):
                sp.dma_start(O["p_mlstm_m"][bass.ds(l, 1)].rearrange("o b h -> h (o b)"), m[:, SEQ - 1:SEQ]).then_inc(S["stored"], 16)
                sp.dma_start(O["s_mlstm_m"][bass.ds(l, 1)].rearrange("o r h -> h (o r)"),
                             m[:, last:NT:DEC_SEQ]).then_inc(S["stored"], 16)
            n += 2
            sp.wait_ge(S["s_state_added"], 2 * H)
            cw = O["s_mlstm_c"][bass.ds(l, 1)].rearrange("o (q j) h d e -> j h (o d) q e", j=2)
            for j in range(2):
                for h in range(H):
                    sp.dma_start(cw[j, h], c0[j * HD:(j + 1) * HD, :, h, 0:HD]).then_inc(S["stored"], 16)
                    n += 1
            sp.wait_ge(S["n_copied"], 2)
            sp.dma_start(O["p_mlstm_n"][bass.ds(l, 1)].rearrange("o b h d -> (o b h) d"), np_[:]).then_inc(S["stored"], 16)
            nw = O["s_mlstm_n"][bass.ds(l, 1)].rearrange("o (q j) h d -> q h (o j) d", j=2)
            for q in range(4):
                sp.dma_start(nw[q], pn[H * q:H * q + H, :].rearrange("p (j d) -> p j d", j=2)).then_inc(S["stored"], 16)
            n += 5
            sp.wait_ge(S["stored"], 16 * n)

        units = [(h, c) for h in range(H) for c in range(TILES)]

        def width(c):
            return SEQ - c * P if c < PT_TILES else NS

        def queries(c):
            return slice(c * P, SEQ) if c < PT_TILES else slice(SEQ, NT)

        @block.vector
        def _(dve):
            step = stepper(dve, S["dve_step"])
            dve.wait_ge(S["bias"], 48)
            dve.wait_ge(S["consts"], 16 * 8)
            step(dve.tensor_scalar(ig[:], M["gates"][GATE_I:GATE_I + H, :], b_i[:, 0:1], None, ALU.add))
            dve.tensor_scalar(fy[:], M["gates"][GATE_F:GATE_F + H, :], b_f[GATE_F:GATE_F + H, 0:1], None,
                              ALU.add).then_inc(S["dve_to_act"], 1)
            dve.wait_ge(S["dve_to_act"], 1)
            dve.wait_ge(S["act_to_dve"], 3)
            step(dve.scalar_tensor_tensor(lf[:], fy[:], 0.0, sp_[:], ALU.min, ALU.subtract))
            step(dve.tensor_tensor_scan(bsum[:], keep[:], lf[:], 0.0, ALU.mult, ALU.add))
            step(dve.tensor_tensor(lfc[:], lf[:], cut[:], ALU.add))
            step(dve.tensor_copy(floor[:], ig[:]))
            step(dve.tensor_tensor(st0[:], lf[:, first:NT:DEC_SEQ], m0[:], ALU.add))
            step(dve.tensor_tensor(floor[:, first:NT:DEC_SEQ], ig[:, first:NT:DEC_SEQ], st0[:], ALU.max))
            step(dve.tensor_tensor_scan(m[:], lfc[:], floor[:], 0.0, ALU.add, ALU.max))
            step(dve.tensor_tensor(a[:], bsum[:], m[:], ALU.subtract))
            step(dve.tensor_tensor(wrow[:], ig[:], bsum[:], ALU.subtract))
            step(dve.tensor_scalar(ws[:, 0:SEQ], wrow[:, 0:SEQ], a[:, SEQ - 1:SEQ], None, ALU.add))
            step(dve.tensor_tensor(s_rows(ws), s_rows(wrow),
                                   a[:, last:NT:DEC_SEQ].unsqueeze(2).to_broadcast([H, DEC_BATCH, DEC_SEQ]), ALU.add))
            dve.tensor_tensor(ea[:].rearrange("p (r t) -> p r t", t=DEC_SEQ), s_rows(a),
                              m0[:].unsqueeze(2).to_broadcast([H, DEC_BATCH, DEC_SEQ]), ALU.add).then_inc(S["dve_to_act"], 1)

            dve.wait_ge(S["cols_turned"], 1)
            n = TILES * H
            cps = ps[:, 7, 0:3 * n].rearrange("p (k t h) -> p k t h", k=3, t=TILES)
            for rs, ts in PARTS:
                step(dve.tensor_copy(cols[rs, :, ts, :], cps[rs, :, ts, :]))
            dve.tensor_copy(ea_col[:], ps[:NS, 7, 3 * n:3 * n + H]).then_inc(S["cols_copied"], 1)
            dve.wait_ge(S["n0_turned"], 1)
            dve.wait_ge(S["state"], 16 * 12)
            step(dve.tensor_copy(decay[:], ps[:, 7, 0:16].rearrange("p (q h) -> p q h", q=4)))
            step(dve.tensor_copy(c0[:, :, :, HD], ps[:, 7, 16:32].rearrange("p (q h) -> p q h", q=4)))

            dve.wait_ge(S["query_bcast"], 1)
            for h in range(H):
                o = (h % 2) * HD
                for j in range(2):
                    step(dve.tensor_tensor(qd[j * HD:(j + 1) * HD, h, :], M["TR"][o:o + HD, AQ + h // 2, SEQ:NT],
                                           ps[j * HD:(j + 1) * HD, 6, h * NS:(h + 1) * NS], ALU.mult))
            for h in range(H):
                dve.tensor_tensor(qm[:, h], pair_tok[:], qd[:, h, :].unsqueeze(1).to_broadcast([P, 4, NS]),
                                  ALU.mult).then_inc(S["query_ready"], 1)
            for rs, ts in PARTS:
                kv = M["KA"][rs, ts, :].rearrange("p t (h d) -> p t h d", h=H)
                step(dve.tensor_tensor(kv, kv, cols[rs, 1, ts, :].unsqueeze(3).to_broadcast(list(kv.shape)), ALU.mult))
            for h in range(H):
                dve.tensor_tensor(km[:, h], M["KA"][:NS, PT_TILES, h * HD:(h + 1) * HD].unsqueeze(1).to_broadcast(
                    [NS, DEC_BATCH, HD]), tok_req[:].unsqueeze(2).to_broadcast([NS, DEC_BATCH, HD]),
                    ALU.mult).then_inc(S["keys_ready"], 1)
            for u, (h, c) in enumerate(units):
                dve.wait_ge(S["weights_done"], u + 1)
                dve.wait_ge(S["scores_done"], u + 1)
                r, w = ROWS[c], width(c)
                if u >= 2:
                    dve.wait_ge(S["pe_step"], u - 1)
                dve.tensor_tensor(pr[:r, u % 2, 0:w], ex[:r, u % 2, 0:w], ps[:r, 2 + u % 2, 0:w],
                                  ALU.mult).then_inc(S["probs_done"], 1)
            dve.wait_ge(S["p_state_done"], 1)
            dve.tensor_copy(pc[:], ps[:HD, 6, 0:H * (HD + 1)].rearrange("p (h e) -> p h e", h=H)).then_inc(S["p_state_copied"], 1)
            for h in range(H):
                dve.wait_ge(S["out_copied"], H)
                dve.tensor_tensor(c0[:, :, h, :], c0[:, :, h, :],
                                  decay[:, :, h].unsqueeze(2).to_broadcast([P, 4, HD + 1]), ALU.mult).then_inc(S["s_state_added"], 1)
                dve.wait_ge(S["s_state_added"], 2 * h + 1)
                dve.wait_ge(S["s_state_done"], h + 1)
                dve.tensor_tensor(c0[:, :, h, :], c0[:, :, h, :],
                                  ps[:, h % 2, 0:4 * (HD + 1)].rearrange("p (q e) -> p q e", q=4), ALU.add).then_inc(S["s_state_added"], 1)
            for rs, ts in PARTS:
                dv = oc[rs, :, ts, HD].rearrange("p h t -> p t h")
                step(dve.tensor_copy(den[rs, ts], dv))
                step(dve.scalar_tensor_tensor(den2[rs, ts], den[rs, ts], -1.0, den[rs, ts], ALU.mult, ALU.max))
                step(dve.tensor_tensor(den2[rs, ts], den2[rs, ts], cols[rs, 2, ts, :], ALU.max))
                step(dve.reciprocal(den2[rs, ts], den2[rs, ts]))
                for h in range(H):
                    nt = ts.stop - ts.start
                    step(dve.tensor_tensor(hA[rs, ts, h * HD:(h + 1) * HD], oc[rs, h, ts, 0:HD],
                                           den2[rs, ts, h].unsqueeze(2).to_broadcast([rs.stop, nt, HD]), ALU.mult))
            dve.wait_ge(S["gains"], 16)
            dve.wait_ge(S["gate_done"], 2)
            for rs, ts in PARTS:
                nt = ts.stop - ts.start
                step(dve.tensor_tensor(M["AO"][rs, ts, :], M["AO"][rs, ts, :],
                                       gain[rs].unsqueeze(1).to_broadcast([rs.stop, nt, W4]), ALU.mult))
            head_vector(dve, S, HB, hA, M["AO"])

        @block.scalar
        def _(act):
            act.wait_ge(S["dve_to_act"], 1)
            act.preload_act_table_set("natural_log_exp_and_others")
            act.activation(sp_[:], fy[:], ACT.Abs).then_inc(S["act_to_dve"], 1)
            act.wait_ge(S["act_to_dve"], 1)
            act.activation(sp_[:], sp_[:], ACT.Exp, scale=-1.0).then_inc(S["act_to_dve"], 1)
            act.wait_ge(S["act_to_dve"], 2)
            act.activation(sp_[:], sp_[:], ACT.Ln, bias=1.0).then_inc(S["act_to_dve"], 1)
            act.wait_ge(S["dve_to_act"], 2)
            act.activation(ws[:], ws[:], ACT.Exp).then_inc(S["exps_done"], 1)
            act.activation(em[:], m[:], ACT.Exp, scale=-1.0).then_inc(S["exps_done"], 1)
            act.activation(ea[:], ea[:], ACT.Exp).then_inc(S["exps_done"], 1)
            act.wait_ge(S["cols_copied"], 1)
            for u, (h, c) in enumerate(units):
                act.wait_ge(S["bcast_done"], u + 1)
                r, w = ROWS[c], width(c)
                if u >= 2:
                    act.wait_ge(S["probs_done"], u - 1)
                act.activation(ex[:r, u % 2, 0:w], ps[:r, u % 2, 0:w], ACT.Exp,
                               bias=cols[:r, 0, c, h:h + 1]).then_inc(S["weights_done"], 1)
                if c == TILES - 1:
                    act.wait_ge(S["out_whole"], h + 1)
                    act.activation(oc[:, h, 0:PT_TILES, :],
                                   ps[:, 4 + h % 2, 0:PT_TILES * (HD + 1)].rearrange("p (t e) -> p t e", t=PT_TILES),
                                   ACT.Copy)
                    act.activation(oc[:NS, h, PT_TILES, :],
                                   ps[:NS, 4 + h % 2, PT_TILES * (HD + 1):TILES * (HD + 1)], ACT.Copy).then_inc(S["out_copied"], 1)
            for rs, ts in PARTS:
                act.activation(M["AO"][rs, ts, :], M["AO"][rs, ts, :], ACT.Sigmoid).then_inc(S["gate_done"], 1)
            head_scalar_root(act, E, S, HB)
            head_scalar_out(act, E, M, S, 0, 2)
            act.wait_ge(S["n_turned"], 1)
            act.activation(np_[:], ps[:H, 4, 0:HD], ACT.Copy).then_inc(S["n_copied"], 1)
            act.activation(pn[:], ps[:4 * H, 4, P:2 * P], ACT.Copy).then_inc(S["n_copied"], 1)

        @block.tensor
        def _(pe):
            pe.wait_ge(S["exps_done"], 3)
            n = TILES * H
            for k, row in enumerate((wrow, ws, em)):
                for t, r in enumerate(ROWS):
                    pe.transpose(ps[:r, 7, k * n + t * H:k * n + (t + 1) * H], row[:, tok(t)], E["ident"][:H, :H])
            pe.transpose(ps[:NS, 7, 3 * n:3 * n + H], ea[:], E["ident"][:H, :H]).then_inc(S["cols_turned"], 1)
            pe.wait_ge(S["consts"], 16 * 8)
            for h in range(H):
                mm = pe.matmul(ps[:, 6, h * NS:(h + 1) * NS], sel[:, h, :], ea[:], start=True, stop=True)
            mm.then_inc(S["query_bcast"], 1)
            pe.wait_ge(S["cols_copied"], 1)
            pe.wait_ge(S["state"], 16 * 12)
            for q in range(4):
                pe.matmul(ps[:, 7, q * H:(q + 1) * H], pair_last[:, q, :], ea_col[:], start=True, stop=True)
            pe.transpose(ps[:, 7, 16:32], n0[:], E["ident"][:4 * H, :4 * H]).then_inc(S["n0_turned"], 1)

            def scores(u):
                h, c = units[u]
                r, w, o = ROWS[c], width(c), (h % 2) * HD
                qs = queries(c)
                if u >= 2:
                    pe.wait_ge(S["weights_done"], u - 1)
                    pe.wait_ge(S["probs_done"], u - 1)
                pe.matmul(ps[:r, u % 2, 0:r], E["ident"][:r, :r], (mask if c < PT_TILES else s_mask)[:r, :r],
                          start=True, stop=False, skip_group_check=True)
                pe.matmul(ps[:r, u % 2, 0:w], sel[:, h, 0:r], a[:, qs], start=False, stop=True,
                          skip_group_check=True).then_inc(S["bcast_done"], 1)
                pe.matmul(ps[:r, 2 + u % 2, 0:w], M["TR"][o:o + HD, AK + h // 2, tok(c)],
                          M["TR"][o:o + HD, AQ + h // 2, qs], start=True, stop=True).then_inc(S["scores_done"], 1)

            def outputs(u):
                h, c = units[u]
                r = ROWS[c]
                pe.wait_ge(S["probs_done"], u + 1)
                if c == 0 and h >= 2:
                    pe.wait_ge(S["out_copied"], h - 1)
                if c < PT_TILES:
                    for t in range(c, PT_TILES):
                        mm = pe.matmul(ps[:, 4 + h % 2, t * (HD + 1):(t + 1) * (HD + 1)],
                                       pr[:r, u % 2, (t - c) * P:(t - c + 1) * P], M["VA"][:r, c, h, :],
                                       start=(c == 0 and t == 0), stop=(c == t), skip_group_check=True)
                    mm.then_inc(S["pe_step"], 1)
                else:
                    out = ps[:NS, 4 + h % 2, PT_TILES * (HD + 1):TILES * (HD + 1)]
                    pe.matmul(out, pr[:NS, u % 2, 0:NS], M["VA"][:NS, c, h, :], start=False, stop=False,
                              skip_group_check=True).then_inc(S["pe_step"], 1)
                    for q in range(4):
                        mm = pe.matmul(out, qm[:, h, q, :], c0[:, q, h, :], start=False, stop=(q == 3),
                                       skip_group_check=True)
                    mm.then_inc(S["out_whole"], 1)

            pe.wait_ge(S["query_ready"], H)
            for u in range(len(units) + 1):
                if u < len(units):
                    scores(u)
                if u >= 1:
                    outputs(u - 1)
            pe.wait_ge(S["keys_ready"], H)
            for h in range(H):
                for t in range(PT_TILES):
                    mm = pe.matmul(ps[:HD, 6, h * (HD + 1):(h + 1) * (HD + 1)], M["KA"][:, t, h * HD:(h + 1) * HD],
                                   M["VA"][:, t, h, :], start=(h == 0 and t == 0), stop=(t == PT_TILES - 1),
                                   skip_group_check=True)
            mm.then_inc(S["p_state_done"], 1)
            pe.wait_ge(S["weights_done"], len(units))
            for h in range(H):
                if h >= 2:
                    pe.wait_ge(S["s_state_added"], 2 * (h - 1))
                for q in range(4):
                    mm = pe.matmul(ps[:, h % 2, q * (HD + 1):(q + 1) * (HD + 1)],
                                   km[:, h, 2 * q:2 * q + 2, :].rearrange("p j d -> p (j d)"),
                                   M["VA"][:NS, PT_TILES, h, :], start=True, stop=True)
                mm.then_inc(S["s_state_done"], 1)
            pe.wait_ge(S["p_state_copied"], 1)
            pe.wait_ge(S["s_state_added"], 2 * H)
            pe.wait_ge(S["out_copied"], H)
            pe.transpose(ps[:H, 4, 0:HD], pc[:, :, HD], E["ident"][:HD, :HD])
            pe.transpose(ps[:4 * H, 4, P:2 * P], c0[:, :, :, HD].rearrange("p q h -> p (q h)"), E["ident"][:]).then_inc(S["n_turned"], 1)
            head_tensor(pe, E, S, hA, 2)


def gla(nc, E, M, l, I, O, C):
    NCH = SEQ // CHUNK
    sems = HEAD_SEMS + ("consts params states cleared dve_step low_ready pre_done pre_out y_ready act_to_dve "
                        "sums_ready exps_done factors_ready query_ready att_done att_ready keys_turned keys_ready "
                        "update_done state_new out_done out_copied s_query_ready s_keys_ready s_update_done "
                        "s_state_new gate_done stored")
    with stage(nc, "gl", sems) as (S, sb, block):
        HB = head_buffers(sb)
        keep = sb("keep", [P, NT])
        mask = sb("mask", [P, P])
        s_mask = sb("s_mask", [NS, NS])
        head = sb("head", [P, H])
        head_cols = sb("head_cols", [P, W4])
        req_tok = sb("req_tok", [P, DEC_BATCH, NS])
        tok_req = sb("tok_req", [NS, DEC_BATCH])
        w2 = sb("w2", [RANK, P])
        bias = sb("bias", [P, 1])
        gain = sb("gain", [P, W4])
        low = sb("low", [RANK, NT])
        y = sb("y", [P, NT])
        sp_ = sb("softplus", [P, NT])
        bsum = sb("bsum", [P, NT])
        mid = sb("mid", [P, NT])
        rest = sb("rest", [P, NT])
        e1 = sb("e1", [P, NT])
        whole = sb("whole", [P, NCH + DEC_BATCH])
        state = sb("state", [P, NCH + 1, W4])
        s_state = sb("s_state", [P, DEC_BATCH, W4])
        upd = sb("upd", [P, W4])
        qq = sb("qq", [P, NT])
        qi = sb("qi", [P, NT])
        kk = sb("kk", [P, NT])
        kd = sb("kd", [P, NT])
        qh = sb("qh", [P, 2, H, P])
        att = sb("att", [P, 2, H, P])
        kdt = sb("kdt", [P, TILES, P])
        s_qi = sb("s_qi", [P, DEC_BATCH, NS])
        s_kd = sb("s_kd", [NS, DEC_BATCH, P])
        hB = sb("hB", [P, TILES, W4])
        ps = E["ps"]

        def chunks(x):
            return (x[:, 0:SEQ].rearrange("p (c t) -> p c t", t=CHUNK),
                    x[:, SEQ:NT].rearrange("p (c t) -> p c t", t=DEC_SEQ))

        @block.sync
        def _(sp):
            for dst, n in ((keep, "keep_b"), (mask, "gla_mask"), (s_mask, "s_gla_mask"), (head, "gla_head"),
                           (head_cols, "gla_cols"), (req_tok, "request_tokens"), (tok_req, "token_request")):
                sp.dma_start(dst[:], C[n]).then_inc(S["consts"], 16)
            sp.dma_start(w2[:], I["w_gla_a2"][bass.ds(l, 1)].rearrange("o r n -> (o r) n")).then_inc(S["params"], 16)
            sp.dma_start(bias[:], layer_col(I["b_gla_a"], l)).then_inc(S["params"], 16)
            sp.dma_start(gain[:], layer_row(I["g_head_b"], l)).then_inc(S["params"], 16)
            sp.wait_ge(S["cleared"], 2)
            for h in range(H):
                sp.dma_start(s_state[h * DK_B:(h + 1) * DK_B, :, h * HD:(h + 1) * HD],
                             I["state_gla_s"][bass.ds(l, 1), :, h].rearrange("o r d e -> d (o r) e")).then_inc(S["states"], 16)
            n = 0
            sp.wait_ge(S["state_new"], NCH)
            for h in range(H):
                sp.dma_start(O["p_gla_s"][bass.ds(l, 1), 0, h].rearrange("o d e -> (o d) e"),
                             state[h * DK_B:(h + 1) * DK_B, NCH, h * HD:(h + 1) * HD]).then_inc(S["stored"], 16)
            sp.wait_ge(S["s_state_new"], DEC_BATCH)
            for h in range(H):
                sp.dma_start(O["s_gla_s"][bass.ds(l, 1), :, h].rearrange("o r d e -> d (o r) e"),
                             s_state[h * DK_B:(h + 1) * DK_B, :, h * HD:(h + 1) * HD]).then_inc(S["stored"], 16)
            sp.wait_ge(S["stored"], 16 * 2 * H)

        @block.vector
        def _(dve):
            step = stepper(dve, S["dve_step"])
            dve.memset(state[:, 0, :], 0.0).then_inc(S["cleared"], 1)
            dve.memset(s_state[:], 0.0).then_inc(S["cleared"], 1)
            dve.tensor_copy(low[:], M["gates"][LOWRANK:LOWRANK + RANK, :]).then_inc(S["low_ready"], 1)
            dve.wait_ge(S["params"], 48)
            dve.wait_ge(S["consts"], 16 * 7)
            dve.wait_ge(S["pre_done"], 1)
            for half in range(2):
                dve.tensor_scalar(y[:, half * HALF:(half + 1) * HALF], ps[:, half, 0:HALF], bias[:, 0:1], None,
                                  ALU.add).then_inc(S["y_ready"], 1)
            dve.wait_ge(S["y_ready"], 2)
            dve.wait_ge(S["act_to_dve"], 3)
            step(dve.scalar_tensor_tensor(y[:], y[:], 0.0, sp_[:], ALU.min, ALU.subtract))
            step(dve.tensor_scalar(y[:], y[:], 1.0 / TAU, None, ALU.mult))
            step(dve.tensor_tensor_scan(bsum[:], keep[:], y[:], 0.0, ALU.mult, ALU.add))
            for v, mv, rv, size in ((chunks(bsum)[0], chunks(mid)[0], chunks(rest)[0], CHUNK),
                                    (chunks(bsum)[1], chunks(mid)[1], chunks(rest)[1], DEC_SEQ)):
                shape = [P, v.shape[1], size]
                step(dve.tensor_tensor(mv, v, v[:, :, size // 2 - 1:size // 2].to_broadcast(shape), ALU.subtract))
                step(dve.tensor_tensor(rv, v[:, :, size - 1:size].to_broadcast(shape), v, ALU.subtract))
            step(dve.tensor_copy(whole[:, 0:NCH], bsum[:, CHUNK - 1:SEQ:CHUNK]))
            dve.tensor_copy(whole[:, NCH:], bsum[:, SEQ + DEC_SEQ - 1:NT:DEC_SEQ]).then_inc(S["sums_ready"], 1)
            for n, (dst, x, e) in enumerate(((qi, BQ, y), (qq, BQ, e1), (kk, BK, mid), (kd, BK, rest))):
                dve.wait_ge(S["exps_done"], n + 1)
                dve.tensor_tensor(dst[:], M["TR"][:, x, :], e[:], ALU.mult).then_inc(S["factors_ready"], 1)
            dve.wait_ge(S["factors_ready"], 4)
            dve.wait_ge(S["exps_done"], 5)
            dve.wait_ge(S["states"], 16 * H)

            def spread_query(t):
                r = ROWS[t]
                if t >= 2:
                    dve.wait_ge(S["att_done"], t - 1)
                dve.tensor_tensor(qh[:, t % 2, :, 0:r], qq[:, tok(t)].unsqueeze(1).to_broadcast([P, H, r]),
                                  head[:].unsqueeze(2).to_broadcast([P, H, r]), ALU.mult).then_inc(S["query_ready"], 1)

            spread_query(0)
            for t, r in enumerate(ROWS):
                if t + 1 < TILES:
                    spread_query(t + 1)
                dve.wait_ge(S["att_done"], t + 1)
                if t >= 2:
                    dve.wait_ge(S["out_done"], t - 1)
                mk = (mask if t < PT_TILES else s_mask)[:r, :r]
                dve.tensor_tensor(att[:r, t % 2, :, 0:r], ps[:r, t % 2, 0:H * r].rearrange("p (h t) -> p h t", h=H),
                                  mk.unsqueeze(1).to_broadcast([r, H, r]), ALU.mult).then_inc(S["att_ready"], 1)
                dve.wait_ge(S["keys_turned"], t + 1)
                dve.tensor_copy(kdt[:r, t, :], ps[:r, 2 + t % 2, 0:P]).then_inc(S["keys_ready"], 1)
                if t < PT_TILES:
                    for j in range(2):
                        c = 2 * t + j
                        dve.wait_ge(S["update_done"], c + 1)
                        step(dve.tensor_tensor(upd[:], ps[:, 4 + j, 0:W4], head_cols[:], ALU.mult))
                        dve.scalar_tensor_tensor(state[:, c + 1, :], state[:, c, :], whole[:, c:c + 1], upd[:],
                                                 ALU.mult, ALU.add).then_inc(S["state_new"], 1)
                        dve.wait_ge(S["state_new"], c + 1)
            dve.tensor_tensor(s_qi[:], qi[:, SEQ:NT].unsqueeze(1).to_broadcast([P, DEC_BATCH, NS]), req_tok[:],
                              ALU.mult).then_inc(S["s_query_ready"], 1)
            dve.wait_ge(S["keys_ready"], TILES)
            dve.tensor_tensor(s_kd[:], kdt[:NS, PT_TILES, :].unsqueeze(1).to_broadcast([NS, DEC_BATCH, P]),
                              tok_req[:].unsqueeze(2).to_broadcast([NS, DEC_BATCH, P]), ALU.mult).then_inc(S["s_keys_ready"], 1)
            dve.wait_ge(S["out_done"], TILES)
            for s in range(DEC_BATCH):
                dve.wait_ge(S["s_update_done"], s + 1)
                step(dve.tensor_tensor(upd[:], ps[:, 4 + s % 2, 0:W4], head_cols[:], ALU.mult))
                dve.scalar_tensor_tensor(s_state[:, s, :], s_state[:, s, :], whole[:, NCH + s:NCH + s + 1], upd[:],
                                         ALU.mult, ALU.add).then_inc(S["s_state_new"], 1)
                dve.wait_ge(S["s_state_new"], s + 1)
            dve.wait_ge(S["gate_done"], 2)
            for rs, ts in PARTS:
                nt = ts.stop - ts.start
                step(dve.tensor_tensor(M["BVG"][rs, ts, W4:], M["BVG"][rs, ts, W4:],
                                       gain[rs].unsqueeze(1).to_broadcast([rs.stop, nt, W4]), ALU.mult))
            dve.wait_ge(S["out_copied"], TILES)
            head_vector(dve, S, HB, hB, M["BVG"][:, :, W4:])

        @block.scalar
        def _(act):
            for rs, ts in PARTS:
                act.activation(M["BVG"][rs, ts, W4:], M["BVG"][rs, ts, W4:], ACT.Silu).then_inc(S["gate_done"], 1)
            act.wait_ge(S["y_ready"], 2)
            act.preload_act_table_set("natural_log_exp_and_others")
            act.activation(sp_[:], y[:], ACT.Abs).then_inc(S["act_to_dve"], 1)
            act.wait_ge(S["act_to_dve"], 1)
            act.activation(sp_[:], sp_[:], ACT.Exp, scale=-1.0).then_inc(S["act_to_dve"], 1)
            act.wait_ge(S["act_to_dve"], 2)
            act.activation(sp_[:], sp_[:], ACT.Ln, bias=1.0).then_inc(S["act_to_dve"], 1)
            act.wait_ge(S["sums_ready"], 1)
            act.activation(y[:], bsum[:], ACT.Exp).then_inc(S["exps_done"], 1)
            act.activation(e1[:], mid[:], ACT.Exp).then_inc(S["exps_done"], 1)
            act.wait_ge(S["exps_done"], 2)
            act.activation(mid[:], mid[:], ACT.Exp, scale=-1.0).then_inc(S["exps_done"], 1)
            act.activation(rest[:], rest[:], ACT.Exp).then_inc(S["exps_done"], 1)
            act.activation(whole[:], whole[:], ACT.Exp).then_inc(S["exps_done"], 1)
            for t, r in enumerate(ROWS):
                act.wait_ge(S["out_done"], t + 1)
                act.activation(hB[:r, t, :], ps[:r, 6 + t % 2, 0:W4], ACT.Copy).then_inc(S["out_copied"], 1)
            head_scalar_root(act, E, S, HB)
            head_scalar_out(act, E, M, S, 2, 2)

        @block.tensor
        def _(pe):
            pe.wait_ge(S["params"], 48)
            pe.wait_ge(S["low_ready"], 1)
            for half in range(2):
                mm = pe.matmul(ps[:, half, 0:HALF], w2[:], low[:, half * HALF:(half + 1) * HALF], start=True, stop=True)
            mm.then_inc(S["pre_done"], 1)
            pe.wait_ge(S["factors_ready"], 4)

            def inside(t):
                r = ROWS[t]
                if t >= 2:
                    pe.wait_ge(S["att_ready"], t - 1)
                    pe.wait_ge(S["keys_ready"], t - 1)
                pe.wait_ge(S["query_ready"], t + 1)
                rhs = qh[:, t % 2, :, 0:r]
                out = ps[:r, t % 2, 0:H * r].rearrange("p (h t) -> p h t", h=H)
                pe.matmul(out, kk[:, tok(t)], rhs, start=True, stop=True).then_inc(S["att_done"], 1)
                pe.transpose(ps[:r, 2 + t % 2, 0:P], kd[:, tok(t)], E["ident"][:]).then_inc(S["keys_turned"], 1)

            inside(0)
            for t, r in enumerate(ROWS):
                if t + 1 < TILES:
                    inside(t + 1)
                pe.wait_ge(S["keys_ready"], t + 1)
                if t < PT_TILES:
                    for j in range(2):
                        c = 2 * t + j
                        if c >= 2:
                            pe.wait_ge(S["state_new"], c - 1)
                        pe.matmul(ps[:, 4 + j, 0:W4], kdt[j * CHUNK:(j + 1) * CHUNK, t, :],
                                  M["BVG"][j * CHUNK:(j + 1) * CHUNK, t, 0:W4], start=True, stop=True).then_inc(S["update_done"], 1)
                pe.wait_ge(S["att_ready"], t + 1)
                if t >= 2:
                    pe.wait_ge(S["out_copied"], t - 1)
                for h in range(H):
                    pe.matmul(ps[:r, 6 + t % 2, h * HD:(h + 1) * HD], att[:r, t % 2, h, 0:r],
                              M["BVG"][:r, t, h * HD:(h + 1) * HD], start=(h == 0), stop=False, skip_group_check=True)
                if t < PT_TILES:
                    for j in range(2):
                        c = 2 * t + j
                        if c >= 1:
                            pe.wait_ge(S["state_new"], c)
                        else:
                            pe.wait_ge(S["cleared"], 1)
                        mm = pe.matmul(ps[j * CHUNK:(j + 1) * CHUNK, 6 + t % 2, 0:W4], qi[:, c * CHUNK:(c + 1) * CHUNK],
                                       state[:, c, :], start=False, stop=True, skip_group_check=True)
                else:
                    pe.wait_ge(S["s_query_ready"], 1)
                    pe.wait_ge(S["states"], 16 * H)
                    for s in range(DEC_BATCH):
                        mm = pe.matmul(ps[:NS, 6 + t % 2, 0:W4], s_qi[:, s, :], s_state[:, s, :], start=False,
                                       stop=(s == DEC_BATCH - 1), skip_group_check=True)
                mm.then_inc(S["out_done"], 1)
            pe.wait_ge(S["s_keys_ready"], 1)
            pe.wait_ge(S["state_new"], NCH)
            for s in range(DEC_BATCH):
                if s >= 2:
                    pe.wait_ge(S["s_state_new"], s - 1)
                pe.matmul(ps[:, 4 + s % 2, 0:W4], s_kd[:, s, :], M["BVG"][:NS, PT_TILES, 0:W4], start=True,
                          stop=True).then_inc(S["s_update_done"], 1)
            head_tensor(pe, E, S, hB, 2)


def rotary(nc, E, M, l, O, C):
    with stage(nc, "ro", "consts dve_step turned_q turned_k act_out dve_out rotated") as (S, sb, block):
        cos = sb("cos", [P, TILES, ROPE_HALF])
        sin = sb("sin", [P, TILES, ROPE_HALF])
        tmp = sb("tmp", [P, 4, TILES, 2 * H, ROPE_HALF])

        @block.sync
        def _(sp):
            sp.dma_start(cos[:], C["cos"]).then_inc(S["consts"], 16)
            sp.dma_start(sin[:], C["sin"]).then_inc(S["consts"], 16)

        @block.vector
        def _(dve):
            step = stepper(dve, S["dve_step"])
            dve.wait_ge(S["consts"], 32)
            for rs, ts in PARTS:
                for t in range(ts.start, ts.stop):
                    v = M["CQK"][rs, t, :].rearrange("p (h d) -> p h d", h=2 * H)
                    shape = [rs.stop, 2 * H, ROPE_HALF]
                    x1, x2 = v[:, :, 0:ROPE_HALF], v[:, :, ROPE_HALF:2 * ROPE_HALF]
                    for k, (x, f) in enumerate(((x1, cos), (x2, sin), (x1, sin), (x2, cos))):
                        ins = dve.tensor_tensor(tmp[rs, k, t], x, f[rs, t, :].unsqueeze(1).to_broadcast(shape), ALU.mult)
                        if k == 3:
                            step(ins)
                        else:
                            ins.then_inc(S["dve_out"], 1)
            dve.wait_ge(S["dve_out"], 3 * TILES)
            for rs, ts in PARTS:
                for a, b, o, op in ((0, 1, 0, ALU.subtract), (2, 3, ROPE_HALF, ALU.add)):
                    v = M["CQK"][rs, ts, :].rearrange("p t (h d) -> p t h d", h=2 * H)[:, :, :, o:o + ROPE_HALF]
                    dve.tensor_tensor(v, tmp[rs, a, ts], tmp[rs, b, ts], op).then_inc(S["rotated"], 1)
            for n in range(2 * TILES):
                t, pair = n // 2, n % 2
                dve.wait_ge(S["turned_k"], n + 1)
                dve.tensor_copy(M["CKT"][:, pair, tok(t)], E["ps"][:, 2 + n % 2, 0:ROWS[t]]).then_inc(S["dve_out"], 1)

        @block.scalar
        def _(act):
            for n in range(2 * TILES):
                t, pair = n // 2, n % 2
                act.wait_ge(S["turned_q"], n + 1)
                act.activation(M["CQT"][:, pair, tok(t)], E["ps"][:, n % 2, 0:ROWS[t]], ACT.Copy,
                               scale=QK_SCALE).then_inc(S["act_out"], 1)

        @block.tensor
        def _(pe):
            pe.wait_ge(S["rotated"], 4)
            for n in range(2 * TILES):
                t, pair = n // 2, n % 2
                r = ROWS[t]
                if n >= 2:
                    pe.wait_ge(S["act_out"], n - 1)
                    pe.wait_ge(S["dve_out"], 3 * TILES + n - 1)
                pe.transpose(E["ps"][:, n % 2, 0:r], M["CQK"][:r, t, pair * P:(pair + 1) * P],
                             E["ident"][:r, :r]).then_inc(S["turned_q"], 1)
                pe.transpose(E["ps"][:, 2 + n % 2, 0:r], M["CQK"][:r, t, W4 + pair * P:W4 + (pair + 1) * P],
                             E["ident"][:r, :r]).then_inc(S["turned_k"], 1)


def prompt_attention(nc, E, M, l, kind, qT, kT, v, chunk, I, O, C):
    sems = ("consts scores_done z_ready maxima negated sums_done inverse act_step dve_step scanned a_ready "
            "turned pt_act pt_dve out_done out_copied stored")
    window = kind == "window"
    with stage(nc, "pw" if window else "pd", sems) as (S, sb, block):
        ps = E["ps"]
        mask = sb("mask", [P, SEQ if window else P])
        z = sb("z", [P, H, SEQ])
        f = sb("f", [P, H, SEQ])
        ones = sb("ones", [P, SEQ])
        mx = sb("mx", [P, H])
        total = sb("total", [P, H])
        bias = sb("bias", [P, H])
        pT = sb("pT", [P, 2, SEQ])
        n_in = 1 if window else 2

        @block.sync
        def _(sp):
            sp.dma_start(mask[:], C["win_mask" if window else "strict_mask"]).then_inc(S["consts"], 16)
            if not window:
                sp.dma_start(bias[:], layer_row(I["b_sb"], l)).then_inc(S["consts"], 16)
            if window:
                n = 0
                for src, pn, sn in ((M["DKV"][:, :, 0:W4], "p_sb_k", "s_sb_k"), (M["DKV"][:, :, W4:], "p_sb_v", "s_sb_v"),
                                    (M["CV"][:], "p_win_v", "s_win_v"), (M["CQK"][:, :, W4:], "p_win_k", "s_win_k")):
                    po = O[pn][bass.ds(l, 1)].rearrange("o b (t p) h d -> p (o b t) (h d)", p=P)
                    so = O[sn][bass.ds(l, 1)].rearrange("o b t h d -> (o b t) (h d)")
                    sp.dma_start(po, src[:, 0:PT_TILES, :]).then_inc(S["stored"], 16)
                    sp.dma_start(so, src[:NS, PT_TILES, :]).then_inc(S["stored"], 16)
                    n += 2
                sp.wait_ge(S["stored"], 16 * n)

        @block.tensor
        def _(pe):
            for i in range(PT_TILES):
                w = (i + 1) * P
                if i > 0:
                    pe.wait_ge(S["z_ready"], i)
                for h in range(H):
                    o = (h % 2) * HD
                    mm = pe.matmul(ps[:, h, 0:w], qT[o:o + HD, h // 2, i * P:(i + 1) * P],
                                   kT[o:o + HD, h // 2, 0:w], start=True, stop=True)
                mm.then_inc(S["scores_done"], 1)
                pe.wait_ge(S["a_ready"], i + 1)

                def turn(h):
                    n = H * i + h
                    if n >= 2:
                        pe.wait_ge(S["pt_act"] if h % 2 == 0 else S["pt_dve"], (n - 2) // 2 + 1)
                    for c in range(i + 1):
                        mm = pe.transpose(ps[:, 4 + h % 2, c * P:(c + 1) * P], z[:, h, c * P:(c + 1) * P], E["ident"][:])
                    mm.then_inc(S["turned"], 1)

                turn(0)
                for h in range(H):
                    if h + 1 < H:
                        turn(h + 1)
                    n = H * i + h
                    pe.wait_ge(S["pt_act"] if h % 2 == 0 else S["pt_dve"], n // 2 + 1)
                    if h % 2 == 0 and i > 0:
                        pe.wait_ge(S["out_copied"], 2 * (i - 1) + h // 2 + 1)
                    o = (h % 2) * HD
                    for c in range(i + 1):
                        mm = pe.matmul(ps[o:o + HD, 6 + h // 2, 0:P], v[:, c, h * HD:(h + 1) * HD],
                                       pT[:, h % 2, c * P:(c + 1) * P], start=(c == 0), stop=(c == i))
                    mm.then_inc(S["out_done"], 1)

        @block.vector
        def _(dve):
            step = stepper(dve, S["dve_step"])
            dve.memset(ones[:], 1.0).then_inc(S["inverse"], 1)
            dve.wait_ge(S["consts"], 16 * n_in)
            for i in range(PT_TILES):
                w = (i + 1) * P
                dve.wait_ge(S["scores_done"], i + 1)
                if i > 0:
                    dve.wait_ge(S["turned"], H * i)
                if window:
                    dve.tensor_tensor(z[:, :, 0:w], ps[:, 0:H, 0:w],
                                      mask[:, SEQ - w:SEQ].unsqueeze(1).to_broadcast([P, H, w]), ALU.add).then_inc(S["z_ready"], 1)
                    dve.wait_ge(S["z_ready"], i + 1)
                    step(dve.tensor_reduce(mx[:], z[:, :, 0:w], AX.X, ALU.max))
                    dve.tensor_scalar(mx[:], mx[:], -1.0, None, ALU.mult).then_inc(S["negated"], 1)
                    dve.wait_ge(S["sums_done"], H * (i + 1))
                    step(dve.reciprocal(total[:], total[:]))
                    dve.tensor_tensor(z[:, :, 0:w], z[:, :, 0:w], total[:].unsqueeze(2).to_broadcast([P, H, w]),
                                      ALU.mult).then_inc(S["a_ready"], 1)
                else:
                    dve.tensor_tensor(z[:, :, 0:w], ps[:, 0:H, 0:w], bias[:, 0:H].unsqueeze(2).to_broadcast([P, H, w]),
                                      ALU.add).then_inc(S["z_ready"], 1)
                    dve.wait_ge(S["z_ready"], i + 1)
                    dve.tensor_tensor(z[:, :, w - P:w], z[:, :, w - P:w], mask[:].unsqueeze(1).to_broadcast([P, H, P]),
                                      ALU.add).then_inc(S["maxima"], 1)
                    dve.wait_ge(S["maxima"], i + 1)
                    dve.wait_ge(S["act_step"], 3 * (i + 1))
                    step(dve.scalar_tensor_tensor(f[:, :, 0:w], z[:, :, 0:w], 0.0, f[:, :, 0:w], ALU.max, ALU.add))
                    for h in range(H):
                        step(dve.tensor_tensor_scan(f[:, h, 0:w][:, ::-1], ones[:, 0:w], f[:, h, 0:w][:, ::-1], 0.0,
                                                    ALU.mult, ALU.add))
                    dve.tensor_tensor(z[:, :, 0:w], z[:, :, 0:w], f[:, :, 0:w], ALU.subtract).then_inc(S["scanned"], 1)
                for h in range(1, H, 2):
                    n = H * i + h
                    dve.wait_ge(S["turned"], n + 1)
                    if n >= 2:
                        dve.wait_ge(S["out_done"], n - 1)
                    dve.tensor_copy(pT[:, 1, 0:w], ps[:, 5, 0:w]).then_inc(S["pt_dve"], 1)

        @block.scalar
        def _(act):
            act.preload_act_table_set("natural_log_exp_and_others")
            for i in range(PT_TILES):
                w = (i + 1) * P
                if window:
                    act.wait_ge(S["negated"], i + 1)
                    for h in range(H):
                        act.activation(z[:, h, 0:w], z[:, h, 0:w], ACT.Exp, bias=mx[:, h:h + 1],
                                       accum_out=total[:, h:h + 1]).then_inc(S["sums_done"], 1)
                else:
                    act.wait_ge(S["maxima"], i + 1)
                    act.activation(f[:, :, 0:w], z[:, :, 0:w], ACT.Abs).then_inc(S["act_step"], 1)
                    act.wait_ge(S["act_step"], 3 * i + 1)
                    act.activation(f[:, :, 0:w], f[:, :, 0:w], ACT.Exp, scale=-1.0).then_inc(S["act_step"], 1)
                    act.wait_ge(S["act_step"], 3 * i + 2)
                    act.activation(f[:, :, 0:w], f[:, :, 0:w], ACT.Ln, bias=1.0).then_inc(S["act_step"], 1)
                    act.wait_ge(S["scanned"], i + 1)
                    act.activation(z[:, :, 0:w], z[:, :, 0:w], ACT.Exp).then_inc(S["a_ready"], 1)
                for h in range(0, H, 2):
                    n = H * i + h
                    act.wait_ge(S["turned"], n + 1)
                    if n >= 2:
                        act.wait_ge(S["out_done"], n - 1)
                    act.activation(pT[:, 0, 0:w], ps[:, 4, 0:w], ACT.Copy).then_inc(S["pt_act"], 1)
                for pair in range(2):
                    act.wait_ge(S["out_done"], H * i + 2 * pair + 2)
                    act.activation(M["mixT"][:, chunk + pair, i * P:(i + 1) * P], ps[:, 6 + pair, 0:P],
                                   ACT.Copy).then_inc(S["out_copied"], 1)


SLOTS = 4


def sample_attention(nc, E, M, l, I, C):
    ps = E["ps"]
    DQT, DKT = M["TR"][:, DQ:DQ + 2, :], M["TR"][:, DK:DK + 2, :]
    MAXK = N_PAGES * P
    passes = []
    unit0 = chunk0 = 0
    for g in range(GROUPS):
        for kind in ("stick", "window"):
            tiles = WIN_TILES if kind == "window" else N_PAGES
            cks = [(c, min(UT, tiles - c)) for c in range(0, tiles, UT)]
            passes.append(dict(kind=kind, window=kind == "window", g=g, chunks=cks, unit0=unit0, chunk0=chunk0,
                               sticks=g + 1,
                               keys=tiles * P, NC=len(cks),
                               units=[(k, j) for k in range(len(cks)) for j in range(SG)]))
            unit0 += SG * len(cks)
            chunk0 += len(cks) + 1
    NP_ = len(passes)
    units = [(p, k, j, q["chunks"][k][1]) for p, q in enumerate(passes) for k, j in q["units"]]
    ORDER = []
    for p in range(NP_ + 2):
        if p < NP_:
            ORDER.append(("keys", p))
        if p == 0:
            continue
        if p >= 2:
            ORDER.append(("gather", p - 2))
        if p - 1 < NP_:
            ORDER.append(("values", p - 1))

    def pt_before(p, odd):
        return sum((q["NC"] + 1 + (0 if odd else 1)) // 2 for q in passes[:p])

    sems = ("consts bias_loaded k0 k1 k2 k3 v0 v1 v2 v3 spread q_ready bias_turned bias_ready turned kt_act kt_dve "
            "scores_done z_ready maxed negated abs_done exp_done ln_done f_done sum_done scanned a_ready inv_done "
            "pt_turned pt_act pt_dve out_units out_done rows_ready gathered out_copied ones_ready pages_moved")
    with stage(nc, "sa", sems) as (S, sb, block):
        ksem, vsem = (S["k0"], S["k1"], S["k2"], S["k3"]), (S["v0"], S["v1"], S["v2"], S["v3"])
        kn = sb("kn", [P, SLOTS, UT, W4])
        vn = sb("vn", [P, SLOTS, UT, W4])
        kt = sb("kt", [P, 2, 2, UT * P])
        z = sb("z", [P, 2, MAXK + NS])
        f = sb("f", [P, MAXK + NS])
        one = sb("one", [P, 1])
        win_mask = sb("win_mask", [P, WIN_TILES * P])
        pT = sb("pT", [P, 2, UT * P])
        new_mask = sb("new_mask", [P, 2, GROUPS, NS])
        head_cols = sb("head_cols", [P, W4])
        gather = sb("gather", [P, SG * DEC_SEQ])
        pair_head = sb("pair_head", [P, 2, H])
        bias_rows = sb("bias_rows", [H, P])
        b = sb("b", [H, 1])
        bcol = sb("bcol", [P, 1])
        qb = sb("qb", [P, NP_, 2, SG, H, DEC_SEQ])
        mx = sb("mx", [P, NP_])
        total = sb("total", [P, NP_])
        rows = sb("rows", [P, W4])

        def load_unit(eng, values, n):
            p, k, j, nt = units[n]
            q = passes[p]
            buf, sem = (vn, vsem[n % SLOTS]) if values else (kn, ksem[n % SLOTS])
            c0, _ = q["chunks"][k]
            by_sp = eng is nc.sync
            if q["window"]:
                if not by_sp:
                    return
                cache = I["cache_win_v"] if values else I["cache_win_k"]
                rows_ = cache[bass.ds(l, 1), SG * q["g"] + j].rearrange("o r n d -> (o r) (n d)")
                far = max(0, min(FAR_TILES - c0, nt))
                if far:
                    src = rows_[c0 * 2 * P:(c0 + far) * 2 * P, :].rearrange("(a b i) x -> a b (i x)", b=16 // far, i=far)
                    eng.dma_start(buf[:, n % SLOTS, 0:far, :].rearrange("p i x -> p (i x)"),
                                  src[:, 0:8 // far]).then_inc(sem, 16)
                if far < nt:
                    r0 = PAST_LEN - NEAR + (c0 + far - FAR_TILES) * P
                    src = rows_[r0:r0 + (nt - far) * P, :].rearrange("(p i) x -> p (i x)", p=P)
                    eng.dma_start(buf[:, n % SLOTS, far:nt, :].rearrange("p i x -> p (i x)"), src).then_inc(sem, 16)
            else:
                cache = I["cache_sb_v"] if values else I["cache_sb_k"]
                first, half = (nt // 2, nt - nt // 2) if by_sp else (0, nt // 2)
                at = (SG * q["g"] + j) * N_PAGES + c0 + first
                _, pages = nc.values_load_multi_w_load_instructions(
                    E["pages"][0:1, at:at + half], engines=(eng.engine,), min_val=0, max_val=DEPTH * N_POOL - 1,
                    skip_runtime_bounds_check_because="the page table numbers pages of the pool")
                for i, page in enumerate(pages, first):
                    src = cache.rearrange("l q n h d -> (l q) n (h d)")[bass.ds(page, 1)].rearrange("o n x -> (o n) x")
                    eng.dma_start(buf[:, n % SLOTS, i, :], src).then_inc(sem, 16)

        def loads(n):
            p, k, j, nt = units[n]
            if not passes[p]["window"]:
                return nt
            c0, _ = passes[p]["chunks"][k]
            return int(c0 < FAR_TILES) + int(c0 + nt > FAR_TILES)

        def arrived(eng, sems_, n):
            eng.wait_ge(sems_[n % SLOTS], 16 * sum(loads(x) for x in range(n % SLOTS, n + 1, SLOTS)))

        @block.sync
        def _(sp):
            for dst, src in ((new_mask[:, 0], "s_win_new"), (new_mask[:, 1], "s_sb_new"), (head_cols[:], "head_cols"),
                             (gather[:], "gather_rows"), (pair_head[:], "pair_head"), (bias_rows[:], "bias_rows"),
                             (win_mask[:], "s_win_mask")):
                sp.dma_start(dst, C[src]).then_inc(S["consts"], 16)
            sp.dma_start(b[:], layer_col(I["b_sb"], l)).then_inc(S["bias_loaded"], 16)
            nc.disable_value_cache = True
            for n in range(SLOTS):
                load_unit(sp, False, n)
            for n in range(SLOTS):
                load_unit(sp, True, n)
            for what, p in ORDER:
                if what == "gather":
                    continue
                q = passes[p]
                for n in range(q["unit0"], q["unit0"] + len(q["units"])):
                    if n + SLOTS < len(units):
                        sp.wait_ge(S["turned"] if what == "keys" else S["out_units"], n + 1)
                        load_unit(sp, what == "values", n + SLOTS)
            nc.disable_value_cache = False

        @block.tensor
        def _(pe):
            pe.wait_ge(S["consts"], 16 * 7)
            pe.wait_ge(S["bias_loaded"], 16)
            pe.matmul(ps[:, 7, 0:1], bias_rows[:], b[:], start=True, stop=True).then_inc(S["bias_turned"], 1)

            def turn(n):
                arrived(pe, ksem, n)
                if n >= 2:
                    pe.wait_ge(S["kt_act"], n - 1)
                    pe.wait_ge(S["kt_dve"], n - 1)
                for pair in range(2):
                    for i in range(units[n][3]):
                        mm = pe.transpose(ps[:, 2 * (n % 2) + pair, i * P:(i + 1) * P],
                                          kn[:, n % SLOTS, i, pair * P:(pair + 1) * P], E["ident"][:])
                mm.then_inc(S["turned"], 1)

            def scores(n):
                p, k, j, nt = units[n]
                kc = passes[p]["chunk0"] + k
                pe.wait_ge(S["kt_act"], n + 1)
                pe.wait_ge(S["kt_dve"], n + 1)
                if j == 0 and kc >= 2:
                    pe.wait_ge(S["z_ready"], kc - 1)
                for pair in range(2):
                    mm = pe.matmul(ps[32 * j:32 * j + 32, 4 + kc % 2, 0:nt * P],
                                   qb[:, p, pair, j].rearrange("p h q -> p (h q)"), kt[:, n % 2, pair, 0:nt * P],
                                   start=(pair == 0), stop=(pair == 1), tile_position=(0, 32 * j))
                mm.then_inc(S["scores_done"], 1)

            def keys(p):
                q = passes[p]
                first, last = q["unit0"], q["unit0"] + len(q["units"])
                turn(first)
                pe.wait_ge(S["q_ready"], 2 * NP_)
                for n in range(first, last):
                    if n + 1 < last:
                        turn(n + 1)
                    scores(n)
                kc = q["chunk0"] + q["NC"]
                kT = M["CKT"] if q["window"] else DKT
                pe.wait_ge(S["z_ready"], kc - 1)
                for j in range(SG):
                    for pair in range(2):
                        mm = pe.matmul(ps[32 * j:32 * j + 32, 4 + kc % 2, 0:NS],
                                       qb[:, p, pair, j].rearrange("p h q -> p (h q)"), kT[:, pair, SEQ:NT],
                                       start=(pair == 0), stop=(pair == 1), tile_position=(0, 32 * j))
                mm.then_inc(S["scores_done"], 1)

            def values(p):
                q = passes[p]
                NC = q["NC"]
                pe.wait_ge(S["a_ready"], p + 1)

                def turn_p(k):
                    c0, nt = q["chunks"][k] if k < NC else (q["keys"] // P, 1)
                    if k >= 2:
                        pe.wait_ge(S["pt_act"] if k % 2 == 0 else S["pt_dve"], pt_before(p, k % 2) + (k - 2) // 2 + 1)
                    for i in range(nt):
                        cs = slice((c0 + i) * P, (c0 + i) * P + (P if k < NC else NS))
                        mm = pe.transpose(ps[:cs.stop - cs.start, k % 2, i * P:(i + 1) * P], z[:, p % 2, cs],
                                          E["ident"][:])
                    mm.then_inc(S["pt_turned"], 1)

                turn_p(0)
                if p >= 1:
                    pe.wait_ge(S["rows_ready"], p)
                for k in range(NC):
                    turn_p(k + 1)
                    pe.wait_ge(S["pt_act"] if k % 2 == 0 else S["pt_dve"], pt_before(p, k % 2) + k // 2 + 1)
                    for j in range(SG):
                        n = q["unit0"] + SG * k + j
                        arrived(pe, vsem, n)
                        for i in range(units[n][3]):
                            mm = pe.matmul(ps[32 * j:32 * j + 32, 6, 0:W4],
                                           pT[:, k % 2, i * P + 32 * j:i * P + 32 * j + 32], vn[:, n % SLOTS, i, :],
                                           start=(k == 0 and i == 0), stop=False, skip_group_check=True,
                                           tile_position=(0, 32 * j))
                        mm.then_inc(S["out_units"], 1)
                pe.wait_ge(S["pt_act"] if NC % 2 == 0 else S["pt_dve"], pt_before(p, NC % 2) + NC // 2 + 1)
                v_new = M["CV"][:NS, PT_TILES, :] if q["window"] else M["DKV"][:NS, PT_TILES, W4:]
                pe.matmul(ps[:, 6, 0:W4], pT[:NS, NC % 2, 0:P], v_new, start=False, stop=True,
                          skip_group_check=True).then_inc(S["out_done"], 1)

            def gather_rows(p):
                pe.wait_ge(S["rows_ready"], p + 1)
                if p >= 1:
                    pe.wait_ge(S["out_copied"], p)
                for pair in range(2):
                    mm = pe.matmul(ps[:, 7, pair * 32:pair * 32 + 32], rows[:, pair * P:(pair + 1) * P], gather[:],
                                   start=True, stop=True)
                mm.then_inc(S["gathered"], 1)

            for what, p in ORDER:
                if what == "keys":
                    keys(p)
                elif what == "values":
                    values(p)
                else:
                    gather_rows(p)

        def spread_over(steps, n_units, first):
            at = {}
            for i, s in enumerate(steps):
                at.setdefault(min(first + 2 * i, n_units - 1), []).append(s)
            return at

        @block.scalar
        def _(act):
            act.preload_act_table_set("natural_log_exp_and_others")
            nc.disable_value_cache = True
            for n in range(SLOTS):
                load_unit(act, False, n)
            for n in range(SLOTS):
                load_unit(act, True, n)

            def weigh(p):
                q = passes[p]
                zp, fp = z[:, p % 2, 0:q["keys"] + NS], f[:, 0:q["keys"] + NS]
                s = q["sticks"]

                def exp_window():
                    act.wait_ge(S["negated"], q["g"] + 1)
                    act.activation(zp, zp, ACT.Exp, bias=mx[:, p:p + 1], accum_out=total[:, p:p + 1]).then_inc(S["a_ready"], 1)

                def abs_():
                    act.wait_ge(S["z_ready"], q["chunk0"] + q["NC"] + 1)
                    if s > 1:
                        act.wait_ge(S["scanned"], s - 1)
                    act.activation(fp, zp, ACT.Abs).then_inc(S["abs_done"], 1)

                def exp_():
                    act.wait_ge(S["abs_done"], s)
                    act.activation(fp, fp, ACT.Exp, scale=-1.0).then_inc(S["exp_done"], 1)

                def ln_():
                    act.wait_ge(S["exp_done"], s)
                    act.activation(fp, fp, ACT.Ln, bias=1.0).then_inc(S["ln_done"], 1)

                def last():
                    act.wait_ge(S["scanned"], s)
                    act.activation(zp, zp, ACT.Exp).then_inc(S["a_ready"], 1)

                return [exp_window] if q["window"] else [abs_, exp_, ln_, lambda: None, lambda: None, last]

            def keys(p):
                q = passes[p]
                before = spread_over(weigh(p - 1), len(q["units"]), 1) if p >= 1 else {}
                for x in range(len(q["units"])):
                    n = q["unit0"] + x
                    w = units[n][3] * P
                    act.wait_ge(S["turned"], n + 1)
                    if n >= 2:
                        act.wait_ge(S["scores_done"], n - 1 + sum(r["unit0"] + len(r["units"]) <= n - 2 for r in passes))
                    act.activation(kt[:, n % 2, 0, 0:w], ps[:, 2 * (n % 2), 0:w], ACT.Copy).then_inc(S["kt_act"], 1)
                    if n + SLOTS < len(units):
                        load_unit(act, False, n + SLOTS)
                    for step in before.get(x, ()):
                        step()

            def values(p):
                q = passes[p]
                NC = q["NC"]
                if p == NP_ - 1:
                    for step in weigh(p):
                        step()

                def copy(k):
                    w, r = (q["chunks"][k][1] * P, P) if k < NC else (P, NS)
                    act.wait_ge(S["pt_turned"], q["chunk0"] + k + 1)
                    if k >= 2:
                        act.wait_ge(S["out_units"], q["unit0"] + SG * (k - 1))
                    elif p >= 1:
                        act.wait_ge(S["out_done"], p)
                    act.activation(pT[:r, 0, 0:w], ps[:r, 0, 0:w], ACT.Copy).then_inc(S["pt_act"], 1)

                copy(0)
                for k in range(NC):
                    for n in range(q["unit0"] + SG * k, q["unit0"] + SG * (k + 1)):
                        if n + SLOTS < len(units) and not passes[units[n + SLOTS][0]]["window"]:
                            act.wait_ge(S["out_units"], n + 1)
                            load_unit(act, True, n + SLOTS)
                    if k % 2 == 0 and k + 2 <= NC:
                        copy(k + 2)

            for what, p in ORDER:
                if what == "keys":
                    keys(p)
                elif what == "values":
                    values(p)
                else:
                    q = passes[p]
                    chunk, at = (4 if q["window"] else 6), SEQ + SG * DEC_SEQ * q["g"]
                    act.wait_ge(S["gathered"], p + 1)
                    act.activation(M["mixT"][:, chunk:chunk + 2, at:at + SG * DEC_SEQ],
                                   ps[:, 7, 0:64].rearrange("p (k t) -> p k t", k=2), ACT.Copy).then_inc(S["out_copied"], 1)
            nc.disable_value_cache = False

        @block.vector
        def _(dve):
            dve.memset(one[:], 1.0).then_inc(S["ones_ready"], 1)
            dve.wait_ge(S["consts"], 16 * 7)
            for p, q in enumerate(passes):
                qT = M["CQT"] if q["window"] else DQT
                for pair in range(2):
                    qv = qT[:, pair, SEQ + 32 * q["g"]:SEQ + 32 * q["g"] + 32].rearrange("p (s q) -> p s q", q=DEC_SEQ)
                    for h in range(H):
                        ins = dve.tensor_scalar(qb[:, p, pair, :, h, :], qv, pair_head[:, pair, h:h + 1], None, ALU.mult)
                        ins.then_inc(S["q_ready"] if h == H - 1 else S["spread"], 1)
            dve.wait_ge(S["bias_turned"], 1)
            dve.tensor_copy(bcol[:], ps[:, 7, 0:1]).then_inc(S["bias_ready"], 1)
            dve.wait_ge(S["bias_ready"], 1)
            dve.wait_ge(S["ones_ready"], 1)
            dve.wait_ge(S["spread"], 2 * (H - 1) * NP_)

            def take(p, k):
                q = passes[p]
                NC, kc = q["NC"], q["chunk0"] + k
                dve.wait_ge(S["scores_done"], q["unit0"] + p + (SG * (k + 1) if k < NC else SG * NC + 1))
                if p >= 2 and k == 0:
                    dve.wait_ge(S["pt_turned"], passes[p - 2]["chunk0"] + passes[p - 2]["NC"] + 1)
                if k == NC:
                    cs = slice(q["keys"], q["keys"] + NS)
                    mk = new_mask[:, 0 if q["window"] else 1, q["g"], :]
                else:
                    cs = slice(q["chunks"][k][0] * P, (q["chunks"][k][0] + q["chunks"][k][1]) * P)
                    mk = win_mask[:, cs] if q["window"] else None
                src, dst = ps[:, 4 + kc % 2, 0:cs.stop - cs.start], z[:, p % 2, cs]
                if q["window"]:
                    ins = dve.tensor_tensor(dst, src, mk, ALU.add)
                elif k == NC:
                    ins = dve.scalar_tensor_tensor(dst, src, bcol[:, 0:1], mk, ALU.add, ALU.add)
                else:
                    ins = dve.tensor_scalar(dst, src, bcol[:, 0:1], None, ALU.add)
                ins.then_inc(S["z_ready"], 1)

            def weigh(p):
                q = passes[p]
                zp, fp = z[:, p % 2, 0:q["keys"] + NS], f[:, 0:q["keys"] + NS]
                s = q["sticks"]

                def maximum():
                    dve.wait_ge(S["z_ready"], q["chunk0"] + q["NC"] + 1)
                    dve.tensor_reduce(mx[:, p:p + 1], zp, AX.X, ALU.max).then_inc(S["maxed"], 1)
                    dve.wait_ge(S["maxed"], q["g"] + 1)
                    dve.tensor_scalar(mx[:, p:p + 1], mx[:, p:p + 1], -1.0, None, ALU.mult).then_inc(S["negated"], 1)

                def softplus():
                    dve.wait_ge(S["ln_done"], s)
                    dve.scalar_tensor_tensor(fp, zp, 0.0, fp, ALU.max, ALU.add).then_inc(S["f_done"], 1)

                def sums():
                    dve.wait_ge(S["f_done"], s)
                    dve.tensor_tensor_scan(fp[:, ::-1], one[:, 0:1].to_broadcast([P, q["keys"] + NS]), fp[:, ::-1], 0.0,
                                           ALU.mult, ALU.add).then_inc(S["sum_done"], 1)
                    dve.wait_ge(S["sum_done"], s)
                    dve.tensor_tensor(zp, zp, fp, ALU.subtract).then_inc(S["scanned"], 1)

                return [maximum] if q["window"] else [lambda: None, lambda: None, softplus, sums]

            def keys(p):
                q = passes[p]
                before = spread_over(weigh(p - 1), len(q["units"]), 0 if passes[p - 1]["window"] else 3) if p >= 1 else {}
                for x, (k, j) in enumerate(q["units"]):
                    n = q["unit0"] + x
                    w = units[n][3] * P
                    dve.wait_ge(S["turned"], n + 1)
                    if n >= 2:
                        dve.wait_ge(S["scores_done"], n - 1 + sum(r["unit0"] + len(r["units"]) <= n - 2 for r in passes))
                    dve.tensor_copy(kt[:, n % 2, 1, 0:w], ps[:, 2 * (n % 2) + 1, 0:w]).then_inc(S["kt_dve"], 1)
                    if j == 1 and k >= 1:
                        take(p, k - 1)
                    for step in before.get(x, ()):
                        step()
                take(p, q["NC"] - 1)
                take(p, q["NC"])

            def values(p):
                q = passes[p]
                NC = q["NC"]
                if p == NP_ - 1:
                    for step in weigh(p):
                        step()
                for k in range(1, NC + 1, 2):
                    w, r = (q["chunks"][k][1] * P, P) if k < NC else (P, NS)
                    dve.wait_ge(S["pt_turned"], q["chunk0"] + k + 1)
                    if k >= 2:
                        dve.wait_ge(S["out_units"], q["unit0"] + SG * (k - 1))
                    elif p >= 1:
                        dve.wait_ge(S["out_done"], p)
                    dve.tensor_copy(pT[:r, 1, 0:w], ps[:r, 1, 0:w]).then_inc(S["pt_dve"], 1)
                dve.wait_ge(S["out_done"], p + 1)
                if p >= 1:
                    dve.wait_ge(S["gathered"], p)
                if q["window"]:
                    dve.wait_ge(S["a_ready"], p + 1)
                    dve.reciprocal(total[:, p:p + 1], total[:, p:p + 1]).then_inc(S["inv_done"], 1)
                    dve.wait_ge(S["inv_done"], q["g"] + 1)
                    dve.scalar_tensor_tensor(rows[:], ps[:, 6, 0:W4], total[:, p:p + 1], head_cols[:], ALU.mult,
                                             ALU.mult).then_inc(S["rows_ready"], 1)
                else:
                    dve.tensor_tensor(rows[:], ps[:, 6, 0:W4], head_cols[:], ALU.mult).then_inc(S["rows_ready"], 1)

            for what, p in ORDER:
                if what == "keys":
                    keys(p)
                elif what == "values":
                    values(p)
            dve.tensor_scalar(E["pages"][:], E["pages"][:], N_POOL, None, ALU.add).then_inc(S["pages_moved"], 1)
            dve.wait_ge(S["pages_moved"], 1)


def output(nc, E, M, l, I):
    with stage(nc, "ou", POST_SEMS + WEIGHT_SEMS + "mix_hi mix_lo") as (S, sb, block):
        W = weight_buffers(sb)
        hi = sb("mix_hi", [P, KC, NT], F32R)
        lo = sb("mix_lo", [P, KC, NT], F32R)
        gain = sb("gain", [P, D_MODEL])
        Y = post_buffers(sb)
        Y["scale"], Y["eps"] = 1.0 / D_MODEL, EPS
        turned = M["TR"][:].rearrange("p m n -> p (m n)")
        y = turned[:, 0:2 * TILES * 512].rearrange("p (h n) -> p h n", h=2)
        y_scratch = turned[:, 2 * TILES * 512:2 * TILES * 512 + 512]
        x_scratch = W["raw"][:, 0, 0:D_MODEL]

        @block.sync
        def _(sp):
            sp.dma_start(gain[:], layer_row(I["g_mix_post"], l)).then_inc(S["post_gain_loaded"], 16)
            post_sync(sp, S, W, I["w_out"], l, KC, 0)

        @block.tensor
        def _(pe):
            pe.wait_ge(S["mix_lo"], KC)
            post_tensor(pe, E, S, W, hi, lo, KC, 0)

        @block.scalar
        def _(act):
            split_scalar(act, S, W, 0, 0, 0, False)
            split_scalar(act, S, W, 1, 1, 0, False)
            for c in range(KC):
                act.activation(hi[:, c], M["mixT"][:, c], ACT.Copy).then_inc(S["mix_hi"], 1)
            post_scalar(act, E, S, W, Y, y_scratch, x_scratch, KC, 0)

        @block.vector
        def _(dve):
            split_vector(dve, S, W, 0, 0)
            split_vector(dve, S, W, 1, 1)
            for c in range(KC):
                dve.wait_ge(S["mix_hi"], c + 1)
                dve.tensor_tensor(lo[:, c], M["mixT"][:, c], hi[:, c].bitcast(F32), ALU.subtract).then_inc(S["mix_lo"], 1)
            post_vector(dve, E, S, W, Y, y, gain, KC, 0)


def mixing(nc, E, l, I, O, C):
    with ExitStack() as ctx:
        def sb(n, shape, dt=F32):
            return ctx.enter_context(nc.sbuf_tensor(n, shape, dt))

        M = dict(
            TR=sb("TR", [P, 10, NT]), gates=sb("gates", [GATE_ROWS, NT]),
            KA=sb("KA", [P, TILES, W4]), VA=sb("VA", [P, TILES, H, HD + 1]), AO=sb("AO", [P, TILES, W4]),
            CV=sb("CV", [P, TILES, W4]), BVG=sb("BVG", [P, TILES, 2 * W4]), CQK=sb("CQK", [P, TILES, 2 * W4]),
            DKV=sb("DKV", [P, TILES, 2 * W4]))
        M["CQT"], M["CKT"] = M["TR"][:, AQ:AQ + 2, :], M["TR"][:, AK:AK + 2, :]
        project(nc, E, M, l, I["g_mix_pre"], I["w_in"], O)
        M["mixT"] = sb("mixT", [P, KC, NT])
        mlstm(nc, E, M, l, I, O, C)
        gla(nc, E, M, l, I, O, C)
        rotary(nc, E, M, l, O, C)
        DQT, DKT = M["TR"][:, DQ:DQ + 2, :], M["TR"][:, DK:DK + 2, :]
        prompt_attention(nc, E, M, l, "window", M["CQT"], M["CKT"], M["CV"], 4, I, O, C)
        prompt_attention(nc, E, M, l, "stick", DQT, DKT, M["DKV"][:, :, W4:], 6, I, O, C)
        sample_attention(nc, E, M, l, I, C)
        output(nc, E, M, l, I)



def program(nc, I, O, C):
    with ExitStack() as ctx:
        def sb(n, shape, dt=F32):
            return ctx.enter_context(nc.sbuf_tensor(n, shape, dt))

        E = dict(
            x=sb("x", [P, TILES, D_MODEL]),
            ident=sb("ident", [P, P]), sumsq=sb("sumsq", [P, TILES]), eps=sb("eps", [P, 1]),
            pages=sb("pages", [1, DEC_BATCH * N_PAGES], I32),
            ps=ctx.enter_context(nc.psum_tensor("ps", [P, 8, 512], F32)))

        with stage(nc, "start", "loaded cleared squares_done") as (S, stage_sb, block):
            scratch = stage_sb("scratch", [P, D_MODEL])

            @block.sync
            def _(sp):
                sp.dma_start(E["x"][:, 0:PT_TILES, :], I["x_prompt"].rearrange("b (t p) n -> p (b t) n", p=P)).then_inc(S["loaded"], 16)
                sp.dma_start(E["x"][:NS, PT_TILES, :], I["x_sample"].rearrange("b t n -> (b t) n")).then_inc(S["loaded"], 16)
                sp.dma_start(E["ident"][:], C["ident"]).then_inc(S["loaded"], 16)
                sp.dma_start(E["pages"][:], I["page_table"].rearrange("(o b) n -> o (b n)", o=1)).then_inc(S["loaded"], 16)
                sp.wait_ge(S["loaded"], 64)

            @block.vector
            def _(dve):
                dve.memset(E["sumsq"][:], 0.0).then_inc(S["cleared"], 1)
                dve.memset(E["eps"][:], EPS)

            @block.scalar
            def _(act):
                act.wait_ge(S["loaded"], 64)
                act.wait_ge(S["cleared"], 1)
                for t, r in enumerate(ROWS):
                    if t > 0:
                        act.wait_ge(S["squares_done"], t)
                    act.activation(scratch[:r], E["x"][:r, t, :], ACT.Square,
                                   accum_out=E["sumsq"][:r, t:t + 1]).then_inc(S["squares_done"], 1)

        with nc.Fori(0, DEPTH) as l:
            ffn(nc, E, l, "f1", I["g_ffn1_pre"], I["w_ffn1_in"], I["w_ffn1_out"], I["g_ffn1_post"])
            mixing(nc, E, l, I, O, C)
            ffn(nc, E, l, "f2", I["g_ffn2_pre"], I["w_ffn2_in"], I["w_ffn2_out"], I["g_ffn2_post"])

        with stage(nc, "end", "stored") as (S, _sb, block):
            @block.sync
            def _(sp):
                sp.dma_start(O["y_prompt"].rearrange("b (t p) n -> p (b t) n", p=P), E["x"][:, 0:PT_TILES, :]).then_inc(S["stored"], 16)
                sp.dma_start(O["y_sample"].rearrange("b t n -> (b t) n"), E["x"][:NS, PT_TILES, :]).then_inc(S["stored"], 16)
                sp.wait_ge(S["stored"], 32)


INPUTS = ("x_prompt", "x_sample", "cache_sb_k", "cache_sb_v", "page_table", "cache_win_k", "cache_win_v",
          "state_mlstm_c", "state_mlstm_n", "state_mlstm_m", "state_gla_s",
          "g_ffn1_pre", "w_ffn1_in", "w_ffn1_out", "g_ffn1_post", "g_mix_pre", "w_in", "b_ig", "b_fg",
          "g_head_a", "w_gla_a2", "b_gla_a", "g_head_b", "b_sb", "w_out", "g_mix_post",
          "g_ffn2_pre", "w_ffn2_in", "w_ffn2_out", "g_ffn2_post")
OUTPUTS = {
    "y_prompt": (1, SEQ, D_MODEL), "y_sample": (DEC_BATCH, DEC_SEQ, D_MODEL),
    "p_sb_k": (DEPTH, 1, SEQ, H, HD), "p_sb_v": (DEPTH, 1, SEQ, H, HD),
    "p_win_k": (DEPTH, 1, SEQ, H, HD), "p_win_v": (DEPTH, 1, SEQ, H, HD),
    "p_mlstm_c": (DEPTH, 1, H, HD, HD), "p_mlstm_n": (DEPTH, 1, H, HD), "p_mlstm_m": (DEPTH, 1, H),
    "p_gla_s": (DEPTH, 1, H, DK_B, HD),
    "s_sb_k": (DEPTH, DEC_BATCH, DEC_SEQ, H, HD), "s_sb_v": (DEPTH, DEC_BATCH, DEC_SEQ, H, HD),
    "s_win_k": (DEPTH, DEC_BATCH, DEC_SEQ, H, HD), "s_win_v": (DEPTH, DEC_BATCH, DEC_SEQ, H, HD),
    "s_mlstm_c": (DEPTH, DEC_BATCH, H, HD, HD), "s_mlstm_n": (DEPTH, DEC_BATCH, H, HD),
    "s_mlstm_m": (DEPTH, DEC_BATCH, H), "s_gla_s": (DEPTH, DEC_BATCH, H, DK_B, HD),
}


def kernel(**inputs):
    import concourse.bacc as _bacc
    from concourse.bass_utils import run_bass_kernel_spmd as _run

    nc = _bacc.Bacc("TRN2", target_bir_lowering=False, num_devices=1)
    arrays, I, O, C = {}, {}, {}, {}
    for name in INPUTS:
        a = np.ascontiguousarray(inputs[name])
        arrays[f"in_{name}"] = a
        I[name] = nc.dram_tensor(f"in_{name}", a.shape, mybir.dt.from_np(a.dtype), kind="ExternalInput").ap()
    for name, a in constants().items():
        arrays[f"const_{name}"] = a
        C[name] = nc.dram_tensor(f"const_{name}", a.shape, F32, kind="ExternalInput").ap()
    for name, shape in OUTPUTS.items():
        O[name] = nc.dram_tensor(f"out_{name}", shape, F32, kind="ExternalOutput").ap()
    program(nc, I, O, C)
    r = _run(nc, [arrays], core_ids=[0])
    return tuple(r.results[0][f"out_{name}"] for name in OUTPUTS)
```
